# Optimizing a Trainium2 kernel written in Bass

```python
import jax, jax.numpy as jnp
from jax import lax
import numpy as np
import math
import jax
import jax.numpy as jnp

D_MODEL = 1024
BATCH = 1
SEQ = 256
DEPTH = 1

NSA_HEADS = 8
NSA_KV_GROUPS = 2
NSA_HEAD_DIM = 64
NSA_HEADS_PER_GROUP = NSA_HEADS // NSA_KV_GROUPS
NSA_WIDTH = NSA_HEADS * NSA_HEAD_DIM
NSA_KV_WIDTH = NSA_KV_GROUPS * NSA_HEAD_DIM
CMP_LEN = 32
CMP_STRIDE = 16
SLC_LEN = 64
SLC_TOPN = 16
WINDOW = 512
Q_BLOCK = 128
ROPE_THETA = 500000.0
ROPE_DIM = NSA_HEAD_DIM // 4
HG_HEADS = 4
HG_KEY_DIM = 128
HG_VAL_DIM = 128
HG_WIDTH = HG_HEADS * HG_VAL_DIM
HG_CHUNK = 64
N_GROUPS = 4
EXPERTS_PER_GROUP = 8
N_EXPERTS = N_GROUPS * EXPERTS_PER_GROUP
TOP_K_IN_GROUP = 2
D_FF_EXPERT = 512
RMS_EPS = 1e-6
NEG_INF = -1e30
FORCE_SCORE = 1e4

IN_SPLITS = [NSA_WIDTH, 6 * NSA_KV_WIDTH, 3 * NSA_HEADS,
             HG_HEADS * HG_KEY_DIM, HG_HEADS * HG_KEY_DIM, HG_WIDTH, HG_WIDTH, 2 * D_MODEL]
IN_COLS = sum(IN_SPLITS)


def rmsnorm(x, g):
    x32 = x.astype(jnp.float32)
    y = x32 * lax.rsqrt(jnp.mean(x32 * x32, axis=-1, keepdims=True) + RMS_EPS)
    return (y * g.astype(jnp.float32)).astype(x.dtype)

def partial_rope(t, pos):
    half = ROPE_DIM // 2
    inv_freq = ROPE_THETA ** (-jnp.arange(half, dtype=jnp.float32) / half)
    ang = pos.astype(jnp.float32)[:, None] * inv_freq[None, :]
    cos = jnp.cos(ang)[:, None, :]
    sin = jnp.sin(ang)[:, None, :]
    t1 = t[..., :half]
    t2 = t[..., half:ROPE_DIM]
    return jnp.concatenate([t1 * cos - t2 * sin, t2 * cos + t1 * sin, t[..., ROPE_DIM:]], axis=-1)

def masked_softmax(s, mask):
    s = jnp.where(mask, s, NEG_INF)
    return jax.nn.softmax(s, axis=-1) * mask

def nsa_mixer(q, k_cmp_in, v_cmp_in, k_slc, v_slc, k_win, v_win, gate_logits, w_cmp_k, w_cmp_v, cmp_pos):
    f32 = jnp.float32
    b, s = q.shape[0], q.shape[1]
    G, R, dk = NSA_KV_GROUPS, NSA_HEADS_PER_GROUP, NSA_HEAD_DIM
    pos = jnp.arange(s)
    scale = dk ** -0.5
    q = partial_rope(q.astype(f32), pos).reshape(b, s, G, R, dk)
    k_slc = partial_rope(k_slc.astype(f32), pos)
    k_win = partial_rope(k_win.astype(f32), pos)
    v_slc = v_slc.astype(f32)
    v_win = v_win.astype(f32)
    gates = jax.nn.sigmoid(gate_logits.astype(f32)).reshape(b, s, G, R, 3)

    n_cmp = (s - CMP_LEN) // CMP_STRIDE + 1
    cmp_start = jnp.arange(n_cmp) * CMP_STRIDE
    cmp_end = cmp_start + CMP_LEN - 1
    cmp_idx = cmp_start[:, None] + jnp.arange(CMP_LEN)[None, :]

    def compress(t, w):
        blk = t.astype(f32)[:, cmp_idx] + cmp_pos.astype(f32)[None, None, :, None, :]
        blk = blk.transpose(0, 1, 3, 2, 4).reshape(b, n_cmp, G, CMP_LEN * dk)
        return jnp.einsum('bngc,cd->bngd', blk, w.astype(f32))

    k_cmp = partial_rope(compress(k_cmp_in, w_cmp_k), cmp_start)
    v_cmp = compress(v_cmp_in, w_cmp_v)

    n_sel = s // SLC_LEN
    top_n = min(SLC_TOPN, n_sel)
    sel_start = jnp.arange(n_sel) * SLC_LEN
    blk_ids = jnp.arange(n_sel)
    overlap = ((cmp_start[:, None] < sel_start[None, :] + SLC_LEN) &
               (cmp_end[:, None] >= sel_start[None, :])).astype(f32)
    k_sel_blocks = k_slc.reshape(b, n_sel, SLC_LEN, G, dk).transpose(0, 3, 1, 2, 4)
    v_sel_blocks = v_slc.reshape(b, n_sel, SLC_LEN, G, dk).transpose(0, 3, 1, 2, 4)
    gather_blocks = jax.vmap(jax.vmap(lambda blocks, ids: blocks[ids]))
    slc_offsets = jnp.arange(SLC_LEN)

    k_win_pad = jnp.pad(k_win, ((0, 0), (WINDOW, 0), (0, 0), (0, 0)))
    v_win_pad = jnp.pad(v_win, ((0, 0), (WINDOW, 0), (0, 0), (0, 0)))
    win_offsets = jnp.arange(WINDOW + Q_BLOCK) - WINDOW
    q_offsets = jnp.arange(Q_BLOCK)

    def query_block(c):
        t0 = c * Q_BLOCK
        tpos = t0 + q_offsets
        qb = lax.dynamic_slice_in_dim(q, t0, Q_BLOCK, axis=1)
        gb = lax.dynamic_slice_in_dim(gates, t0, Q_BLOCK, axis=1)
        cmask = cmp_end[None, :] <= tpos[:, None]
        p_cmp = masked_softmax(jnp.einsum('bqgrd,bngd->bgrqn', qb, k_cmp) * scale, cmask)
        o_cmp = jnp.einsum('bgrqn,bngd->bqgrd', p_cmp, v_cmp)
        imp = jnp.einsum('bgrqn,nj->bgqj', p_cmp, overlap)
        force = (blk_ids[None, :] == (tpos // SLC_LEN)[:, None]) | (blk_ids[None, :] == 0)
        valid = sel_start[None, :] <= tpos[:, None]
        score = jnp.where(force, FORCE_SCORE, jnp.where(valid, imp, -1.0))
        _, sel_idx = lax.top_k(score, top_n)
        k_sel = gather_blocks(k_sel_blocks, sel_idx).reshape(b, G, Q_BLOCK, top_n * SLC_LEN, dk)
        v_sel = gather_blocks(v_sel_blocks, sel_idx).reshape(b, G, Q_BLOCK, top_n * SLC_LEN, dk)
        sel_pos = (sel_idx[..., None] * SLC_LEN + slc_offsets).reshape(b, G, Q_BLOCK, top_n * SLC_LEN)
        smask = (sel_pos <= tpos[None, None, :, None])[:, :, None]
        p_slc = masked_softmax(jnp.einsum('bqgrd,bgqmd->bgrqm', qb, k_sel) * scale, smask)
        o_slc = jnp.einsum('bgrqm,bgqmd->bqgrd', p_slc, v_sel)
        kw = lax.dynamic_slice_in_dim(k_win_pad, t0, WINDOW + Q_BLOCK, axis=1)
        vw = lax.dynamic_slice_in_dim(v_win_pad, t0, WINDOW + Q_BLOCK, axis=1)
        kpos = t0 + win_offsets
        rel = tpos[:, None] - kpos[None, :]
        wmask = (rel >= 0) & (rel < WINDOW) & (kpos[None, :] >= 0)
        p_win = masked_softmax(jnp.einsum('bqgrd,bmgd->bgrqm', qb, kw) * scale, wmask)
        o_win = jnp.einsum('bgrqm,bmgd->bqgrd', p_win, vw)
        return gb[..., 0:1] * o_cmp + gb[..., 1:2] * o_slc + gb[..., 2:3] * o_win

    out = lax.map(query_block, jnp.arange(s // Q_BLOCK))
    return out.transpose(1, 0, 2, 3, 4, 5).reshape(b, s, NSA_WIDTH)

def hgrn2_mixer(q, f_logit, i_in, lb):
    f32 = jnp.float32
    b, s = q.shape[0], q.shape[1]
    q = q.astype(f32).reshape(b, s, HG_HEADS, HG_KEY_DIM)
    f = lb + (1.0 - lb) * jax.nn.sigmoid(f_logit.astype(f32).reshape(b, s, HG_HEADS, HG_KEY_DIM))
    log_f = jnp.log(f)
    k = 1.0 - f
    v = i_in.astype(f32).reshape(b, s, HG_HEADS, HG_VAL_DIM)
    n_ch = s // HG_CHUNK

    def to_chunks(t):
        return t.reshape(b, n_ch, HG_CHUNK, HG_HEADS, t.shape[-1]).transpose(1, 0, 3, 2, 4)

    causal = jnp.tril(jnp.ones((HG_CHUNK, HG_CHUNK), dtype=bool))

    def chunk_step(state, inp):
        qc, kc, vc, gc = inp
        bcum = jnp.cumsum(gc, axis=2)
        o_inter = jnp.einsum('bhtk,bhkv->bhtv', qc * jnp.exp(bcum), state)
        rel = jnp.where(causal[:, :, None], bcum[:, :, :, None, :] - bcum[:, :, None, :, :], -jnp.inf)
        attn = jnp.einsum('bhtk,bhsk,bhtsk->bhts', qc, kc, jnp.exp(rel))
        o_intra = jnp.einsum('bhts,bhsv->bhtv', attn, vc)
        b_last = bcum[:, :, -1:, :]
        new_state = (jnp.exp(b_last[:, :, 0, :])[..., None] * state +
                     jnp.einsum('bhsk,bhsv->bhkv', kc * jnp.exp(b_last - bcum), vc))
        return new_state, o_inter + o_intra

    state0 = jnp.zeros((b, HG_HEADS, HG_KEY_DIM, HG_VAL_DIM), f32)
    _, o = lax.scan(chunk_step, state0, (to_chunks(q), to_chunks(k), to_chunks(v), to_chunks(log_f)))
    return o.transpose(1, 0, 3, 2, 4).reshape(b, s, HG_HEADS, HG_VAL_DIM)

def hier_moe(h, w_grp, b_grp, w_rtr, b_rtr, w_gate, w_up, w_down):
    f32 = jnp.float32
    b, s, d = h.shape
    t = h.reshape(b * s, d)
    grp_logits = (t @ w_grp).astype(f32) + b_grp.astype(f32)
    grp_sel = jnp.argmax(grp_logits, axis=-1)
    grp_prob = jnp.take_along_axis(jax.nn.softmax(grp_logits, axis=-1), grp_sel[:, None], axis=1)
    exp_logits = ((t @ w_rtr).astype(f32) + b_rtr.astype(f32)).reshape(-1, N_GROUPS, EXPERTS_PER_GROUP)
    in_grp = jnp.take_along_axis(exp_logits, grp_sel[:, None, None], axis=1)[:, 0]
    top_logits, top_idx = lax.top_k(in_grp, TOP_K_IN_GROUP)
    top_w = jax.nn.softmax(top_logits, axis=-1) * grp_prob
    expert_ids = grp_sel[:, None] * EXPERTS_PER_GROUP + top_idx
    combine = jnp.sum(jax.nn.one_hot(expert_ids, N_EXPERTS, dtype=f32) * top_w[..., None], axis=1)
    out = jnp.zeros((b * s, d), f32)
    for e in range(N_EXPERTS):
        hid = jax.nn.silu(t @ w_gate[e]) * (t @ w_up[e])
        out = out + combine[:, e:e + 1] * (hid @ w_down[e]).astype(f32)
    return out.reshape(b, s, d).astype(h.dtype)

def first_inputs(seed: int = 0) -> dict:
    key = jax.random.key(seed)
    ks = jax.random.split(key, 24)
    f32 = jnp.float32
    nrm = lambda k, shape, scale: jax.random.normal(k, shape, f32) * scale
    return {
        'x': nrm(ks[0], (BATCH, SEQ, D_MODEL), 1.0),
        'attn_norm': 1.0 + nrm(ks[1], (DEPTH, D_MODEL), 0.01),
        'w_in': nrm(ks[2], (DEPTH, D_MODEL, IN_COLS), D_MODEL ** -0.5),
        'w_cmp_k': nrm(ks[3], (DEPTH, CMP_LEN * NSA_HEAD_DIM, NSA_HEAD_DIM), (CMP_LEN * NSA_HEAD_DIM) ** -0.5),
        'w_cmp_v': nrm(ks[4], (DEPTH, CMP_LEN * NSA_HEAD_DIM, NSA_HEAD_DIM), (CMP_LEN * NSA_HEAD_DIM) ** -0.5),
        'cmp_pos': nrm(ks[5], (DEPTH, CMP_LEN, NSA_HEAD_DIM), 0.02),
        'hg_lb_logits': nrm(ks[6], (DEPTH + 1, HG_HEADS * HG_KEY_DIM), 0.5),
        'hg_norm': 1.0 + nrm(ks[7], (DEPTH, HG_VAL_DIM), 0.01),
        'w_br_nsa': nrm(ks[8], (DEPTH, NSA_WIDTH, D_MODEL), NSA_WIDTH ** -0.5),
        'w_br_hg': nrm(ks[9], (DEPTH, HG_WIDTH, D_MODEL), HG_WIDTH ** -0.5),
        'w_out': nrm(ks[10], (DEPTH, D_MODEL, D_MODEL), D_MODEL ** -0.5),
        'ffn_norm': 1.0 + nrm(ks[11], (DEPTH, D_MODEL), 0.01),
        'w_grp': nrm(ks[12], (DEPTH, D_MODEL, N_GROUPS), D_MODEL ** -0.5),
        'b_grp': nrm(ks[13], (DEPTH, N_GROUPS), 0.01),
        'w_rtr': nrm(ks[14], (DEPTH, D_MODEL, N_EXPERTS), D_MODEL ** -0.5),
        'b_rtr': nrm(ks[15], (DEPTH, N_EXPERTS), 0.01),
        'w_gate': nrm(ks[16], (DEPTH, N_EXPERTS, D_MODEL, D_FF_EXPERT), D_MODEL ** -0.5),
        'w_up': nrm(ks[17], (DEPTH, N_EXPERTS, D_MODEL, D_FF_EXPERT), D_MODEL ** -0.5),
        'w_down': nrm(ks[18], (DEPTH, N_EXPERTS, D_FF_EXPERT, D_MODEL), D_FF_EXPERT ** -0.5),
        'final_norm': 1.0 + nrm(ks[19], (D_MODEL,), 0.01),
    }

def first_block(x, attn_norm, w_in, w_cmp_k, w_cmp_v, cmp_pos, hg_lb_logits, hg_norm, w_br_nsa, w_br_hg,
              w_out, ffn_norm, w_grp, b_grp, w_rtr, b_rtr, w_gate, w_up, w_down, final_norm):
    b, s, _ = x.shape
    lower_bounds = jnp.cumsum(jax.nn.softmax(hg_lb_logits.astype(jnp.float32), axis=0), axis=0)
    split_points = np.cumsum(IN_SPLITS)[:-1].tolist()
    for layer in range(DEPTH):
        h = rmsnorm(x, attn_norm[layer])
        proj = h @ w_in[layer]
        nsa_q, nsa_kv, nsa_gate, hg_q, hg_f, hg_i, hg_g, merge_logits = jnp.split(proj, split_points, axis=-1)
        kv = nsa_kv.reshape(b, s, 6, NSA_KV_GROUPS, NSA_HEAD_DIM)
        o_nsa = nsa_mixer(nsa_q.reshape(b, s, NSA_HEADS, NSA_HEAD_DIM),
                          kv[:, :, 0], kv[:, :, 1], kv[:, :, 2], kv[:, :, 3], kv[:, :, 4], kv[:, :, 5],
                          nsa_gate.reshape(b, s, NSA_HEADS, 3),
                          w_cmp_k[layer], w_cmp_v[layer], cmp_pos[layer])
        lb = lower_bounds[layer].reshape(HG_HEADS, HG_KEY_DIM)
        o_hg = hgrn2_mixer(hg_q, hg_f, hg_i, lb)
        o_hg = rmsnorm(o_hg, hg_norm[layer]) * jax.nn.silu(
            hg_g.astype(jnp.float32).reshape(b, s, HG_HEADS, HG_VAL_DIM))
        o_hg = o_hg.reshape(b, s, HG_WIDTH).astype(x.dtype)
        gate_nsa, gate_hg = jnp.split(jax.nn.sigmoid(merge_logits), 2, axis=-1)
        mixed = (gate_nsa * (o_nsa.astype(x.dtype) @ w_br_nsa[layer]) +
                 gate_hg * (o_hg @ w_br_hg[layer]))
        x = x + mixed @ w_out[layer]
        x = x + hier_moe(rmsnorm(x, ffn_norm[layer]), w_grp[layer], b_grp[layer], w_rtr[layer], b_rtr[layer],
                         w_gate[layer], w_up[layer], w_down[layer])
    return rmsnorm(x, final_norm)


D_MIX = D_MODEL
D_ATTN = D_MIX // 2
D_SSM = D_MIX - D_ATTN
ATTN_HEADS = 4
ATTN_QK_DIM = D_ATTN // (2 * ATTN_HEADS)
ATTN_V_DIM = D_ATTN // ATTN_HEADS
SSM_GROUP_WIDTH = 16
SSM_GROUPS = D_SSM // SSM_GROUP_WIDTH
SSM_STATE = 64
D_IN_PROJ = 3 * D_ATTN + D_SSM
N_EXPERTS_2 = 32
TOP_K = 4
D_FF = D_MODEL
SWIGLU_LIMIT = 7.0
SWIGLU_ALPHA = 1.702
MOE_BLOCK = 128
DT_MIN = 1e-3
DT_MAX = 1e-1
MASK_VALUE = -1e30


def _rmsnorm(x, g):
    xf = x.astype(jnp.float32)
    y = xf * lax.rsqrt(jnp.mean(xf * xf, axis=-1, keepdims=True) + RMS_EPS)
    return (y * g.astype(jnp.float32)).astype(x.dtype)

def _modulate(h, shift, scale):
    return h * (1.0 + scale[:, None, :]) + shift[:, None, :]

def _diff_attention(q, k, v, lam, lambda_init, subln_g):
    b, s, h, _, dk = q.shape
    dv = v.shape[-1]
    n_blk = s // Q_BLOCK
    q_blocks = q.reshape(b, n_blk, Q_BLOCK, h, 2, dk).transpose(1, 0, 2, 3, 4, 5)
    key_pos = jnp.arange(s)
    scale = dk ** -0.5

    def one_block(args):
        q_blk, i = args
        sc = jnp.einsum('bqhmd,bkhmd->bhmqk', q_blk, k).astype(jnp.float32) * scale
        q_pos = i * Q_BLOCK + jnp.arange(Q_BLOCK)
        causal = key_pos[None, :] <= q_pos[:, None]
        p = jax.nn.softmax(jnp.where(causal, sc, MASK_VALUE), axis=-1)
        att = p[:, :, 0] - lam * p[:, :, 1]
        return jnp.einsum('bhqk,bkhe->bqhe', att.astype(v.dtype), v)

    out = lax.map(one_block, (q_blocks, jnp.arange(n_blk)))
    out = out.transpose(1, 0, 2, 3, 4).reshape(b, s, h, dv)
    out = _rmsnorm(out, subln_g) * (1.0 - lambda_init)
    return out.reshape(b, s, h * dv)

def _s5(u, a_re, a_im, log_dt, b_re, b_im, c_re, c_im, d_skip, w_glu, b_glu):
    bsz, s, _ = u.shape
    f32 = jnp.float32
    ug = u.reshape(bsz, s, SSM_GROUPS, SSM_GROUP_WIDTH).astype(f32)
    dt = jnp.exp(log_dt.astype(f32))[:, None]
    lam = lax.complex(jnp.minimum(a_re.astype(f32), -1e-4), a_im.astype(f32))
    lam_bar = jnp.exp(lam * dt)
    b_cplx = lax.complex(b_re.astype(f32), b_im.astype(f32))
    b_bar = ((lam_bar - 1.0) / lam)[..., None] * b_cplx
    bu = jnp.einsum('bsgc,gpc->bsgp', ug.astype(jnp.complex64), b_bar)
    a = jnp.broadcast_to(lam_bar[None, None], (1, s, SSM_GROUPS, SSM_STATE))

    def combine(e_i, e_j):
        a_i, x_i = e_i
        a_j, x_j = e_j
        return a_j * a_i, a_j * x_i + x_j

    _, states = lax.associative_scan(combine, (a, bu), axis=1)
    c_cplx = lax.complex(c_re.astype(f32), c_im.astype(f32))
    y = jnp.einsum('bsgp,gcp->bsgc', states, c_cplx).real
    y = y + d_skip.astype(f32).reshape(SSM_GROUPS, SSM_GROUP_WIDTH) * ug
    y = y.reshape(bsz, s, D_SSM).astype(u.dtype)
    z = jax.nn.gelu(y)
    return z * jax.nn.sigmoid(z @ w_glu + b_glu)

def _moe(h, w_router, b_router, w1, b1, w2, b2):
    bsz, s, d = h.shape
    n_tok = bsz * s
    hf = h.reshape(n_tok, d)
    logits = (hf @ w_router + b_router).astype(jnp.float32)
    top_val, top_idx = lax.top_k(logits, TOP_K)
    gates = jax.nn.softmax(top_val, axis=-1)
    m = n_tok * TOP_K
    flat_e = top_idx.reshape(m)
    flat_tok = jnp.arange(m, dtype=jnp.int32) // TOP_K
    flat_gate = gates.reshape(m)
    order = jnp.argsort(flat_e)
    sorted_e = flat_e[order]
    counts = jnp.bincount(flat_e, length=N_EXPERTS_2)
    padded = ((counts + MOE_BLOCK - 1) // MOE_BLOCK) * MOE_BLOCK
    pend = jnp.cumsum(padded)
    pstart = pend - padded
    ustart = jnp.cumsum(counts) - counts
    dest = pstart[sorted_e] + (jnp.arange(m) - ustart[sorted_e])
    n_blocks = -(-m // MOE_BLOCK) + N_EXPERTS_2
    n_rows = n_blocks * MOE_BLOCK
    row_tok = jnp.zeros((n_rows,), jnp.int32).at[dest].set(flat_tok[order])
    row_gate = jnp.zeros((n_rows,), jnp.float32).at[dest].set(flat_gate[order])
    block_e = jnp.minimum(
        jnp.searchsorted(pend, jnp.arange(n_blocks) * MOE_BLOCK, side='right'),
        N_EXPERTS_2 - 1)
    x_blocks = hf[row_tok].reshape(n_blocks, MOE_BLOCK, d)

    def expert_block(args):
        xb, e = args
        gu = xb @ w1[e] + b1[e]
        gate, up = jnp.split(gu, 2, axis=-1)
        gate = jnp.minimum(gate, SWIGLU_LIMIT)
        up = jnp.clip(up, -SWIGLU_LIMIT, SWIGLU_LIMIT)
        glu = gate * jax.nn.sigmoid(SWIGLU_ALPHA * gate)
        return ((up + 1.0) * glu) @ w2[e] + b2[e]

    y_rows = lax.map(expert_block, (x_blocks, block_e)).reshape(n_rows, d)
    y_rows = y_rows * row_gate[:, None].astype(y_rows.dtype)
    y = jnp.zeros((n_tok, d), h.dtype).at[row_tok].add(y_rows.astype(h.dtype))
    return y.reshape(bsz, s, d)

def second_inputs(seed: int = 0) -> dict:
    key = jax.random.key(seed)
    ks = jax.random.split(key, 32)
    f32 = jnp.float32
    L, D, G, P, W = DEPTH, D_MODEL, SSM_GROUPS, SSM_STATE, SSM_GROUP_WIDTH

    def nrm(k, shape, std):
        return jax.random.normal(k, shape, f32) * std

    a_im_base = jnp.pi * jnp.arange(P, dtype=f32)[None, None, :]
    return {
        'x': nrm(ks[0], (BATCH, SEQ, D), 1.0),
        'c': nrm(ks[1], (BATCH, D), 1.0),
        'w_ada': nrm(ks[2], (L, D, 6 * D), 0.5 * D ** -0.5),
        'b_ada': nrm(ks[3], (L, 6 * D), 0.01),
        'norm1_g': 1.0 + nrm(ks[4], (L, D), 0.01),
        'w_in': nrm(ks[5], (L, D, D_IN_PROJ), D ** -0.5),
        'lq1': nrm(ks[6], (L, ATTN_QK_DIM), 0.1),
        'lk1': nrm(ks[7], (L, ATTN_QK_DIM), 0.1),
        'lq2': nrm(ks[8], (L, ATTN_QK_DIM), 0.1),
        'lk2': nrm(ks[9], (L, ATTN_QK_DIM), 0.1),
        'subln_g': 1.0 + nrm(ks[10], (L, ATTN_V_DIM), 0.01),
        'ssm_a_re': -0.5 + nrm(ks[11], (L, G, P), 0.01),
        'ssm_a_im': a_im_base + nrm(ks[12], (L, G, P), 0.01),
        'ssm_log_dt': jax.random.uniform(ks[13], (L, G), f32,
                                         minval=math.log(DT_MIN), maxval=math.log(DT_MAX)),
        'ssm_b_re': nrm(ks[14], (L, G, P, W), (2 * W) ** -0.5),
        'ssm_b_im': nrm(ks[15], (L, G, P, W), (2 * W) ** -0.5),
        'ssm_c_re': nrm(ks[16], (L, G, W, P), (2 * P) ** -0.5),
        'ssm_c_im': nrm(ks[17], (L, G, W, P), (2 * P) ** -0.5),
        'ssm_d': nrm(ks[18], (L, D_SSM), 1.0),
        'w_glu': nrm(ks[19], (L, D_SSM, D_SSM), D_SSM ** -0.5),
        'b_glu': nrm(ks[20], (L, D_SSM), 0.01),
        'w_out': nrm(ks[21], (L, D_MIX, D), D_MIX ** -0.5),
        'norm2_g': 1.0 + nrm(ks[22], (L, D), 0.01),
        'w_router': nrm(ks[23], (L, D, N_EXPERTS_2), D ** -0.5),
        'b_router': nrm(ks[24], (L, N_EXPERTS_2), 0.01),
        'w1': nrm(ks[25], (L, N_EXPERTS_2, D, 2 * D_FF), D ** -0.5),
        'b1': nrm(ks[26], (L, N_EXPERTS_2, 2 * D_FF), 0.01),
        'w2': nrm(ks[27], (L, N_EXPERTS_2, D_FF, D), D_FF ** -0.5),
        'b2': nrm(ks[28], (L, N_EXPERTS_2, D), 0.01),
        'final_g': 1.0 + nrm(ks[29], (D,), 0.01),
    }

def second_block(x, c, w_ada, b_ada, norm1_g, w_in, lq1, lk1, lq2, lk2, subln_g,
              ssm_a_re, ssm_a_im, ssm_log_dt, ssm_b_re, ssm_b_im, ssm_c_re, ssm_c_im,
              ssm_d, w_glu, b_glu, w_out, norm2_g, w_router, b_router, w1, b1, w2, b2,
              final_g):
    bsz, s, _ = x.shape
    c_act = jax.nn.silu(c)
    for l in range(DEPTH):
        lambda_init = 0.8 - 0.6 * math.exp(-0.3 * l)
        mod = c_act @ w_ada[l] + b_ada[l]
        sh1, sc1, g1, sh2, sc2, g2 = jnp.split(mod, 6, axis=-1)

        h = _modulate(_rmsnorm(x, norm1_g[l]), sh1, sc1)
        proj = h @ w_in[l]
        q, k, v, u = jnp.split(proj, [D_ATTN, 2 * D_ATTN, 3 * D_ATTN], axis=-1)
        q = q.reshape(bsz, s, ATTN_HEADS, 2, ATTN_QK_DIM)
        k = k.reshape(bsz, s, ATTN_HEADS, 2, ATTN_QK_DIM)
        v = v.reshape(bsz, s, ATTN_HEADS, ATTN_V_DIM)
        lam = (jnp.exp(jnp.sum(lq1[l].astype(jnp.float32) * lk1[l].astype(jnp.float32)))
               - jnp.exp(jnp.sum(lq2[l].astype(jnp.float32) * lk2[l].astype(jnp.float32)))
               + lambda_init)
        attn_out = _diff_attention(q, k, v, lam, lambda_init, subln_g[l])
        ssm_out = _s5(u, ssm_a_re[l], ssm_a_im[l], ssm_log_dt[l], ssm_b_re[l], ssm_b_im[l],
                      ssm_c_re[l], ssm_c_im[l], ssm_d[l], w_glu[l], b_glu[l])
        mix = jnp.concatenate([attn_out, ssm_out.astype(attn_out.dtype)], axis=-1) @ w_out[l]
        x = x + g1[:, None, :] * mix

        h = _modulate(_rmsnorm(x, norm2_g[l]), sh2, sc2)
        x = x + g2[:, None, :] * _moe(h, w_router[l], b_router[l], w1[l], b1[l], w2[l], b2[l])
    return _rmsnorm(x, final_g)


def setup_inputs(seed=0):
    out = dict(first_inputs(seed))
    for name, value in second_inputs(seed + 1).items():
        if name != "x":
            out[name + "_2"] = value
    return out


def reference(
    x, attn_norm, w_in, w_cmp_k, w_cmp_v, cmp_pos, hg_lb_logits, hg_norm, w_br_nsa, w_br_hg,
    w_out, ffn_norm, w_grp, b_grp, w_rtr, b_rtr, w_gate, w_up, w_down, final_norm, c_2, w_ada_2,
    b_ada_2, norm1_g_2, w_in_2, lq1_2, lk1_2, lq2_2, lk2_2, subln_g_2, ssm_a_re_2, ssm_a_im_2,
    ssm_log_dt_2, ssm_b_re_2, ssm_b_im_2, ssm_c_re_2, ssm_c_im_2, ssm_d_2, w_glu_2, b_glu_2,
    w_out_2, norm2_g_2, w_router_2, b_router_2, w1_2, b1_2, w2_2, b2_2, final_g_2,
):
    x = first_block(
        x, attn_norm, w_in, w_cmp_k, w_cmp_v, cmp_pos, hg_lb_logits, hg_norm, w_br_nsa, w_br_hg,
        w_out, ffn_norm, w_grp, b_grp, w_rtr, b_rtr, w_gate, w_up, w_down, final_norm,
    )
    return second_block(
        x, c_2, w_ada_2, b_ada_2, norm1_g_2, w_in_2, lq1_2, lk1_2, lq2_2, lk2_2, subln_g_2,
        ssm_a_re_2, ssm_a_im_2, ssm_log_dt_2, ssm_b_re_2, ssm_b_im_2, ssm_c_re_2, ssm_c_im_2,
        ssm_d_2, w_glu_2, b_glu_2, w_out_2, norm2_g_2, w_router_2, b_router_2, w1_2, b1_2, w2_2,
        b2_2, final_g_2,
    )


_drawn_inputs = setup_inputs


def setup_inputs(seed=0):
    import zlib

    import numpy as np

    out = dict(_drawn_inputs(seed))
    spreads = {}
    factors = {'attn_norm': 4.212,
     'cmp_pos': 3.187,
     'hg_norm': 3.736,
     'b_grp': 8.0,
     'b_rtr': 7.124,
     'final_norm': 4.387,
     'b_ada_2': 3.291,
     'norm1_g_2': 8.0,
     'lq1_2': 6.937,
     'lk1_2': 5.326,
     'lk2_2': 5.032,
     'subln_g_2': 64.0,
     'ssm_a_re_2': 64.0,
     'ssm_a_im_2': 43.472,
     'ssm_log_dt_2': 47.2,
     'ssm_b_re_2': 58.976,
     'ssm_b_im_2': 64.0,
     'ssm_c_re_2': 54.888,
     'ssm_c_im_2': 53.912,
     'b_glu_2': 177.66,
     'norm2_g_2': 19.895,
     'b_router_2': 49.611,
     'b1_2': 33.774,
     'b2_2': 200.0,
     'final_g_2': 175.103,
     'ffn_norm': 2.928}
    for name, (base, spread) in spreads.items():
        noise = np.random.default_rng([zlib.crc32(name.encode()), seed]).standard_normal(out[name].shape)
        drawn = base * np.exp(spread * noise) if base else spread * noise
        out[name] = jnp.asarray(drawn.astype(out[name].dtype))
    for name, factor in factors.items():
        out[name] = (out[name] * factor).astype(out[name].dtype)
    return out
```

```python
import numpy as np
import concourse.bass as bass
from concourse import mybir
from contextlib import ExitStack

F32 = mybir.dt.float32
I32 = mybir.dt.int32
ALU = mybir.AluOpType
ACT = mybir.ActivationFunctionType
AX = mybir.AxisListType

T, D = 256, 1024
NT = T // 128
KC = D // 128
EPS = 1e-6
NEG = -1e30
IN_COLS = 5400
C_KV, C_GATE, C_HQ, C_HF, C_HI, C_HG, C_MRG = 512, 1280, 1304, 1816, 2328, 2840, 3352
NCMP = 15
NE = 32
CAP = 64
ROUNDS = T // CAP
PAIRS = NE // 2
RING = 6
UNIT = 4096
LEVELS = 7

WIDTHS = [("ident", 128), ("ones", 128), ("iota", 128), ("before", 128), ("causal", 128),
          ("lvl", LEVELS * 128), ("cos", NT * 8), ("sin", NT * 8), ("ccos", 8), ("csin", 8),
          ("cadd", NT * 16), ("cmul", NT * 16), ("tie32", 1024), ("tie8", 64), ("tie4", 16),
          ("even", 1), ("odd", 1), ("geven", 1), ("godd", 1), ("full", 256)]
CO = {}
NCST = 0
for _n, _w in WIDTHS:
    CO[_n] = (NCST, _w)
    NCST += _w


def constants():
    c = np.zeros((128, NCST), np.float32)

    def put(name, a):
        o, w = CO[name]
        c[:, o:o + w] = np.broadcast_to(np.asarray(a, np.float32).reshape(-1, w), (128, w))

    p = np.arange(128)
    put("ident", np.eye(128))
    put("ones", np.ones((128, 128)))
    s = np.arange(128) % 64
    put("iota", s)
    put("before", p[:, None] < p[None, :])
    put("causal", np.where(p[None, :] <= p[:, None], 0.0, NEG))
    lv = []
    for l in range(LEVELS):
        half, blk = 1 << l, 2 << l
        s_, t_ = p[:, None], p[None, :]
        lv.append((s_ // blk == t_ // blk) & (s_ % blk < half) & (t_ % blk >= half))
    put("lvl", np.stack(lv, 1).reshape(128, -1))
    inv = (np.float32(500000.0) ** (-np.arange(8, dtype=np.float32) / 8)).astype(np.float32)
    pos = np.arange(T, dtype=np.float32)
    ang = (pos[:, None] * inv[None, :]).reshape(NT, 128, 8).transpose(1, 0, 2)
    put("cos", np.cos(ang).reshape(128, -1))
    put("sin", np.sin(ang).reshape(128, -1))
    cang = ((p % 32) * 16).astype(np.float32)[:, None] * inv[None, :]
    put("ccos", np.cos(cang))
    put("csin", np.sin(cang))
    tp = np.arange(T).reshape(NT, 128).T
    ok = (np.arange(16)[None, None, :] * 16 + 31 <= tp[:, :, None])
    put("cadd", np.where(ok, 0.0, NEG).reshape(128, -1))
    put("cmul", ok.reshape(128, -1))
    for n in (32, 8, 4):
        i = np.arange(n)
        put(f"tie{n}", (i[None, :] < i[:, None]).reshape(-1))
    put("even", (p < 64)[:, None])
    put("odd", (p >= 64)[:, None])
    put("geven", ((p // 16) % 2 == 0)[:, None])
    put("godd", ((p // 16) % 2 == 1)[:, None])
    put("full", np.ones(256))
    return c


def bass_block_pair(nc, A, out):
    top = ExitStack()
    with top:
        def sbuf(ctx, name, shape, dt=F32):
            return ctx.enter_context(nc.sbuf_tensor(name, shape, dt))

        sems = {}
        cleared = []
        LASTING = {"units_used", "gain_in"} | {f"ring_ready{j}" for j in range(RING)}

        def S(name):
            if name not in sems:
                sems[name] = cleared.pop() if cleared else top.enter_context(nc.semaphore(name))
            return sems[name]

        def retire_semaphores():
            old = [n for n in sems if n not in LASTING]
            with nc.Block() as block:
                @block.gpsimd
                def _(g):
                    for n in old:
                        g.sem_clear(sems[n])
            for n in old:
                cleared.append(sems.pop(n))
            chains.clear()

        CS = sbuf(top, "CS", [128, NCST])
        ring = sbuf(top, "ring", [128, RING, UNIT])
        X = sbuf(top, "X", [128, NT, D])
        hn = sbuf(top, "hn", [128, NT, KC, 128])
        hT = sbuf(top, "hT", [128, KC, T])
        grow = sbuf(top, "grow", [128, D])
        st = sbuf(top, "st", [128, 8])
        junk = sbuf(top, "junk", [128, D])
        ps = top.enter_context(nc.psum_tensor("ps", [128, 8, 512], F32))

        def K(name, parts=128):
            o, w = CO[name]
            return CS[0:parts, o:o + w]

        ident = K("ident")
        ring_ready = [S(f"ring_ready{j}") for j in range(RING)]
        units_used = S("units_used")

        units = []

        def cols(w, c0, c1):
            return [(w[0].rearrange("(p t) n -> p t n", t=KC)[:, :, c0:c1], KC, c1 - c0)]

        def rows(w, t0, t1, nt):
            n = w.shape[-1]
            return [(w[0].rearrange("(t p) n -> p t n", t=nt)[:, t0:t1, :], t1 - t0, n)]

        SECT = [(0, 512), (512, 1024), (1024, C_HQ), (C_HF, C_HI), (C_HQ, C_HF), (C_HI, C_HG), (C_HG, C_MRG)] + \
               [(C_MRG + 512 * j, C_MRG + 512 * (j + 1)) for j in range(4)]
        for c0, c1 in SECT:
            units += cols(A["w_in"], c0, c1)
        K_BR = len(units)
        units += rows(A["w_br_nsa"], 0, 4, 4) + rows(A["w_br_hg"], 0, 4, 4)
        K_OUT = len(units)
        units += rows(A["w_out"], 0, 4, 8) + rows(A["w_out"], 4, 8, 8)
        K_MOE1 = len(units)
        units += [None] * (3 * NE)
        K_ADA = len(units)
        for j in range(12):
            units += cols(A["w_ada_2"], 512 * j, 512 * (j + 1))
        K_IN2 = len(units)
        for j in range(4):
            units += cols(A["w_in_2"], 512 * j, 512 * (j + 1))
        K_GLU = len(units)
        units += rows(A["w_glu_2"], 0, 4, 4)
        K_OUT2 = len(units)
        units += rows(A["w_out_2"], 0, 4, 8) + rows(A["w_out_2"], 4, 8, 8)
        K_MOE2 = len(units)
        units += [None] * (6 * NE)

        def load_unit(sp, k):
            if k >= RING:
                sp.wait_ge(units_used, k - RING + 1)
            if K_MOE1 <= k < K_ADA:
                src, dst = moe1_src(0, k - K_MOE1), ring[:, k % RING, :]
            elif k >= K_MOE2:
                src, dst = moe2_src(0, k - K_MOE2), ring[:, k % RING, :]
            else:
                src, n, w = units[k]
                dst = ring[:, k % RING, 0:n * w].rearrange("p (t n) -> p t n", t=n)
            sp.dma_start(dst, src).then_inc(ring_ready[k % RING], 16)

        def unit_arrived(pe, k):
            pe.wait_ge(ring_ready[k % RING], 16 * (k // RING + 1))

        def unit(k):
            n, w = units[k][1:]
            return ring[:, k % RING, 0:n * w].rearrange("p (t n) -> p t n", t=n)

        def moe1_src(e0, j):
            w = A[("w_gate", "w_up", "w_down")[j // 2]]
            t = 4 if j >= 4 else KC
            return w[0, bass.ds(e0 + j % 2, 1), :, :].rearrange("a (p t) n -> (a p) (t n)", t=t)

        def moe2_src(e0, j):
            e = bass.ds(e0 + j % 2, 1)
            if j < 8:
                return A["w1_2"][0, e, :, :].rearrange("a (p u t) n -> (a p) u (t n)", u=4, t=2)[:, j // 2, :]
            return A["w2_2"][0, e, :, :].rearrange("a (p u t) n -> (a p) u (t n)", u=2, t=4)[:, j // 2 - 4, :]

        def chain(eng, name):
            s, n = S(name), chains.setdefault(name, [0])

            def link(ins):
                n[0] += 1
                ins.then_inc(s, 1)
                eng.wait_ge(s, n[0])
            return link
        chains = {}

        class Norm:

            def __init__(self, tag, shift=None):
                self.tag, self.shift = tag, shift
                self.sq, self.sd, self.rt = S(tag + "_squares"), S(tag + "_variance"), S(tag + "_root")
                self.hn, self.tr, self.ev = S(tag + "_normed"), S(tag + "_transposed"), S(tag + "_hT")

            def act_root(self, a):
                a.wait_ge(self.sd, 1)
                nc.scalar.activation(st[:, 2:4], st[:, 2:4], ACT.Sqrt).then_inc(self.rt, 1)

            def act(self, a):
                self.act_root(a)
                for t in range(KC):
                    if t % 2 == 0:
                        a.wait_ge(self.tr, t // 2 + 1)
                        nc.scalar.activation(hT[:, t:t + 2, :].rearrange("p t q -> p (t q)"), ps[:, t // 2, :],
                                             ACT.Copy).then_inc(self.ev, 1)

            def dve_stats(self, v, link):
                for i in range(NT):
                    link(nc.vector.tensor_tensor_reduce(out=junk[:], in0=X[:, i, :], in1=X[:, i, :], scale=1.0,
                                                        scalar=0.0, op0=ALU.mult, op1=ALU.add,
                                                        accum_out=st[:, i:i + 1]))
                nc.vector.tensor_scalar(st[:, 2:4], st[:, 0:2], 1.0 / D, EPS, ALU.mult, ALU.add).then_inc(self.sd, 1)
                v.wait_ge(self.rt, 1)
                link(nc.vector.reciprocal(st[:, 4:6], st[:, 2:4]))

            def dve(self, v, link):
                self.dve_stats(v, link)
                for i in range(NT):
                    o = hn[:, i].rearrange("q t p -> q p t")
                    x = X[:, i, :].rearrange("q (p t) -> q p t", t=KC)
                    g = grow[:].rearrange("q (p t) -> q p t", t=KC)
                    ins = nc.vector.scalar_tensor_tensor(out=o, in0=x, scalar=st[:, 4 + i:5 + i], in1=g,
                                                         op0=ALU.mult, op1=ALU.mult)
                    if self.shift is not None:
                        link(ins)
                        b = self.shift.rearrange("q (p t) -> q p t", t=KC)
                        ins = nc.vector.tensor_tensor(o, o, b, ALU.add)
                    ins.then_inc(self.hn, 1)

            def pe(self, pe):
                for t in range(KC):
                    for i in range(NT):
                        pe.wait_ge(self.hn, i + 1)
                        ins = nc.tensor.transpose(ps[:, t // 2, (t % 2) * 256 + i * 128:(t % 2) * 256 + i * 128 + 128],
                                                  hn[:, i, t, :], ident)
                    if t % 2 == 1:
                        ins.then_inc(self.tr, 1)

        p1 = ExitStack()
        qkv = sbuf(p1, "qkv", [128, NT, C_HQ])
        hgi = sbuf(p1, "hgi", [128, NT, 512])
        hgg = sbuf(p1, "hgg", [128, NT, 512])
        mrg = sbuf(p1, "mrg", [128, NT, 2 * D])
        hqT = sbuf(p1, "hqT", [128, 4, T])
        hfT = sbuf(p1, "hfT", [128, 4, T])
        NATURAL = {0: (qkv, 0, 512), 1: (qkv, 512, 1024), 2: (qkv, 1024, C_HQ), 5: (hgi, 0, 512), 6: (hgg, 0, 512),
                   7: (mrg, 0, 512), 8: (mrg, 512, 1024), 9: (mrg, 1024, 1536), 10: (mrg, 1536, 2048)}
        FUNC = {3: ACT.Sigmoid, 6: ACT.Silu, 7: ACT.Sigmoid, 8: ACT.Sigmoid, 9: ACT.Sigmoid, 10: ACT.Sigmoid}
        n0 = Norm("n0")
        s_cst, s_x, s_grow = S("consts_in"), S("x_in"), S("gain_in")
        s_proj, s_pev = S("proj_done"), S("proj_kept")
        with nc.Block() as block:
            @block.sync
            def _(sp):
                sp.dma_start(X[:], A["x"][0].rearrange("(i q) d -> q i d", i=NT)).then_inc(s_x, 16)
                for k in range(K_BR + RING):
                    load_unit(sp, k)

            @block.scalar
            def _(a):
                a.dma_start(CS[:], A["cst"]).then_inc(s_cst, 16)
                a.dma_start(grow[:], A["attn_norm"].to_broadcast([128, D])).then_inc(s_grow, 16)
                n0.act(a)
                for u in range(K_BR):
                    for h in range(2):
                        n = 2 * u + h
                        a.wait_ge(s_proj, n + 1)
                        bank = 4 + n % 4
                        f = FUNC.get(u, ACT.Copy)
                        if u in NATURAL:
                            dst, c0, c1 = NATURAL[u]
                            ins = nc.scalar.activation(dst[:, h, c0:c1], ps[:, bank, 0:c1 - c0], f)
                        else:
                            dst = hqT if u == 4 else hfT
                            ins = nc.scalar.activation(dst[:, 2 * h:2 * h + 2, :].rearrange("p a b -> p (a b)"),
                                                       ps[:, bank, :], f)
                        ins.then_inc(s_pev, 1)
                a.wait_ge(s_pev, 2 * K_BR)
                nc.scalar.activation(qkv[:, :, C_GATE:C_HQ], qkv[:, :, C_GATE:C_HQ], ACT.Sigmoid).then_inc(s_pev, 1)

            @block.vector
            def _(v):
                link = chain(v, "v_chain")
                v.wait_ge(s_x, 16)
                v.wait_ge(s_grow, 16)
                n0.dve(v, link)

            @block.tensor
            def _(pe):
                pe.wait_ge(s_cst, 16)
                n0.pe(pe)
                pe.wait_ge(n0.ev, 4)
                for u in range(K_BR):
                    unit_arrived(pe, u)
                    w = unit(u)
                    width = units[u][2]
                    for h in range(2):
                        n = 2 * u + h
                        if n >= 4:
                            pe.wait_ge(s_pev, n - 3)
                        if u in NATURAL:
                            for t in range(KC):
                                ins = nc.tensor.matmul(ps[:, 4 + n % 4, 0:width], hT[:, t, h * 128:h * 128 + 128],
                                                       w[:, t, :], start=t == 0, stop=t == KC - 1)
                        else:
                            for cb in range(2):
                                c = (2 * h + cb) * 128
                                for t in range(KC):
                                    ins = nc.tensor.matmul(ps[:, 4 + n % 4, cb * 256:cb * 256 + 256],
                                                           w[:, t, c:c + 128], hT[:, t, :],
                                                           start=t == 0, stop=t == KC - 1)
                        ins.then_inc(s_proj, 1)
                    pe.wait_ge(s_proj, 2 * u + 2)
                    pe.sem_inc(units_used, 1)
        W1 = sbuf(p1, "W1", [128, 5376])
        qT = W1[:, 0:1024].rearrange("p (a q) -> p a q", a=4)
        kT = W1[:, 1024:2048].rearrange("p (a q) -> p a q", a=4)
        kvT = W1[:, 2048:2560].rearrange("p (g q) -> p g q", g=2)
        kvc = W1[:, 2560:3072].rearrange("p (i g c) -> p i g c", i=2, g=2)
        Sc = W1[:, 3072:3328].rearrange("p (i h n) -> p i h n", i=2, h=8)
        Pc = W1[:, 3328:3840].rearrange("p (i r g n) -> p i r g n", i=2, r=4, g=2)
        PcT = W1[0:64, 3840:4864].rearrange("p (i r q) -> p i r q", i=2, r=4)
        sm = W1[:, 4864:5376]
        kc, vcb = sm[0:64, 0:64], sm[0:64, 64:192]
        kcd = sm[0:64, 192:320]
        kcT = sm[:, 320:384]
        posT, lraw = sm[:, 384:416], sm[:, 416:424]
        wts = sm[:, 424:488]
        rt1 = junk[:, 0:512]
        kdup = junk[:].rearrange("p (i a b c) -> p i a b c", i=2, a=4, b=2)
        blkT = hn[:].rearrange("p i t q -> p (i t q)").rearrange("p (l g n) -> p l g n", l=32, g=2)
        Wc = hT[:].rearrange("p t q -> p (t q)").rearrange("p (l e) -> p l e", l=32)
        P = hn[:].rearrange("p i t q -> p (i t q)").rearrange("p (s a k) -> p s a k", s=2, a=4)
        PT = hT[:].rearrange("p t q -> p (t q)").rearrange("p (b h q) -> p b h q", b=2, h=8)
        pos2 = sbuf(p1, "pos2", [32, 128])
        lbn = sbuf(p1, "lbn", [8, 128])
        hgn = sbuf(p1, "hgn", [128, 1])
        rtmp = W1[:, 3072:3840]
        s_in, s_rope, s_tr, s_trk = S("nsa_small_in"), S("nsa_roped"), S("nsa_transposed"), S("nsa_transposes_kept")
        s_blk, s_cmp, s_kcd, s_kct, s_kctk = S("blocks_built"), S("compressed"), S("kcmp_roped"), S("kcmpT_done"), S("kcmpT_kept")
        s_sc, s_scs, s_sce, s_pc, s_pct, s_pctk = (S("cmp_scores"), S("cmp_shifted"), S("cmp_exp"), S("cmp_probs"),
                                                   S("cmp_probsT"), S("cmp_probsT_kept"))
        s_s, s_mx, s_exp, s_p, s_pt, s_ptk, s_pv = (S("scores"), S("scores_max"), S("scores_exp"),
                                                    S("probs"), S("probsT"), S("probsT_kept"), S("pv_done"))
        s_o, s_oT, s_oTk = S("nsa_out_kept"), S("nsa_outT"), S("nsa_outT_kept")
        onsa = junk[:].rearrange("p (i c) -> p i c", i=2)
        onT = grow[:].rearrange("p (a q) -> p a q", a=4)
        STEPS = [(i, ty) for i in range(NT) for ty in range(2)]

        def bc(ap, shape):
            return ap.to_broadcast(shape)

        with nc.Block() as block:
            @block.sync
            def _(sp):
                sp.dma_start(pos2[:, 0:64], A["cmp_pos"][0]).then_inc(s_in, 16)
                sp.dma_start(pos2[:, 64:128], A["cmp_pos"][0]).then_inc(s_in, 16)
                sp.dma_start(lbn[:], A["hg_lb_logits"].rearrange("r (h k) -> (r h) k", h=4)).then_inc(s_in, 16)
                sp.dma_start(Wc[0:64], A["w_cmp_k"][0].rearrange("(l d) e -> d l e", l=32)).then_inc(s_in, 16)
                sp.dma_start(Wc[64:128], A["w_cmp_v"][0].rearrange("(l d) e -> d l e", l=32)).then_inc(s_in, 16)
                sp.dma_start(hgn[:], A["hg_norm"].rearrange("a v -> v a")).then_inc(s_in, 16)

            @block.vector
            def _(v):
                link = chain(v, "v_chain")
                nv = nc.vector

                def rope(t1, t2, cos, sin, shape, tmp):
                    n = int(np.prod(shape[1:]))
                    names = "abcd"[:len(shape) - 1]
                    pat = "p (" + " ".join(names) + ") -> p " + " ".join(names)
                    kw = dict(zip(names, shape[1:]))
                    b = [tmp[0:shape[0], j * n:(j + 1) * n].rearrange(pat, **kw) for j in range(4)]
                    nv.tensor_tensor(b[0], t1, cos, ALU.mult)
                    nv.tensor_tensor(b[1], t2, sin, ALU.mult)
                    nv.tensor_tensor(b[2], t2, cos, ALU.mult)
                    link(nv.tensor_tensor(b[3], t1, sin, ALU.mult))
                    nv.tensor_tensor(t1, b[0], b[1], ALU.subtract)
                    return nv.tensor_tensor(t2, b[2], b[3], ALU.add)

                for i in range(NT):
                    cos = K("cos")[:, i * 8:i * 8 + 8]
                    sin = K("sin")[:, i * 8:i * 8 + 8]
                    q = qkv[:, i, 0:512].rearrange("p (h d) -> p h d", h=8)
                    link(rope(q[:, :, 0:8], q[:, :, 8:16], bc(cos.rearrange("p (a c) -> p a c", a=1), [128, 8, 8]),
                              bc(sin.rearrange("p (a c) -> p a c", a=1), [128, 8, 8]), [128, 8, 8], rtmp))
                    for c in (768, 1024):
                        k = qkv[:, i, c:c + 128].rearrange("p (h d) -> p h d", h=2)
                        link(rope(k[:, :, 0:8], k[:, :, 8:16], bc(cos.rearrange("p (a c) -> p a c", a=1), [128, 2, 8]),
                                  bc(sin.rearrange("p (a c) -> p a c", a=1), [128, 2, 8]), [128, 2, 8], rtmp))
                for i in range(NT):
                    for ty in range(2):
                        src = qkv[:, i, 768 + 256 * ty:768 + 256 * ty + 128].rearrange("p (g a d) -> p g a d", g=2, a=1)
                        nv.tensor_copy(kdup[:, i, 2 * ty:2 * ty + 2], bc(src, [128, 2, 2, 64]))
                    src = qkv[:, i, 512:768].rearrange("p (k g d) -> p g k d", k=2, g=2)
                    ins = nv.tensor_copy(kvc[:, i].rearrange("p g (k d) -> p g k d", k=2), src)
                ins.then_inc(s_rope, 1)
                link(nv.memset(blkT[:, :, :, :], 0.0))
                v.wait_ge(s_trk, 6)
                for g in range(2):
                    for a in range(2):
                        src = kvT[:, g, 16 * a:16 * a + 240].rearrange("p (n b) -> p b n", b=16)
                        po = posT[:, 16 * a:16 * a + 16].rearrange("p (b n) -> p b n", n=1)
                        nv.tensor_tensor(blkT[:, 16 * a:16 * a + 16, g, 0:NCMP], src, bc(po, [128, 16, NCMP]),
                                         ALU.add).then_inc(s_blk, 1)
                v.wait_ge(s_cmp, 1)
                link(nv.tensor_copy(kc, ps[0:64, 6, 0:64]))
                link(nv.memset(vcb, 0.0))
                nv.tensor_copy(vcb[0:32, 0:64], ps[0:32, 7, 0:64])
                link(nv.tensor_copy(vcb[32:64, 64:128], ps[32:64, 7, 0:64]))
                link(rope(kc[:, 0:8], kc[:, 8:16], K("ccos", 64), K("csin", 64), [64, 8], rtmp))
                nv.tensor_copy(kcd.rearrange("p (a d) -> p a d", a=2), bc(kc.rearrange("p (a d) -> p a d", a=1), [64, 2, 64])).then_inc(s_kcd, 1)
                v.wait_ge(s_sc, 1)
                for i in range(NT):
                    add = K("cadd")[:, i * 16:i * 16 + 16].rearrange("p (a n) -> p a n", a=1)
                    for par in range(2):
                        o = Sc[:, i].rearrange("p (a b) n -> p a b n", b=2)[:, :, par, :]
                        link(nv.tensor_tensor(o, ps[:, 6 + par, i * 64:i * 64 + 64].rearrange("p (a n) -> p a n", a=4),
                                              bc(add, [128, 4, 16]), ALU.add))
                S16 = Sc[:].rearrange("p i h n -> p (i h) n")[:, :, 0:NCMP]
                mx, su = wts[:, 0:16], wts[:, 16:32]
                link(nv.tensor_reduce(mx, S16, AX.X, ALU.max))
                nv.tensor_tensor(S16, S16, bc(mx.rearrange("p (h n) -> p h n", n=1), [128, 16, NCMP]),
                                 ALU.subtract).then_inc(s_scs, 1)
                v.wait_ge(s_sce, 1)
                link(nv.tensor_reduce(su, S16, AX.X, ALU.add))
                link(nv.reciprocal(su, su))
                link(nv.tensor_tensor(su.rearrange("p (i h) -> p i h", i=2), su.rearrange("p (i h) -> p i h", i=2),
                                      qkv[:, :, C_GATE:C_HQ].rearrange("p i (h b) -> p i h b", b=3)[:, :, :, 0], ALU.mult))
                link(nv.tensor_tensor(S16, S16, bc(su.rearrange("p (h n) -> p h n", n=1), [128, 16, NCMP]), ALU.mult))
                link(nv.memset(Pc[:, :, :, :, :], 0.0))
                for i in range(NT):
                    for g in range(2):
                        mul = K("cmul")[:, i * 16:i * 16 + NCMP].rearrange("p (a n) -> p a n", a=1)
                        nv.tensor_tensor(Pc[:, i, :, g, 0:NCMP], Sc[:, i, 4 * g:4 * g + 4, 0:NCMP],
                                         bc(mul, [128, 4, NCMP]), ALU.mult).then_inc(s_pc, 1)
                for n, (i, ty) in enumerate(STEPS):
                    nk = 128 * (i + 1)
                    Pv = P[:, :, :, 0:nk]
                    P8 = P[:].rearrange("p s a k -> p (s a) k")[:, :, 0:nk]
                    v.wait_ge(s_s, n + 1)
                    if n:
                        v.wait_ge(s_pt, n)
                    src = ps[:, 2:6, :].rearrange("p b (a k) -> p (b a) k", a=2)
                    ca = K("causal").rearrange("p (a k) -> p a k", a=1)
                    link(nv.tensor_tensor(P8[:, :, nk - 128:nk], src[:, :, nk - 128:nk], bc(ca, [128, 8, 128]), ALU.add))
                    if i:
                        link(nv.tensor_copy(P8[:, :, 0:128], src[:, :, 0:128]))
                    m8, w8 = wts[:, 32:40], wts[:, 48:56]
                    link(nv.tensor_reduce(m8, P8, AX.X, ALU.max))
                    nv.tensor_scalar(wts[:, 40:48], m8, -0.125, None, ALU.mult).then_inc(s_mx, 1)
                    v.wait_ge(s_exp, n + 1)
                    link(nv.reciprocal(w8, w8))
                    gate = qkv[:, i, C_GATE:C_HQ].rearrange("p (a s b) -> p s a b", s=2, b=3)[:, :, :, 1 + ty]
                    link(nv.tensor_tensor(w8.rearrange("p (s a) -> p s a", s=2), w8.rearrange("p (s a) -> p s a", s=2), gate, ALU.mult))
                    nv.tensor_tensor(P8, P8, bc(w8.rearrange("p (h n) -> p h n", n=1), [128, 8, nk]), ALU.mult).then_inc(s_p, 1)

            @block.scalar
            def _(a):
                link = chain(a, "a_chain")
                na = nc.scalar
                a.wait_ge(s_tr, 1)
                for b in range(5):
                    dst = [qT[:, 0:2], qT[:, 2:4], kT[:, 0:2], kT[:, 2:4], kvT[:]][b]
                    na.activation(dst, ps[:, b, :].rearrange("p (a q) -> p a q", a=2), ACT.Copy).then_inc(s_trk, 1)
                na.activation(sm[:, 384:424], ps[:, 5, 0:40], ACT.Copy).then_inc(s_trk, 1)
                a.wait_ge(s_kct, 1)
                na.activation(kcT, ps[:, 5, 128:192], ACT.Copy).then_inc(s_kctk, 1)
                a.wait_ge(s_scs, 1)
                S16 = Sc[:].rearrange("p i h n -> p (i h) n")[:, :, 0:NCMP]
                na.activation(S16, S16, ACT.Exp, scale=0.125).then_inc(s_sce, 1)
                a.wait_ge(s_pct, 1)
                for i in range(NT):
                    na.activation(PcT[:, i], ps[0:64, i, :].rearrange("p (r q) -> p r q", r=4), ACT.Copy).then_inc(s_pctk, 1)
                for n, (i, ty) in enumerate(STEPS):
                    nk = 128 * (i + 1)
                    a.wait_ge(s_mx, n + 1)
                    for h in range(8):
                        row = P[:].rearrange("p s a k -> p (s a) k")[:, h, 0:nk]
                        ins = na.activation(row, row, ACT.Exp, bias=wts[:, 40 + h:41 + h], scale=0.125,
                                            accum_out=wts[:, 48 + h:49 + h])
                    ins.then_inc(s_exp, 1)
                    a.wait_ge(s_pt, n + 1)
                    if n:
                        a.wait_ge(s_pv, n)
                    for kb in range(i + 1):
                        na.activation(PT[:, kb], ps[:, 2 + 2 * kb:4 + 2 * kb, :].rearrange("p b (c q) -> p (b c) q", c=4),
                                      ACT.Copy).then_inc(s_ptk, 1)
                    if ty:
                        a.wait_ge(s_pv, n + 1)
                        na.activation(onsa[:, i], ps[:, 6 + i, :], ACT.Copy).then_inc(s_o, 1)
                a.wait_ge(s_oT, 1)
                for b in range(2):
                    na.activation(onT[:, 2 * b:2 * b + 2], ps[:, b, :].rearrange("p (a q) -> p a q", a=2), ACT.Copy).then_inc(s_oTk, 1)

            @block.tensor
            def _(pe):
                nt = nc.tensor
                pe.wait_ge(s_rope, 1)
                pe.wait_ge(s_in, 96)
                for i in range(NT):
                    for hp in range(4):
                        nt.transpose(ps[:, hp // 2, (hp % 2) * 256 + i * 128:(hp % 2) * 256 + i * 128 + 128],
                                     qkv[:, i, hp * 128:hp * 128 + 128], ident)
                    for x in range(4):
                        nt.transpose(ps[:, 2 + x // 2, (x % 2) * 256 + i * 128:(x % 2) * 256 + i * 128 + 128],
                                     kdup[:, i, x].rearrange("p b c -> p (b c)"), ident)
                    for g in range(2):
                        nt.transpose(ps[:, 4, g * 256 + i * 128:g * 256 + i * 128 + 128], kvc[:, i, g, :], ident)
                nt.transpose(ps[:, 5, 0:32], pos2[:], K("ident", 32)[:, 0:32])
                nt.transpose(ps[:, 5, 32:40], lbn[:], K("ident", 8)[:, 0:8]).then_inc(s_tr, 1)
                pe.wait_ge(s_blk, 4)
                for l in range(32):
                    nt.matmul(ps[0:64, 6, 0:64], blkT[0:64, l].rearrange("p g n -> p (g n)"), Wc[0:64, l, :],
                              start=l == 0, stop=l == 31)
                    ins = nt.matmul(ps[0:64, 7, 0:64], blkT[64:128, l].rearrange("p g n -> p (g n)"), Wc[64:128, l, :],
                                    start=l == 0, stop=l == 31)
                ins.then_inc(s_cmp, 1)
                pe.wait_ge(s_kcd, 1)
                nt.transpose(ps[:, 5, 128:192], kcd, K("ident", 64)[:, 0:64]).then_inc(s_kct, 1)
                pe.wait_ge(s_kctk, 1)
                for i in range(NT):
                    for h in range(8):
                        r = 64 * (h % 2)
                        ins = nt.matmul(ps[:, 6 + h % 2, i * 64 + (h // 2) * 16:i * 64 + (h // 2) * 16 + 16],
                                        qT[r:r + 64, h // 2, i * 128:i * 128 + 128], kcT[r:r + 64, (h // 4) * 32:(h // 4) * 32 + 16],
                                        start=True, stop=True)
                ins.then_inc(s_sc, 1)
                pe.wait_ge(s_pc, 4)
                for i in range(NT):
                    for r in range(4):
                        ins = nt.transpose(ps[0:64, i, r * 128:r * 128 + 128], Pc[:, i, r].rearrange("p g n -> p (g n)"), ident)
                ins.then_inc(s_pct, 1)
                pe.wait_ge(s_pctk, 2)
                for n, (i, ty) in enumerate(STEPS):
                    if n:
                        pe.wait_ge(s_ptk, [0, 1, 2, 4][n])
                    for h in range(8):
                        par, a4 = h % 2, h // 2
                        r = 64 * par
                        for kb in range(i + 1):
                            c = (a4 % 2) * 256 + kb * 128
                            ins = nt.matmul(ps[:, 2 + 2 * par + a4 // 2, c:c + 128], qT[r:r + 64, a4, i * 128:i * 128 + 128],
                                            kT[r:r + 64, 2 * ty + h // 4, kb * 128:kb * 128 + 128], start=True, stop=True)
                    ins.then_inc(s_s, 1)
                    if ty == 0:
                        for r in range(4):
                            o = ps[:, 6 + i, :].rearrange("p (g r d) -> p g r d", g=2, r=4)[:, :, r, :]
                            nt.matmul(o, PcT[:, i, r, :], vcb.rearrange("p (g d) -> p g d", g=2), start=r == 0, stop=False,
                                      skip_group_check=True)
                    pe.wait_ge(s_p, n + 1)
                    for kb in range(i + 1):
                        for h in range(8):
                            par, a4 = h // 4, h % 4
                            ins = nt.transpose(ps[:, 2 + 2 * kb + h // 4, (h % 4) * 128:(h % 4) * 128 + 128],
                                               P[:, par, a4, kb * 128:kb * 128 + 128], ident)
                    ins.then_inc(s_pt, 1)
                    pe.wait_ge(s_ptk, [1, 2, 4, 6][n])
                    for s8 in range(8):
                        h = 2 * (s8 % 4) + s8 // 4
                        for kb in range(i + 1):
                            c = 896 + 256 * ty + (h // 4) * 64
                            ins = nt.matmul(ps[:, 6 + i, h * 64:h * 64 + 64], PT[:, kb, s8, :], qkv[:, kb, c:c + 64],
                                            start=False, stop=(ty == 1 and s8 == 7 and kb == i), skip_group_check=True)
                    ins.then_inc(s_pv, 1)
                pe.wait_ge(s_o, 2)
                for i in range(NT):
                    for c in range(4):
                        ins = nt.transpose(ps[:, c // 2, (c % 2) * 256 + i * 128:(c % 2) * 256 + i * 128 + 128],
                                           onsa[:, i, c * 128:c * 128 + 128], ident)
                ins.then_inc(s_oT, 1)
        hnf = hn[:].rearrange("p i t q -> p (i t q)")
        hTf = hT[:].rearrange("p t q -> p (t q)")
        Dl = [hnf[:, 0:1024], hnf[:, 1024:2048]]
        QK = [hTf[:, 0:1024], hTf[:, 1024:2048]]
        bsum, kk = W1[:, 0:1024], W1[:, 1024:2048]
        Am = [W1[:, 2048:2560], W1[:, 2560:3072], W1[:, 3072:3584]]
        hp_ = W1[:, 3584:4096]
        osq = W1[:, 3584:4608].rearrange("p (i c) -> p i c", i=2)
        hst = sm[:, 424:448]
        lb, oml = sm[:, 448:452], sm[:, 452:456]
        ohn = bsum.rearrange("p (i c) -> p i c", i=2)
        ohT = kk.rearrange("p (a q) -> p a q", a=4)
        h_f, h_ln, h_d, h_e, h_qk, h_a, h_am = (S("forget"), S("log_forget"), S("level_exponents"), S("level_factors"),
                                                S("level_operands"), S("level_products"), S("level_added"))
        h_o, h_sq, h_v, h_r, h_n, h_t, h_tk, h_lb = (S("hg_out"), S("hg_squares"), S("hg_variance"), S("hg_root"), S("hg_normed"),
                                               S("hg_outT"), S("hg_outT_kept"), S("hg_bound"))
        hq, hf = hqT[:].rearrange("p h t -> p (h t)"), hfT[:].rearrange("p h t -> p (h t)")
        SEGS = [(L, L % 2) for L in range(LEVELS + 1)]
        with nc.Block() as block:
            @block.vector
            def _(v):
                link = chain(v, "v_chain")
                nv = nc.vector
                nv.tensor_tensor(lb, lraw[:, 0:4], lraw[:, 4:8], ALU.subtract).then_inc(h_lb, 1)
                v.wait_ge(h_lb, 2)
                link(nv.tensor_scalar(oml, lb, -1.0, 1.0, ALU.mult, ALU.add))
                for h in range(4):
                    ins = nv.tensor_scalar(hfT[:, h], hfT[:, h], oml[:, h:h + 1], lb[:, h:h + 1], ALU.mult, ALU.add)
                link(ins)
                nv.tensor_scalar(kk, hf, -1.0, 1.0, ALU.mult, ALU.add).then_inc(h_f, 1)
                v.wait_ge(h_ln, 1)
                for h in range(4):
                    ins = nv.tensor_tensor_scan(bsum[:, h * T:h * T + T], K("full"), hfT[:, h], 0.0, ALU.mult, ALU.add)
                link(ins)

                def products(n):
                    v.wait_ge(h_a, n + 1)
                    m = ident if n == 0 else K("lvl")[:, (n - 1) * 128:n * 128]
                    m = bc(m.rearrange("p (a t) -> p a t", a=1), [128, 4, 128])
                    for i in range(NT):
                        src = ps[:, 2 * (n % 2) + i, :].rearrange("p (h t) -> p h t", h=4)
                        if n == 0:
                            link(nv.tensor_tensor(Am[i].rearrange("p (h t) -> p h t", h=4), src, m, ALU.mult))
                            continue
                        link(nv.tensor_tensor(hp_.rearrange("p (h t) -> p h t", h=4), src, m, ALU.mult))
                        link(nv.tensor_tensor(Am[i], Am[i], hp_, ALU.add))
                    nv.nop().then_inc(h_am, 1)

                for L, d in SEGS:
                    half = 1 << L
                    bv = bsum.rearrange("p (n k) -> p n k", k=2 * half)
                    dv = Dl[d].rearrange("p (n k) -> p n k", k=2 * half)
                    qv = QK[d].rearrange("p (n k) -> p n k", k=2 * half)
                    hv = hq.rearrange("p (n k) -> p n k", k=2 * half)
                    kv = kk.rearrange("p (n k) -> p n k", k=2 * half)
                    ref = bc(bv[:, :, half - 1:half], [128, 512 // half, half])
                    nv.tensor_tensor(dv[:, :, half:], bv[:, :, half:], ref, ALU.subtract)
                    nv.tensor_tensor(dv[:, :, 0:half], ref, bv[:, :, 0:half], ALU.subtract).then_inc(h_d, 1)
                    if L:
                        products(L - 1)
                    v.wait_ge(h_e, L + 1)
                    if L >= 2:
                        v.wait_ge(h_a, L)
                    nv.tensor_tensor(qv[:, :, half:], hv[:, :, half:], dv[:, :, half:], ALU.mult)
                    nv.tensor_tensor(qv[:, :, 0:half], kv[:, :, 0:half], dv[:, :, 0:half], ALU.mult).then_inc(h_qk, 1)
                products(LEVELS)
                v.wait_ge(h_a, LEVELS + 2)
                nv.tensor_copy(Am[2], ps[:, 6, :]).then_inc(h_am, 1)
                v.wait_ge(h_sq, 2)
                link(nv.tensor_reduce(hst[:, 0:8], osq[:].rearrange("p i (h c) -> p (i h) c", h=4), AX.X, ALU.add))
                nv.tensor_scalar(hst[:, 8:16], hst[:, 0:8], 1.0 / 128, EPS, ALU.mult, ALU.add).then_inc(h_v, 1)
                v.wait_ge(h_r, 1)
                link(nv.reciprocal(hst[:, 16:24], hst[:, 8:16]))
                for i in range(NT):
                    r = bc(hst[:, 16 + 4 * i:20 + 4 * i].rearrange("p (h n) -> p h n", n=1), [128, 4, 128])
                    o = ohn[:, i].rearrange("p (h c) -> p h c", h=4)
                    link(nv.tensor_tensor(o, ps[:, 4 + i, :].rearrange("p (h c) -> p h c", h=4), r, ALU.mult))
                    nv.tensor_tensor(ohn[:, i], ohn[:, i], hgg[:, i], ALU.mult).then_inc(h_n, 1)

            @block.scalar
            def _(a):
                na = nc.scalar
                a.wait_ge(h_lb, 1)
                na.activation(lb, lb, ACT.Sigmoid).then_inc(h_lb, 1)
                a.wait_ge(h_f, 1)
                na.activation(hf, hf, ACT.Ln).then_inc(h_ln, 1)
                for L, d in SEGS:
                    a.wait_ge(h_d, L + 1)
                    na.activation(Dl[d], Dl[d], ACT.Exp).then_inc(h_e, 1)
                for i in range(NT):
                    a.wait_ge(h_o, i + 1)
                    a.wait_ge(h_am, LEVELS + 2)
                    na.activation(osq[:, i], ps[:, 4 + i, :], ACT.Square).then_inc(h_sq, 1)
                a.wait_ge(h_v, 1)
                na.activation(hst[:, 8:16], hst[:, 8:16], ACT.Sqrt).then_inc(h_r, 1)
                a.wait_ge(h_t, 1)
                for b in range(2):
                    na.activation(ohT[:, 2 * b:2 * b + 2], ps[:, b, :].rearrange("p (a q) -> p a q", a=2), ACT.Copy,
                                  scale=hgn[:, 0:1]).then_inc(h_tk, 1)

            @block.tensor
            def _(pe):
                nt = nc.tensor
                pe.wait_ge(h_f, 1)
                for n in range(LEVELS + 2):
                    if n:
                        pe.wait_ge(h_qk, n)
                    if 2 <= n <= LEVELS:
                        pe.wait_ge(h_am, n - 1)
                    if n <= LEVELS:
                        for i in range(NT):
                            for h in range(4):
                                c = h * T + i * 128
                                kx, qx = (kk, hq) if n == 0 else (QK[(n - 1) % 2], QK[(n - 1) % 2])
                                ins = nt.matmul(ps[:, 2 * (n % 2) + i, h * 128:h * 128 + 128], kx[:, c:c + 128], qx[:, c:c + 128],
                                                start=True, stop=True)
                    else:
                        for h in range(4):
                            x = QK[(n - 1) % 2]
                            ins = nt.matmul(ps[:, 6, h * 128:h * 128 + 128], x[:, h * T:h * T + 128], x[:, h * T + 128:h * T + 256],
                                            start=True, stop=True)
                    ins.then_inc(h_a, 1)
                pe.wait_ge(h_am, LEVELS + 2)
                for i in range(NT):
                    for h in range(4):
                        c = slice(h * 128, h * 128 + 128)
                        if i:
                            nt.matmul(ps[:, 5, c], Am[2][:, c], hgi[:, 0, c], start=True, stop=False)
                        ins = nt.matmul(ps[:, 4 + i, c], Am[i][:, c], hgi[:, i, c], start=i == 0, stop=True)
                    ins.then_inc(h_o, 1)
                pe.wait_ge(h_n, 2)
                for i in range(NT):
                    for h in range(4):
                        ins = nt.transpose(ps[:, h // 2, (h % 2) * 256 + i * 128:(h % 2) * 256 + i * 128 + 128],
                                           ohn[:, i, h * 128:h * 128 + 128], ident)
                ins.then_inc(h_t, 1)

        b_m, b_mx, b_t, b_tk, b_o, b_x = (S("branch_done"), S("mixed"), S("mixedT"), S("mixedT_kept"), S("out_proj"), S("x1"))
        with nc.Block() as block:
            @block.sync
            def _(sp):
                for k in range(K_BR + RING, K_MOE1 + RING):
                    load_unit(sp, k)

            @block.tensor
            def _(pe):
                nt = nc.tensor
                for br, (src) in enumerate((onT, ohT)):
                    unit_arrived(pe, K_BR + br)
                    w = unit(K_BR + br)
                    for i in range(NT):
                        for h in range(2):
                            for c in range(4):
                                ins = nt.matmul(ps[:, 4 * i + 2 * br + h, :], src[:, c, i * 128:i * 128 + 128],
                                                w[:, c, h * 512:h * 512 + 512], start=c == 0, stop=c == 3)
                    ins.then_inc(b_m, 1)
                pe.wait_ge(b_m, 2)
                pe.sem_inc(units_used, 2)
                for t in range(KC):
                    for i in range(NT):
                        pe.wait_ge(b_mx, i + 1)
                        ins = nt.transpose(ps[:, t // 2, (t % 2) * 256 + i * 128:(t % 2) * 256 + i * 128 + 128],
                                           mrg[:, i, t * 128:t * 128 + 128], ident)
                    if t % 2:
                        ins.then_inc(b_t, 1)
                pe.wait_ge(b_tk, 4)
                for k in range(2):
                    unit_arrived(pe, K_OUT + k)
                    for i in range(NT):
                        for h in range(2):
                            for c in range(4):
                                ins = nt.matmul(ps[:, 4 + 2 * i + h, :], hT[:, 4 * k + c, i * 128:i * 128 + 128],
                                                unit(K_OUT + k)[:, c, h * 512:h * 512 + 512], start=k == 0 and c == 0,
                                                stop=k == 1 and c == 3)
                    ins.then_inc(b_o, 1)
                pe.wait_ge(b_o, 2)
                pe.sem_inc(units_used, 2)

            @block.scalar
            def _(a):
                a.wait_ge(b_m, 2)
                a.dma_start(grow[:], A["ffn_norm"].to_broadcast([128, D])).then_inc(s_grow, 16)
                for t in range(4):
                    a.wait_ge(b_t, t + 1)
                    nc.scalar.activation(hT[:, 2 * t:2 * t + 2, :].rearrange("p t q -> p (t q)"), ps[:, t, :],
                                         ACT.Copy).then_inc(b_tk, 1)

            @block.vector
            def _(v):
                link = chain(v, "v_chain")
                v.wait_ge(b_m, 2)
                for i in range(NT):
                    link(nc.vector.tensor_tensor(mrg[:, i, :], mrg[:, i, :], ps[:, 4 * i:4 * i + 4, :].rearrange("p b c -> p (b c)"), ALU.mult))
                    nc.vector.tensor_tensor(mrg[:, i, 0:D], mrg[:, i, 0:D], mrg[:, i, D:2 * D], ALU.add).then_inc(b_mx, 1)
                v.wait_ge(b_o, 2)
                for i in range(NT):
                    nc.vector.tensor_tensor(X[:, i, :], X[:, i, :], ps[:, 4 + 2 * i:6 + 2 * i, :].rearrange("p b c -> p (b c)"),
                                            ALU.add).then_inc(b_x, 1)
        p1.close()

        def mixture(tag, base, per_pair, w_src, router, bias, topk, first, norm, after, acc_in_x):
            m = ExitStack()
            nr = 36 if first else 32
            FT = 4 if first else 8
            UP = 6 - 2 if first else 8
            BU = 2 if first else 4
            A0, C0 = 4, 6
            def s(n):
                return S(tag + n)

            wr = sbuf(m, tag + "wr", [128, KC, nr])
            brow = sbuf(m, tag + "brow", [1, nr])
            lgE = sbuf(m, tag + "lgE", [128, NT, 32])
            ex = sbuf(m, tag + "ex", [128, NT, 36])
            rk = sbuf(m, tag + "rk", [128, NT, 36])
            sel = sbuf(m, tag + "sel", [128, NT, 32])
            comb = sbuf(m, tag + "comb", [128, NT, 32])
            posx = sbuf(m, tag + "posx", [128, NT, 34])
            rs = sbuf(m, tag + "rs", [128, 16])
            cnt = sbuf(m, tag + "cnt", [128, 1], I32)
            hTf = hT[:].rearrange("p t q -> p (t q)")
            if not first:
                b1s = sbuf(m, "b1s", [32, 2048])
                b2s = sbuf(m, "b2s", [32, D])
                cT = sbuf(m, "cT", [32, T])
            e3 = ex[:].rearrange("p i n -> p (i n)")
            exE, exG = e3[:, 0:64], e3[:, 64:72]
            r3 = rk[:].rearrange("p i n -> p (i n)")
            rkE, rkG = r3[:, 0:64], r3[:, 64:72]
            q_in, q_lg, q_ex, q_exd, q_sel, q_pos, q_cnt, q_bT, q_bTk, q_b2, q_acc = (
                s("router_in"), s("logits"), s("shifted"), s("exp"), s("selected"), s("positions"), s("slots"),
                s("combT"), s("combT_kept"), s("bias_out"), s("acc_set"))
            acc = X if acc_in_x else sbuf(m, "acc", [128, NT, D])
            with nc.Block() as block:
                @block.scalar
                def _(a):
                    a.dma_start(wr[:, :, 0:nr - 32], A["w_grp"][0].rearrange("(p t) n -> p t n", t=KC)).then_inc(q_in, 16) if first else None
                    a.dma_start(wr[:, :, nr - 32:nr], A[router][0].rearrange("(p t) n -> p t n", t=KC)).then_inc(q_in, 16)
                    if first:
                        a.dma_start(brow[:, 0:4], A["b_grp"]).then_inc(q_in, 16)
                    a.dma_start(brow[:, nr - 32:nr], A[bias]).then_inc(q_in, 16)
                    if not first:
                        a.dma_start(b1s[:], A["b1_2"][0]).then_inc(q_in, 16)
                        a.dma_start(b2s[:], A["b2_2"][0]).then_inc(q_in, 16)
                    norm.act(a)
                    a.wait_ge(q_ex, 1)
                    w = 72 if first else 64
                    nc.scalar.activation(e3[:, 0:w], e3[:, 0:w], ACT.Exp).then_inc(q_exd, 1)
                    if not first:
                        a.wait_ge(q_bT, 1)
                        nc.scalar.activation(cT[:], ps[0:32, 6, 0:T], ACT.Copy).then_inc(q_bTk, 1)

                @block.vector
                def _(v):
                    link = chain(v, "v_chain")
                    nv = nc.vector
                    v.wait_ge(s_grow, 16 * norm.gains)
                    norm.dve(v, link)
                    v.wait_ge(q_lg, 1)
                    lp = ps[:, 4, 0:128].rearrange("p (i n) -> p i n", i=NT)
                    lg = lgE[:]
                    link(nv.tensor_copy(lg, lp[:, :, nr - 32:nr]))
                    n = 8 if first else 32
                    lv = lg.rearrange("p i (g n) -> p (i g) n", n=n)
                    G = 64 // n
                    mx = rs[:, 0:G]
                    link(nv.tensor_reduce(mx, lv, AX.X, ALU.max))
                    ins = nv.tensor_tensor(exE.rearrange("p (g n) -> p g n", n=n), lv,
                                           bc(mx.rearrange("p (g n) -> p g n", n=1), [128, G, n]), ALU.subtract)
                    if first:
                        lgG = rkG.rearrange("p (i n) -> p i n", i=NT)
                        link(nv.tensor_copy(lgG, lp[:, :, 0:4]))
                        link(nv.tensor_reduce(rs[:, 8:10], lgG, AX.X, ALU.max))
                        ins = nv.tensor_tensor(exG.rearrange("p (i n) -> p i n", i=NT), lgG,
                                               bc(rs[:, 8:10].rearrange("p (i n) -> p i n", n=1), [128, NT, 4]), ALU.subtract)
                    ins.then_inc(q_ex, 1)

                    def rank(out, l, g, k):
                        b1_ = hTf[:, 0:g * k * k].rearrange("p (g i j) -> p g i j", g=g, i=k)
                        b2_ = hTf[:, 1024:1024 + g * k * k].rearrange("p (g i j) -> p g i j", g=g, i=k)
                        lj = bc(l.rearrange("p g (a j) -> p g a j", a=1), [128, g, k, k])
                        li = bc(l.rearrange("p g (i a) -> p g i a", a=1), [128, g, k, k])
                        tie = bc(K(f"tie{k}").rearrange("p (g i j) -> p g i j", g=1, i=k), [128, g, k, k])
                        nv.tensor_tensor(b1_, lj, li, ALU.is_gt)
                        link(nv.tensor_tensor(b2_, lj, li, ALU.is_equal))
                        link(nv.tensor_tensor(b2_, b2_, tie, ALU.mult))
                        link(nv.tensor_tensor(b1_, b1_, b2_, ALU.add))
                        link(nv.tensor_reduce(out, b1_, AX.X, ALU.add))

                    if first:
                        rank(rkE.rearrange("p (g i) -> p g i", g=G), lv, G, n)
                        gl = rs[:, 0:8].rearrange("p (i n) -> p i n", i=NT)
                        link(nv.tensor_copy(gl, rkG.rearrange("p (i n) -> p i n", i=NT)))
                        rank(rkG.rearrange("p (i n) -> p i n", i=NT), gl, NT, 4)
                        link(nv.tensor_scalar(rkG, rkG, 0.5, None, ALU.is_lt))
                        link(nv.tensor_scalar(rkE, rkE, topk - 0.5, None, ALU.is_lt))
                        link(nv.tensor_tensor(sel[:].rearrange("p i (g n) -> p (i g) n", n=8), rkE.rearrange("p (g n) -> p g n", n=8),
                                              bc(rkG.rearrange("p (g n) -> p g n", n=1), [128, 8, 8]), ALU.mult))
                    else:
                        for i in range(NT):
                            rank(rkE[:, 32 * i:32 * i + 32].rearrange("p (g i) -> p g i", g=1), lv[:, i:i + 1], 1, 32)
                        link(nv.tensor_scalar(sel[:].rearrange("p i n -> p (i n)"), rkE, topk - 0.5, None, ALU.is_lt))
                    nv.nop().then_inc(q_sel, 1)
                    v.wait_ge(q_exd, 1)
                    link(nv.tensor_tensor(comb[:], sel[:], exE.rearrange("p (i n) -> p i n", i=NT), ALU.mult))
                    link(nv.tensor_reduce(rs[:, 0:2], comb[:], AX.X, ALU.add))
                    if first:
                        link(nv.tensor_reduce(rs[:, 2:4], exG.rearrange("p (i n) -> p i n", i=NT), AX.X, ALU.add))
                        link(nv.tensor_tensor(rs[:, 0:2], rs[:, 0:2], rs[:, 2:4], ALU.mult))
                    link(nv.reciprocal(rs[:, 4:6], rs[:, 0:2]))
                    nv.tensor_tensor(comb[:], comb[:], bc(rs[:, 4:6].rearrange("p (i n) -> p i n", n=1), [128, NT, 32]),
                                     ALU.mult).then_inc(q_sel, 1)
                    link(nv.memset(posx[:], -1.0))
                    v.wait_ge(q_pos, 1)
                    po = posx[:, :, 0:32]
                    link(nv.tensor_scalar(po, ps[:, 5, 0:64].rearrange("p (i n) -> p i n", i=NT), 1.0, None, ALU.add))
                    link(nv.tensor_tensor(po, po, sel[:], ALU.mult))
                    link(nv.tensor_scalar(po, po, -1.0, None, ALU.add))
                    link(nv.tensor_reduce(rs[:, 6:7], ps[:, 5, 64:96], AX.X, ALU.max))
                    nv.tensor_copy(cnt[:], rs[:, 6:7]).then_inc(q_cnt, 1)
                    if not first:
                        v.wait_ge(q_b2, 1)
                        for i in range(NT):
                            nv.tensor_copy(acc[:, i, :], ps[:, 2 * i:2 * i + 2, :].rearrange("p b c -> p (b c)")).then_inc(q_acc, 1)

                @block.tensor
                def _(pe):
                    nt = nc.tensor
                    norm.pe(pe)
                    pe.wait_ge(norm.ev, 4)
                    pe.wait_ge(q_in, 64)
                    for i in range(NT):
                        for t in range(KC):
                            nt.matmul(ps[:, 4, 64 * i:64 * i + nr], hT[:, t, i * 128:i * 128 + 128], wr[:, t, :], start=t == 0, stop=False)
                        ins = nt.matmul(ps[:, 4, 64 * i:64 * i + nr], K("ones", 1), brow[:], start=False, stop=True)
                    ins.then_inc(q_lg, 1)
                    pe.wait_ge(q_sel, 1)
                    nt.matmul(ps[:, 5, 0:32], K("before"), sel[:, 0, :], start=True, stop=True)
                    nt.matmul(ps[:, 5, 32:64], K("before"), sel[:, 1, :], start=True, stop=False)
                    nt.matmul(ps[:, 5, 32:64], K("ones"), sel[:, 0, :], start=False, stop=True)
                    nt.matmul(ps[:, 5, 64:96], K("ones"), sel[:, 0, :], start=True, stop=False)
                    nt.matmul(ps[:, 5, 64:96], K("ones"), sel[:, 1, :], start=False, stop=True).then_inc(q_pos, 1)
                    if not first:
                        pe.wait_ge(q_sel, 2)
                        for i in range(NT):
                            ins = nt.transpose(ps[0:32, 6, i * 128:i * 128 + 128], comb[:, i, :], ident)
                        ins.then_inc(q_bT, 1)
                        pe.wait_ge(q_bTk, 1)
                        for i in range(NT):
                            for h in range(2):
                                ins = nt.matmul(ps[:, 2 * i + h, :], cT[:, i * 128:i * 128 + 128], b2s[:, 512 * h:512 * h + 512],
                                                start=True, stop=True)
                        ins.then_inc(q_b2, 1)

            Pm = sbuf(m, tag + "Pm", [128, NT, 128])
            Pg = sbuf(m, tag + "Pg", [128, NT, 128])
            xgT = hTf[:, 0:1024].rearrange("p (t c) -> p t c", t=KC)
            GT = sbuf(m, tag + "GT", [128, NT, 128])
            sg = sbuf(m, tag + "sg", [128, 512 * BU // 2])
            hid = sbuf(m, tag + "hid", [128, FT, 128])
            hidT = sbuf(m, tag + "hidT", [128, FT, 128])
            y = hTf[:, 1024:2048]
            if not first:
                gm = sbuf(m, "gm", [128, 1024])
                um = junk
                pick = sbuf(m, "pick", [32, 128])

            def rounds(pre, used, ready_value, ready, used_base):
                def z(n):
                    return S(tag + pre + n)
                p_ready, pg_ready, pick_ready, gathered, xg_kept, gatesT, gt_kept = (
                    z("onehot_ready"), z("weighted_ready"), z("pick_ready"), z("gathered"), z("gathered_kept"), z("weightsT"), z("weightsT_kept"))
                act1, clip, hid_ready, hid_tr, hid_kept, y_act, y_dve, scat, acc_a, acc_c = (
                    z("activated"), z("clipped"), z("hidden_ready"), z("hiddenT"), z("hiddenT_kept"), z("y_low_kept"), z("y_high_kept"),
                    z("scattered"), z("added_tile0"), z("added_tile1"))

                def onehot(v, dst, p2):
                    for i in range(NT):
                        ins = nc.vector.tensor_tensor(dst[:, i, :].rearrange("p (e c) -> p e c", e=2),
                                                      K("iota").rearrange("p (e c) -> p e c", e=2),
                                                      bc(posx[:, i, p2].rearrange("p (e c) -> p e c", c=1), [128, 2, 64]), ALU.is_equal)
                    return ins

                def gather(pe):
                    for t in range(KC):
                        for i in range(NT):
                            ins = nc.tensor.matmul(ps[:, A0 + t // 4, (t % 4) * 128:(t % 4) * 128 + 128], hn[:, i, t, :], Pm[:, i, :],
                                                   start=i == 0, stop=i == NT - 1)
                    ins.then_inc(gathered, 1)

                def gather_kept(a):
                    for b in range(2):
                        ins = nc.scalar.activation(xgT[:, 4 * b:4 * b + 4, :].rearrange("p t c -> p (t c)"), ps[:, A0 + b, :], ACT.Copy)
                    ins.then_inc(xg_kept, 1)

                def up_used(it, n):
                    return it * per_pair + (used_base + n)

                def pe_credit(pe):
                    pe.sem_inc(gatesT, 1)

                def pe_start(pe, it, g):
                    pe.wait_ge(p_ready, g + 1)
                    if pre:
                        pe.wait_ge(acc_a, it + 1)
                        pe.wait_ge(gatesT, it + 1)
                    gather(pe)

                def pe_pair(pe, it, g):
                    nt = nc.tensor
                    pe.wait_ge(xg_kept, g + 1)
                    pe.wait_ge(hid_ready, it + 1)
                    if not first:
                        pe.wait_ge(pick_ready, g + 1)
                        for b in range(4):
                            nt.matmul(ps[:, b, :], pick[:], b1s[:, 512 * b:512 * b + 512], start=True, stop=False, skip_group_check=True)

                    def arrived(j):
                        pe.wait_ge(ready[(base + j) % RING], ready_value(it, j))
                    for u in range(UP // 2):
                        arrived(2 * u)
                        arrived(2 * u + 1)
                        for t in range(KC if first else 2):
                            for b in range(1 if first else 4):
                                for e in range(2):
                                    w = ring[:, (base + 2 * u + e) % RING, :]
                                    if first:
                                        ins = nt.matmul(ps[64 * e:64 * e + 64, u, :], xgT[:, t, 64 * e:64 * e + 64], w[:, 512 * t:512 * t + 512],
                                                        start=t == 0, stop=t == KC - 1, skip_group_check=True)
                                    else:
                                        c = 2048 * t + 512 * b
                                        ins = nt.matmul(ps[64 * e:64 * e + 64, b, :], xgT[:, 2 * u + t, 64 * e:64 * e + 64], w[:, c:c + 512],
                                                        start=False, stop=u == 3 and t == 1, skip_group_check=True)
                        ins.then_inc(used, 2)
                    pe.wait_ge(p_ready, g + 2)
                    pe.wait_ge(acc_a, it + 1)
                    gather(pe)
                    pe.wait_ge(xg_kept, g + 2)
                    pe.wait_ge(pg_ready, it + 1)
                    for i in range(NT):
                        ins = nt.transpose(ps[:, A0, i * 128:i * 128 + 128], Pg[:, i, :], ident)
                    ins.then_inc(gatesT, 1)
                    pe.wait_ge(hid_ready, it + 2)
                    pe.wait_ge(acc_c, it + 1)
                    for t in range(FT):
                        ins = nt.transpose(ps[:, C0 + t // 4, (t % 4) * 128:(t % 4) * 128 + 128], hid[:, t, :], ident)
                    ins.then_inc(hid_tr, 1)
                    pe.wait_ge(hid_kept, it + 1)
                    for u in range((per_pair - UP) // 2):
                        j = UP + 2 * u
                        arrived(j)
                        arrived(j + 1)
                        for t in range(4):
                            for h in range(2):
                                for e in range(2):
                                    w = ring[:, (base + j + e) % RING, :]
                                    c = 1024 * t + 512 * h
                                    ins = nt.matmul(ps[64 * e:64 * e + 64, C0 + h, :], hidT[:, 4 * u + t, 64 * e:64 * e + 64], w[:, c:c + 512],
                                                    start=u == 0 and t == 0, stop=4 * u + t == FT - 1, skip_group_check=True)
                        ins.then_inc(used, 2)
                    pe.wait_ge(y_act, it + 1)
                    pe.wait_ge(y_dve, it + 1)
                    pe.wait_ge(gt_kept, it + 1)
                    for i in range(NT):
                        for h in range(2):
                            ins = nt.matmul(ps[:, (A0, C0)[i] + h, :], GT[:, i, :], y[:, 512 * h:512 * h + 512], start=True, stop=True)
                        ins.then_inc(scat, 1)

                def act_start(a, it, g):
                    a.wait_ge(gathered, g + 1)
                    gather_kept(a)

                def act_pair(a, it, g):
                    na = nc.scalar
                    if first:
                        a.wait_ge(used, up_used(it, 2))
                        na.activation(sg[:], ps[:, 0, :], ACT.Silu).then_inc(act1, 1)
                    else:
                        a.wait_ge(clip, it + 1)
                        na.activation(sg[:], gm[:], ACT.Sigmoid, scale=1.702).then_inc(act1, 1)
                    a.wait_ge(gathered, g + 2)
                    gather_kept(a)
                    a.wait_ge(hid_tr, it + 1)
                    for b in range(FT // 4):
                        ins = na.activation(hidT[:, 4 * b:4 * b + 4, :].rearrange("p t c -> p (t c)"), ps[:, C0 + b, :], ACT.Copy)
                    ins.then_inc(hid_kept, 1)
                    a.wait_ge(used, up_used(it, per_pair))
                    na.activation(y[:, 0:512], ps[:, C0, :], ACT.Copy).then_inc(y_act, 1)

                def dve_credit(v):
                    v.sem_inc(hid_ready, 1)
                    v.sem_inc(acc_a, 1)
                    v.sem_inc(acc_c, 1)

                def dve_pick(v, p2):
                    if not first:
                        nc.vector.tensor_copy(pick[:].rearrange("p (e c) -> p e c", e=2),
                                              bc(K("ident", 32)[:, p2].rearrange("p (e c) -> p e c", c=1), [32, 2, 64])).then_inc(pick_ready, 1)

                def dve_start(v, it, g):
                    if pre:
                        v.wait_ge(acc_c, it + 1)
                    onehot(v, Pm, slice(0, 2)).then_inc(p_ready, 1)
                    dve_pick(v, slice(0, 2))

                def dve_pair(v, link, it, g, p):
                    nv = nc.vector
                    e_now = v.snap(2 * p)
                    e_next = v.snap(2 * p + 2)
                    v.wait_ge(gathered, g + 1)
                    onehot(v, Pm, bass.ds(e_next, 2)).then_inc(p_ready, 1)
                    v.wait_ge(gatesT, it + 1)
                    onehot(v, Pg, bass.ds(e_now, 2)).then_inc(s("eq"), 1)
                    v.wait_ge(s("eq"), 1)
                    v.sem_clear(s("eq"))
                    for i in range(NT):
                        pv = Pg[:, i, :].rearrange("p (e c) -> p e c", e=2)
                        ins = nv.tensor_tensor(pv, pv, bc(comb[:, i, bass.ds(e_now, 2)].rearrange("p (e c) -> p e c", c=1), [128, 2, 64]), ALU.mult)
                    ins.then_inc(pg_ready, 1)
                    hv = hid[:].rearrange("q t p -> q p t")
                    if first:
                        v.wait_ge(act1, it + 1)
                        v.wait_ge(used, up_used(it, 4))
                        nv.tensor_tensor(hv, sg[:].rearrange("q (p t) -> q p t", t=FT), ps[:, 1, :].rearrange("q (p t) -> q p t", t=FT),
                                         ALU.mult).then_inc(hid_ready, 1)
                    else:
                        v.wait_ge(used, up_used(it, 8))
                        nv.tensor_scalar(gm[:], ps[:, 0:2, :].rearrange("p b c -> p (b c)"), 7.0, None, ALU.min).then_inc(clip, 1)
                        dve_pick(v, bass.ds(e_next, 2))
                        nv.tensor_scalar(um[:], ps[:, 2:4, :].rearrange("p b c -> p (b c)"), 7.0, -7.0, ALU.min, ALU.max)
                        v.wait_ge(act1, it + 1)
                        nv.tensor_tensor(gm[:], gm[:], sg[:], ALU.mult).then_inc(s("glu"), 1)
                        v.wait_ge(s("glu"), 1)
                        v.sem_clear(s("glu"))
                        nv.scalar_tensor_tensor(out=hv, in0=um[:].rearrange("q (p t) -> q p t", t=FT), scalar=1.0,
                                                in1=gm[:].rearrange("q (p t) -> q p t", t=FT), op0=ALU.add, op1=ALU.mult).then_inc(hid_ready, 1)
                    v.wait_ge(gatesT, it + 2)
                    nv.tensor_copy(GT[:].rearrange("p i c -> p (i c)"), ps[:, A0, 0:256]).then_inc(gt_kept, 1)
                    v.wait_ge(used, up_used(it, per_pair))
                    nv.tensor_copy(y[:, 512:1024], ps[:, C0 + 1, :]).then_inc(y_dve, 1)
                    for i, (b, sm_) in enumerate(((A0, acc_a), (C0, acc_c))):
                        v.wait_ge(scat, it * 2 + (i + 1))
                        nv.tensor_tensor(acc[:, i, :], acc[:, i, :], ps[:, b:b + 2, :].rearrange("p b c -> p (b c)"), ALU.add).then_inc(sm_, 1)

                return pe_credit, pe_start, pe_pair, act_start, act_pair, dve_credit, dve_start, dve_pair

            n6 = per_pair // RING
            main = rounds("", units_used, lambda it, j: it * (16 * n6) + 16 * ((base + j) // RING + 1), ring_ready, base)
            o_used = s("more_used")
            o_ready = [s(f"more_ready{j}") for j in range(RING)]
            more = rounds("more_", o_used, lambda it, j: it * (16 * n6) + 16 * (j // RING + 1), o_ready, RING)
            full_used = base + per_pair * PAIRS

            def pairs(eng, body):
                with eng.Fori(0, PAIRS) as p:
                    body(p)

            def more_rounds(eng, credit, start, body, flag_wait=True):
                most = eng.value_load(cnt[0:1, 0:1], min_val=0, max_val=T)
                with eng.If(most > CAP):
                    credit()
                    with eng.Fori(0, ROUNDS - 1) as r:
                        start(r)
                        if body is not None:
                            with eng.Fori(0, PAIRS) as p:
                                body(eng.snap(r * PAIRS + p), eng.snap(r * (PAIRS + 1) + p), p)

            with nc.Block() as block:
                @block.sync
                def _(sp):
                    def load(sem_ready, sem_used, k_used, e0, j):
                        e0 = sp.snap(e0)
                        sp.wait_ge(sem_used, k_used)
                        sp.dma_start(ring[:, (base + j) % RING, :], w_src(e0, j)).then_inc(sem_ready[(base + j) % RING], 16)
                    with sp.Fori(0, PAIRS - 1) as p:
                        for j in range(RING, per_pair):
                            load(ring_ready, units_used, sp.snap(p * per_pair + (base + j - RING + 1)), 2 * p, j)
                        for j in range(RING):
                            load(ring_ready, units_used, sp.snap(p * per_pair + (base + per_pair + j - RING + 1)), 2 * p + 2, j)
                    for j in range(RING, per_pair):
                        k = base + (PAIRS - 1) * per_pair + j
                        sp.wait_ge(units_used, k - RING + 1)
                        sp.dma_start(ring[:, k % RING, :], w_src(2 * PAIRS - 2, j)).then_inc(ring_ready[k % RING], 16)
                    sp.wait_ge(units_used, full_used)
                    most = sp.value_load(cnt[0:1, 0:1], min_val=0, max_val=T)
                    with sp.If(most > CAP):
                        with sp.Fori(0, ROUNDS - 1) as r:
                            with sp.Fori(0, PAIRS) as p:
                                for j in range(per_pair):
                                    load(o_ready, o_used, sp.snap(r * (PAIRS * per_pair) + p * per_pair + (j + 1)), 2 * p, j)
                        for j in range(RING):
                            sp.wait_ge(o_used, RING + (ROUNDS - 1) * PAIRS * per_pair)
                    after(sp)

                @block.tensor
                def _(pe):
                    credit, start, pair = main[0:3]
                    credit(pe)
                    start(pe, 0, 0)
                    pairs(pe, lambda p: pair(pe, p, p))
                    credit_, start_, pair_ = more[0:3]

                    def credit_more():
                        pe.wait_ge(units_used, full_used)
                        credit_(pe)
                        pe.sem_inc(o_used, RING)
                    more_rounds(pe, credit_more, lambda r: start_(pe, pe.snap(r * PAIRS), pe.snap(r * (PAIRS + 1))),
                                lambda it, g, p: pair_(pe, it, g))

                @block.scalar
                def _(a):
                    main[3](a, 0, 0)
                    pairs(a, lambda p: main[4](a, p, p))
                    more_rounds(a, lambda: None, lambda r: more[3](a, r * PAIRS, a.snap(r * (PAIRS + 1))),
                                lambda it, g, p: more[4](a, it, g))

                @block.vector
                def _(v):
                    link = None
                    main[5](v)
                    main[6](v, 0, 0)
                    pairs(v, lambda p: main[7](v, link, p, p, p))
                    lv = chain(v, "v_chain")

                    def next_round(r):
                        v.wait_ge(S(tag + "more_added_tile1"), v.snap(r * PAIRS + 1))
                        nc.vector.tensor_scalar(posx[:], posx[:], -float(CAP), None, ALU.add).then_inc(S(tag + "round_set"), 1)
                        v.wait_ge(S(tag + "round_set"), r + 1)
                        more[6](v, v.snap(r * PAIRS), v.snap(r * (PAIRS + 1)))
                    more_rounds(v, lambda: more[5](v), next_round, lambda it, g, p: more[7](v, link, it, g, p))
            return m, acc

        n1 = Norm("n1")
        n1.gains = 2

        def after1(sp):
            for k in range(K_ADA, K_ADA + RING):
                load_unit(sp, k)
        m, _ = mixture("m1_", K_MOE1, 6, moe1_src, "w_rtr", "b_rtr", 2, True, n1, after1, True)
        m.close()
        retire_semaphores()
        p2 = ExitStack()
        mod = sbuf(p2, "mod", [128, 6 * D])
        p2b = ExitStack()
        SV = sbuf(p2b, "SV", [57, 128])
        ldr = sbuf(p2b, "ldr", [48, 2])
        VT = sbuf(p2b, "VT", [128, 57])
        lqk = sbuf(p2b, "lqk", [128, 4, 64])
        Bn = sbuf(p2b, "Bn", [128, 2, 16, 16])
        Cn = sbuf(p2b, "Cn", [128, 2, 4, 64])
        cv = sbuf(p2b, "cv", [128, KC])
        cwide = hnf[:, 0:1024].rearrange("p (t c) -> p t c", t=KC)
        f_in, f_c, f_cw, f_ada, f_adak, f_sv, f_ld = (S("mod_in"), S("cond_activated"), S("cond_wide"), S("mod_done"), S("mod_kept"),
                                                S("short_in"), S("dt_spread"))
        nf = Norm("nf")
        nA = Norm("nA", shift=mod[:, 0:D])
        nA.gains = 4
        x3_done, gain_ready = S("x3"), S("gain_ready")
        with nc.Block() as block:
            @block.sync
            def _(sp):
                for k in range(K_ADA + RING, K_IN2 + RING):
                    load_unit(sp, k)

            @block.scalar
            def _(a):
                a.dma_start(grow[:], A["final_norm"].rearrange("(a d) -> a d", a=1).to_broadcast([128, D])).then_inc(s_grow, 16)
                a.dma_start(cv[:], A["c_2"][0].rearrange("(p t) -> p t", t=KC)).then_inc(f_in, 16)
                a.dma_start(mod[:], A["b_ada_2"].to_broadcast([128, 6 * D])).then_inc(f_in, 16)
                for r0, n, ap in ((0, 16, A["ssm_a_re_2"][0].rearrange("(j g) p -> j (g p)", j=16)),
                                  (16, 16, A["ssm_a_im_2"][0].rearrange("(j g) p -> j (g p)", j=16)),
                                  (48, 4, A["ssm_d_2"][0].rearrange("(j c) -> j c", j=4)),
                                  (52, 4, A["b_glu_2"][0].rearrange("(j c) -> j c", j=4)),
                                  (56, 1, A["subln_g_2"])):
                    a.dma_start(SV[r0:r0 + n, :], ap).then_inc(f_sv, 16)
                a.dma_start(ldr[32:48, :], A["ssm_log_dt_2"][0].rearrange("(j g) -> j g", j=16)).then_inc(f_sv, 16)
                for i, n in enumerate(("lq1_2", "lk1_2", "lq2_2", "lk2_2")):
                    a.dma_start(lqk[:, i, :], A[n].to_broadcast([128, 64])).then_inc(f_sv, 16)
                for i, n in enumerate(("ssm_b_re_2", "ssm_b_im_2")):
                    a.dma_start(Bn[:, i], A[n][0].rearrange("(j g) p c -> (g p) j c", j=16)).then_inc(f_sv, 16)
                for i, n in enumerate(("ssm_c_re_2", "ssm_c_im_2")):
                    a.dma_start(Cn[:, i], A[n][0].rearrange("(j g) c p -> (g c) j p", j=4)).then_inc(f_sv, 16)
                a.wait_ge(f_in, 32)
                nc.scalar.activation(cv[:], cv[:], ACT.Silu).then_inc(f_c, 1)
                nf.act_root(a)
                a.wait_ge(x3_done, 2)
                a.dma_start(grow[:], A["norm1_g_2"].to_broadcast([128, D])).then_inc(s_grow, 16)

            @block.vector
            def _(v):
                link = chain(v, "v_chain")
                nv = nc.vector
                v.wait_ge(f_c, 1)
                nv.tensor_copy(cwide, bc(cv[:].rearrange("p (t c) -> p t c", c=1), [128, KC, 128])).then_inc(f_cw, 1)
                v.wait_ge(s_grow, 48)
                nf.dve_stats(v, link)
                for i in range(NT):
                    nv.scalar_tensor_tensor(out=X[:, i, :], in0=X[:, i, :], scalar=st[:, 4 + i:5 + i], in1=grow[:],
                                            op0=ALU.mult, op1=ALU.mult).then_inc(x3_done, 1)
                v.wait_ge(f_sv, 16 * 14)
                nv.tensor_copy(SV[32:48, :].rearrange("j (g p) -> j g p", g=2),
                               bc(ldr[32:48, :].rearrange("j (g p) -> j g p", p=1), [16, 2, 64])).then_inc(f_ld, 1)
                for j in range(12):
                    v.wait_ge(f_ada, j + 1)
                    c = slice(512 * j, 512 * j + 512)
                    nv.tensor_tensor(mod[:, c], mod[:, c], ps[:, 4 + j % 4, :], ALU.add).then_inc(f_adak, 1)
                v.wait_ge(f_adak, 12)
                v.wait_ge(s_grow, 64)
                nv.scalar_tensor_tensor(out=grow[:], in0=mod[:, D:2 * D], scalar=1.0, in1=grow[:], op0=ALU.add,
                                        op1=ALU.mult).then_inc(gain_ready, 1)

            @block.tensor
            def _(pe):
                nt = nc.tensor
                pe.wait_ge(f_cw, 1)
                for j in range(12):
                    unit_arrived(pe, K_ADA + j)
                    if j >= 4:
                        pe.wait_ge(f_adak, j - 3)
                    w = unit(K_ADA + j)
                    for t in range(KC):
                        ins = nt.matmul(ps[:, 4 + j % 4, :], cwide[:, t, :], w[:, t, :], start=t == 0, stop=t == KC - 1)
                    ins.then_inc(f_ada, 1)
                    pe.wait_ge(f_ada, j + 1)
                    pe.sem_inc(units_used, 1)


        q2T = sbuf(p2b, "q2T", [128, 4, T])
        k2T = sbuf(p2b, "k2T", [128, 4, T])
        v2 = sbuf(p2b, "v2", [128, NT, 512])
        uT = sbuf(p2b, "uT", [128, 4, T])
        aT = sbuf(p2b, "aT", [128, 4, T])
        zc = sbuf(p2b, "zc", [128, 12, 16])
        lam = sbuf(p2b, "lam", [128, 8])
        BT = sbuf(p2b, "BT", [128, 2, 4, 128])
        CT = sbuf(p2b, "CT", [128, 2, 4, 128])
        Bp = junk[:].rearrange("p (k j g c) -> p k j g c", k=2, j=16, g=2)
        s2_proj, s2_pev, s2_vt, s2_vtk, s2_e, s2_ek, s2_b, s2_bt, s2_btk, s2_l, s2_lk = (
            S("proj2_done"), S("proj2_kept"), S("shortT"), S("shortT_kept"), S("lam_ready"), S("lam_acted"),
            S("bc_built"), S("bcT"), S("bcT_kept"), S("lam_dots"), S("lam_exps"))
        zr_, zi_, dec, sn, cs_, re, im, cr, ci, t1_, t2_, dt_ = (zc[:, i, :] for i in range(12))
        TWO_PI = 2 * np.pi
        with nc.Block() as block:
            @block.sync
            def _(sp):
                for k in range(K_IN2 + RING, K_IN2 + 4 + RING):
                    load_unit(sp, k)

            @block.scalar
            def _(a):
                na = nc.scalar
                nA.act(a)
                a.wait_ge(s2_vt, 1)
                na.activation(VT[:], ps[:, 4, 0:57], ACT.Copy).then_inc(s2_vtk, 1)
                a.wait_ge(s2_vtk, 1)
                na.activation(dt_, VT[:, 32:48], ACT.Exp).then_inc(s2_vtk, 1)
                a.wait_ge(s2_e, 1)
                na.activation(dec, zr_, ACT.Exp).then_inc(s2_ek, 1)
                a.wait_ge(s2_l, 1)
                na.activation(lam[:, 2:4], lam[:, 0:2], ACT.Exp).then_inc(s2_lk, 1)
                a.wait_ge(s2_e, 2)
                na.activation(sn, t1_, ACT.Sin).then_inc(s2_ek, 1)
                na.activation(cs_, t2_, ACT.Sin).then_inc(s2_ek, 1)
                for u in range(4):
                    for h in range(2):
                        n = 2 * u + h
                        a.wait_ge(s2_proj, n + 1)
                        src = ps[:, 4 + n % 4, :]
                        if u == 2:
                            ins = na.activation(v2[:, h, :], src, ACT.Copy)
                        else:
                            dst = {0: q2T, 1: k2T, 3: uT}[u]
                            ins = na.activation(dst[:, 2 * h:2 * h + 2, :].rearrange("p a b -> p (a b)"), src, ACT.Copy)
                        ins.then_inc(s2_pev, 1)
                a.wait_ge(s2_bt, 1)
                for k in range(2):
                    na.activation(BT[:, k].rearrange("p j c -> p (j c)"), ps[:, k, :], ACT.Copy).then_inc(s2_btk, 1)
                    na.activation(CT[:, k].rearrange("p j c -> p (j c)"), ps[:, 2 + k, :], ACT.Copy,
                                  scale=(1.0, -1.0)[k]).then_inc(s2_btk, 1)

            @block.vector
            def _(v):
                link = chain(v, "v_chain")
                nv = nc.vector
                nA.dve(v, link)
                v.wait_ge(s2_vtk, 2)
                link(nv.tensor_scalar(re, VT[:, 0:16], -1e-4, None, ALU.min))
                link(nv.tensor_copy(im, VT[:, 16:32]))
                link(nv.tensor_tensor(zi_, im, dt_, ALU.mult))
                nv.tensor_tensor(zr_, re, dt_, ALU.mult).then_inc(s2_e, 1)
                link(nv.tensor_scalar(t1_, zi_, 1.0 / TWO_PI, 12582912.0, ALU.mult, ALU.add))
                link(nv.tensor_scalar(t1_, t1_, -12582912.0, None, ALU.add))
                for c in (6.28125, 0.0019350051879882812, TWO_PI - 6.28125 - 0.0019350051879882812):
                    link(nv.scalar_tensor_tensor(out=zi_, in0=t1_, scalar=-c, in1=zi_, op0=ALU.mult, op1=ALU.add))
                link(nv.tensor_scalar(t1_, zi_, 3.1415925, -3.1415925, ALU.min, ALU.max))
                link(nv.tensor_scalar(t2_, t1_, -1.0, None, ALU.mult))
                link(nv.tensor_tensor(t2_, t2_, t1_, ALU.max))
                nv.tensor_scalar(t2_, t2_, -1.0, float(np.pi / 2), ALU.mult, ALU.add).then_inc(s2_e, 1)
                prod = junk[:, 0:128]
                for i in range(2):
                    ins = nv.tensor_tensor_reduce(out=prod[:, 64 * i:64 * i + 64], in0=lqk[:, 2 * i, :], in1=lqk[:, 2 * i + 1, :],
                                                  scale=1.0, scalar=0.0, op0=ALU.mult, op1=ALU.add, accum_out=lam[:, i:i + 1])
                ins.then_inc(s2_l, 1)
                v.wait_ge(s2_lk, 1)
                link(nv.tensor_tensor(lam[:, 4:5], lam[:, 3:4], lam[:, 2:3], ALU.subtract))
                link(nv.tensor_scalar(lam[:, 4:5], lam[:, 4:5], -0.2, None, ALU.add))
                link(nv.tensor_scalar(lam[:, 5:6], VT[:, 56:57], 0.8, None, ALU.mult))
                v.wait_ge(s2_ek, 3)
                link(nv.tensor_tensor(cr, dec, cs_, ALU.mult))
                link(nv.tensor_scalar(cr, cr, -1.0, None, ALU.add))
                link(nv.tensor_tensor(ci, dec, sn, ALU.mult))
                link(nv.tensor_tensor(t1_, re, re, ALU.mult))
                link(nv.tensor_tensor(t2_, im, im, ALU.mult))
                link(nv.tensor_tensor(t1_, t1_, t2_, ALU.add))
                link(nv.reciprocal(dt_, t1_))
                link(nv.tensor_tensor(t1_, cr, re, ALU.mult))
                link(nv.tensor_tensor(t2_, ci, im, ALU.mult))
                link(nv.tensor_tensor(zr_, t1_, t2_, ALU.add))
                link(nv.tensor_tensor(t1_, ci, re, ALU.mult))
                link(nv.tensor_tensor(t2_, cr, im, ALU.mult))
                link(nv.tensor_tensor(zi_, t1_, t2_, ALU.subtract))
                link(nv.tensor_tensor(zr_, zr_, dt_, ALU.mult))
                link(nv.tensor_tensor(zi_, zi_, dt_, ALU.mult))
                zrb = bc(zr_.rearrange("p (j c) -> p j c", c=1), [128, 16, 16])
                zib = bc(zi_.rearrange("p (j c) -> p j c", c=1), [128, 16, 16])
                tmp = hnf[:, 0:512].rearrange("p (k j c) -> p k j c", k=2, j=16)
                for k, (x, y_, op) in enumerate(((0, 1, ALU.subtract), (1, 0, ALU.add))):
                    nv.tensor_tensor(tmp[:, 0], Bn[:, x], zrb, ALU.mult)
                    link(nv.tensor_tensor(tmp[:, 1], Bn[:, y_], zib, ALU.mult))
                    link(nv.tensor_tensor(tmp[:, 0], tmp[:, 0], tmp[:, 1], op))
                    nv.tensor_scalar(Bp[:, k, :, 0, :], tmp[:, 0], K("even"), None, ALU.mult)
                    link(nv.tensor_scalar(Bp[:, k, :, 1, :], tmp[:, 0], K("odd"), None, ALU.mult))
                Cp = hnf[:, 1024:2048].rearrange("p (k j r) -> p k j r", k=2, j=4)
                for k in range(2):
                    nv.tensor_scalar(Cp[:, k, :, 0:64], Cn[:, k], K("geven"), None, ALU.mult)
                    ins = nv.tensor_scalar(Cp[:, k, :, 64:128], Cn[:, k], K("godd"), None, ALU.mult)
                ins.then_inc(s2_b, 1)

            @block.tensor
            def _(pe):
                nt = nc.tensor
                nt.transpose(ps[:, 4, 0:57], SV[:], K("ident", 57)[:, 0:57]).then_inc(s2_vt, 1)
                nA.pe(pe)
                pe.wait_ge(nA.ev, 4)
                pe.wait_ge(s2_vtk, 1)
                for u in range(4):
                    unit_arrived(pe, K_IN2 + u)
                    w = unit(K_IN2 + u)
                    for h in range(2):
                        n = 2 * u + h
                        if n >= 4:
                            pe.wait_ge(s2_pev, n - 3)
                        if u == 2:
                            for t in range(KC):
                                ins = nt.matmul(ps[:, 4 + n % 4, :], hT[:, t, h * 128:h * 128 + 128], w[:, t, :], start=t == 0, stop=t == KC - 1)
                        else:
                            for cb in range(2):
                                c = (2 * h + cb) * 128
                                for t in range(KC):
                                    ins = nt.matmul(ps[:, 4 + n % 4, cb * 256:cb * 256 + 256], w[:, t, c:c + 128], hT[:, t, :],
                                                    start=t == 0, stop=t == KC - 1)
                        ins.then_inc(s2_proj, 1)
                    pe.wait_ge(s2_proj, 2 * u + 2)
                    pe.sem_inc(units_used, 1)
                pe.wait_ge(s2_b, 1)
                Cp = hnf[:, 1024:2048].rearrange("p (k j r) -> p k j r", k=2, j=4)
                for k in range(2):
                    for q in range(4):
                        nt.transpose(ps[:, k, q * 128:q * 128 + 128], Bp[:, k, 4 * q:4 * q + 4].rearrange("p j g c -> p (j g c)"), ident)
                        ins = nt.transpose(ps[:, 2 + k, q * 128:q * 128 + 128], Cp[:, k, q, :], ident)
                ins.then_inc(s2_bt, 1)

        P2 = hnf.rearrange("p (s k) -> p s k", s=8)
        PT2 = hTf.rearrange("p (b h q) -> p b h q", b=2, h=8)
        w2s = sbuf(p2b, "w2s", [128, 48])
        osq2 = junk[:].rearrange("p (i c) -> p i c", i=NT)
        d_s, d_mx, d_exp, d_p, d_t, d_tk, d_o, d_sq, d_v, d_r, d_n, d_nt, d_ntk = (
            S(n) for n in ("a2_scores", "a2_max", "a2_exp", "a2_probs", "a2_probsT", "a2_probsT_kept", "a2_out", "a2_squares",
                           "a2_variance", "a2_root", "a2_normed", "a2_outT", "a2_outT_kept"))
        with nc.Block() as block:
            @block.vector
            def _(v):
                link = chain(v, "v_chain")
                nv = nc.vector
                for i in range(NT):
                    nk = 128 * (i + 1)
                    P8 = P2[:, :, 0:nk]
                    v.wait_ge(d_s, i + 1)
                    if i:
                        v.wait_ge(d_t, i)
                    src = ps[:, 2:6, :].rearrange("p b (a k) -> p (b a) k", a=2)
                    ca = K("causal").rearrange("p (a k) -> p a k", a=1)
                    link(nv.tensor_tensor(P8[:, :, nk - 128:nk], src[:, :, nk - 128:nk], bc(ca, [128, 8, 128]), ALU.add))
                    if i:
                        link(nv.tensor_copy(P8[:, :, 0:128], src[:, :, 0:128]))
                    link(nv.tensor_reduce(w2s[:, 0:8], P8, AX.X, ALU.max))
                    nv.tensor_scalar(w2s[:, 8:16], w2s[:, 0:8], -0.125, None, ALU.mult).then_inc(d_mx, 1)
                    v.wait_ge(d_exp, i + 1)
                    w8 = w2s[:, 16:24]
                    link(nv.reciprocal(w8, w8))
                    link(nv.tensor_scalar(w2s[:, 20:24], w2s[:, 20:24], lam[:, 4:5], None, ALU.mult))
                    link(nv.tensor_tensor(P8, P8, bc(w8.rearrange("p (h n) -> p h n", n=1), [128, 8, nk]), ALU.mult))
                    nv.tensor_tensor(P2[:, 0:4, 0:nk], P2[:, 0:4, 0:nk], P2[:, 4:8, 0:nk], ALU.add).then_inc(d_p, 1)
                v.wait_ge(d_sq, 2)
                link(nv.tensor_reduce(w2s[:, 24:32], osq2.rearrange("p i (h c) -> p (i h) c", h=4), AX.X, ALU.add))
                nv.tensor_scalar(w2s[:, 32:40], w2s[:, 24:32], 1.0 / 128, EPS, ALU.mult, ALU.add).then_inc(d_v, 1)
                v.wait_ge(d_r, 1)
                link(nv.reciprocal(w2s[:, 40:48], w2s[:, 32:40]))
                for i in range(NT):
                    r = bc(w2s[:, 40 + 4 * i:44 + 4 * i].rearrange("p (h n) -> p h n", n=1), [128, 4, 128])
                    nv.tensor_tensor(osq2[:, i].rearrange("p (h c) -> p h c", h=4), ps[:, 6 + i, :].rearrange("p (h c) -> p h c", h=4),
                                     r, ALU.mult).then_inc(d_n, 1)

            @block.scalar
            def _(a):
                na = nc.scalar
                for i in range(NT):
                    nk = 128 * (i + 1)
                    a.wait_ge(d_mx, i + 1)
                    for h in range(8):
                        ins = na.activation(P2[:, h, 0:nk], P2[:, h, 0:nk], ACT.Exp, bias=w2s[:, 8 + h:9 + h], scale=0.125,
                                            accum_out=w2s[:, 16 + h:17 + h])
                    ins.then_inc(d_exp, 1)
                    a.wait_ge(d_t, i + 1)
                    if i:
                        a.wait_ge(d_o, i)
                    for kb in range(i + 1):
                        na.activation(PT2[:, kb, 0:4], ps[:, 2 + kb, :].rearrange("p (c q) -> p c q", c=4), ACT.Copy).then_inc(d_tk, 1)
                for i in range(NT):
                    a.wait_ge(d_o, i + 1)
                    na.activation(osq2[:, i], ps[:, 6 + i, :], ACT.Square).then_inc(d_sq, 1)
                a.wait_ge(d_v, 1)
                na.activation(w2s[:, 32:40], w2s[:, 32:40], ACT.Sqrt).then_inc(d_r, 1)
                a.wait_ge(d_nt, 1)
                for b in range(2):
                    na.activation(aT[:, 2 * b:2 * b + 2], ps[:, b, :].rearrange("p (a q) -> p a q", a=2), ACT.Copy,
                                  scale=lam[:, 5:6]).then_inc(d_ntk, 1)

            @block.tensor
            def _(pe):
                nt = nc.tensor
                for i in range(NT):
                    if i:
                        pe.wait_ge(d_tk, 1)
                    for h in range(4):
                        for m_ in range(2):
                            r = 64 * m_
                            for kb in range(i + 1):
                                c = (h % 2) * 256 + kb * 128
                                ins = nt.matmul(ps[:, 2 + 2 * m_ + h // 2, c:c + 128], q2T[r:r + 64, h, i * 128:i * 128 + 128],
                                                k2T[r:r + 64, h, kb * 128:kb * 128 + 128], start=True, stop=True)
                    ins.then_inc(d_s, 1)
                    pe.wait_ge(d_p, i + 1)
                    for kb in range(i + 1):
                        for h in range(4):
                            ins = nt.transpose(ps[:, 2 + kb, h * 128:h * 128 + 128], P2[:, h, kb * 128:kb * 128 + 128], ident)
                    ins.then_inc(d_t, 1)
                    pe.wait_ge(d_tk, [1, 3][i])
                    for h in range(4):
                        for kb in range(i + 1):
                            ins = nt.matmul(ps[:, 6 + i, h * 128:h * 128 + 128], PT2[:, kb, h, :], v2[:, kb, h * 128:h * 128 + 128],
                                            start=kb == 0, stop=kb == i)
                    ins.then_inc(d_o, 1)
                pe.wait_ge(d_n, 2)
                for i in range(NT):
                    for h in range(4):
                        ins = nt.transpose(ps[:, h // 2, (h % 2) * 256 + i * 128:(h % 2) * 256 + i * 128 + 128],
                                           osq2[:, i, h * 128:h * 128 + 128], ident)
                ins.then_inc(d_nt, 1)

        Wp = sbuf(p2b, "Wp", [128, 2, 4, T])
        sq_ = sbuf(p2b, "sq_", [128, 3, 16])
        w4 = k2T[:, 0:2, :]
        Z = [hnf[:, 0:1024], hnf[:, 1024:2048]]
        Y1, Y2 = hTf[:, 0:1024], hTf[:, 1024:2048]
        xs = [hTf[:, 0:1024], junk[:]]
        dk = grow[:]
        zT = q2T
        e_h = S("ssm_input_half")
        e_bu, e_x, e_y, e_y1, e_sg, e_z = (S(n) for n in ("ssm_input", "ssm_states", "ssm_out", "ssm_gelu_arg", "ssm_gelu_sig", "ssm_gelu"))
        with nc.Block() as block:
            @block.tensor
            def _(pe):
                nt = nc.tensor
                for q in range(4):
                    if q:
                        pe.wait_ge(e_x, q)
                    for jj in (0, 2, 1, 3):
                        if jj == 1:
                            ins.then_inc(e_h, 1)
                            pe.wait_ge(e_h, q + 1)
                        for k in range(2):
                            r = 32 * jj
                            ins = nt.matmul(ps[:, 2 * k + jj // 2, (jj % 2) * 256:(jj % 2) * 256 + 256], BT[r:r + 32, k, q, :], uT[r:r + 32, q, :],
                                            start=True, stop=True, tile_position=(r, 0))
                    ins.then_inc(e_bu, 1)
                    pe.wait_ge(e_x, q + 1)
                    for jj in range(4):
                        for k in range(2):
                            ins = nt.matmul(ps[32 * jj:32 * jj + 32, 4 + q % 2, 0:256], CT[:, k, q, 32 * jj:32 * jj + 32],
                                            xs[k][:, jj * 256:jj * 256 + 256], start=k == 0, stop=k == 1, tile_position=(0, 32 * jj))
                    ins.then_inc(e_y, 1)

            @block.scalar
            def _(a):
                for q in range(4):
                    a.wait_ge(e_y1, q + 1)
                    nc.scalar.activation(w4[:, 1], w4[:, 1], ACT.Sigmoid, scale=1.5957691216057308).then_inc(e_sg, 1)

            @block.vector
            def _(v):
                link = chain(v, "v_chain")
                nv = nc.vector
                for q in range(4):
                    j4 = slice(4 * q, 4 * q + 4)

                    def col(ap, n):
                        return bc(ap.rearrange("p (j n) -> p j n", n=1), [128, 4, n])
                    link(nv.memset(Wp[:, 0, :, 0:1], 1.0))
                    link(nv.memset(Wp[:, 1, :, 0:1], 0.0))
                    wr_, wi_ = sq_[:, 0, 0:4], sq_[:, 1, 0:4]
                    link(nv.tensor_copy(wr_, cs_[:, j4]))
                    link(nv.tensor_copy(wi_, sn[:, j4]))
                    n = 1
                    while n < T:
                        a_r, a_i = Wp[:, 0, :, 0:n], Wp[:, 1, :, 0:n]
                        o_r, o_i = Wp[:, 0, :, n:2 * n], Wp[:, 1, :, n:2 * n]
                        t_ = [Z[0][:, 0:4 * n].rearrange("p (j t) -> p j t", j=4), Z[1][:, 0:4 * n].rearrange("p (j t) -> p j t", j=4)]
                        nv.tensor_tensor(o_r, a_r, col(wr_, n), ALU.mult)
                        nv.tensor_tensor(t_[0], a_i, col(wi_, n), ALU.mult)
                        nv.tensor_tensor(o_i, a_r, col(wi_, n), ALU.mult)
                        link(nv.tensor_tensor(t_[1], a_i, col(wr_, n), ALU.mult))
                        nv.tensor_tensor(o_r, o_r, t_[0], ALU.subtract)
                        link(nv.tensor_tensor(o_i, o_i, t_[1], ALU.add))
                        n *= 2
                        if n < T:
                            x_, y_, w_ = sq_[:, 2, 0:4], sq_[:, 2, 4:8], sq_[:, 2, 8:12]
                            nv.tensor_tensor(x_, wr_, wr_, ALU.mult)
                            nv.tensor_tensor(y_, wi_, wi_, ALU.mult)
                            link(nv.tensor_tensor(w_, wr_, wi_, ALU.mult))
                            link(nv.tensor_tensor(wr_, x_, y_, ALU.subtract))
                            link(nv.tensor_tensor(wi_, w_, w_, ALU.add))
                    W_r, W_i = Wp[:, 0].rearrange("p j t -> p (j t)"), Wp[:, 1].rearrange("p j t -> p (j t)")
                    link(nv.tensor_copy(dk.rearrange("p (j t) -> p j t", j=4), col(dec[:, j4], 256)))
                    v.wait_ge(e_bu, q + 1)
                    if q:
                        v.wait_ge(e_y, q)
                    b_r = ps[:, 0:2, :].rearrange("p b c -> p (b c)")
                    b_i = ps[:, 2:4, :].rearrange("p b c -> p (b c)")
                    nv.tensor_tensor(Y1, b_r, W_r, ALU.mult)
                    nv.tensor_tensor(Z[0], b_i, W_i, ALU.mult)
                    nv.tensor_tensor(Y2, b_i, W_r, ALU.mult)
                    link(nv.tensor_tensor(Z[1], b_r, W_i, ALU.mult))
                    nv.tensor_tensor(Y1, Y1, Z[0], ALU.add)
                    link(nv.tensor_tensor(Y2, Y2, Z[1], ALU.subtract))
                    for jj in range(4):
                        c = slice(256 * jj, 256 * jj + 256)
                        nv.tensor_tensor_scan(Z[0][:, c], dk[:, c], Y1[:, c], 0.0, ALU.mult, ALU.add)
                        ins = nv.tensor_tensor_scan(Z[1][:, c], dk[:, c], Y2[:, c], 0.0, ALU.mult, ALU.add)
                    link(ins)
                    nv.tensor_tensor(xs[0], Z[0], W_r, ALU.mult)
                    nv.tensor_tensor(Y2, Z[1], W_i, ALU.mult)
                    nv.tensor_tensor(xs[1], Z[0], W_i, ALU.mult)
                    link(nv.tensor_tensor(Z[1], Z[1], W_r, ALU.mult))
                    nv.tensor_tensor(xs[0], xs[0], Y2, ALU.subtract)
                    nv.tensor_tensor(xs[1], xs[1], Z[1], ALU.add).then_inc(e_x, 1)
                    v.wait_ge(e_y, q + 1)
                    yq = w4[:, 0]
                    link(nv.scalar_tensor_tensor(out=yq, in0=uT[:, q, :], scalar=VT[:, 48 + q:49 + q], in1=ps[:, 4 + q % 2, 0:256],
                                                 op0=ALU.mult, op1=ALU.add))
                    link(nv.tensor_tensor(w4[:, 1], yq, yq, ALU.mult))
                    link(nv.tensor_scalar(w4[:, 1], w4[:, 1], 0.044715, 1.0, ALU.mult, ALU.add))
                    nv.tensor_tensor(w4[:, 1], w4[:, 1], yq, ALU.mult).then_inc(e_y1, 1)
                    v.wait_ge(e_sg, q + 1)
                    nv.tensor_tensor(zT[:, q, :], yq, w4[:, 1], ALU.mult).then_inc(e_z, 1)

        g_p, g_s, g_m, g_o, g_k = (S(n) for n in ("glu_done", "glu_sig", "ssm_gated", "mix_done", "gain2_set"))
        ssT = k2T
        with nc.Block() as block:
            @block.sync
            def _(sp):
                for k in range(K_IN2 + 4 + RING, K_MOE2 + RING):
                    load_unit(sp, k)

            @block.tensor
            def _(pe):
                nt = nc.tensor
                unit_arrived(pe, K_GLU)
                w = unit(K_GLU)
                for b in range(2):
                    for cb in range(2):
                        for c in range(4):
                            col_ = (2 * b + cb) * 128
                            ins = nt.matmul(ps[:, b, cb * 256:cb * 256 + 256], w[:, c, col_:col_ + 128], zT[:, c, :], start=c == 0, stop=c == 3)
                    ins.then_inc(g_p, 1)
                pe.wait_ge(g_p, 2)
                pe.sem_inc(units_used, 1)
                for k, src in enumerate((aT, ssT)):
                    unit_arrived(pe, K_OUT2 + k)
                    if k:
                        pe.wait_ge(g_m, 1)
                    for i in range(NT):
                        for h in range(2):
                            for c in range(4):
                                ins = nt.matmul(ps[:, 4 + 2 * i + h, :], src[:, c, i * 128:i * 128 + 128],
                                                unit(K_OUT2 + k)[:, c, h * 512:h * 512 + 512], start=k == 0 and c == 0, stop=k == 1 and c == 3)
                    ins.then_inc(g_o, 1)
                pe.wait_ge(g_o, 2)
                pe.sem_inc(units_used, 2)

            @block.scalar
            def _(a):
                a.dma_start(grow[:], A["norm2_g_2"].to_broadcast([128, D])).then_inc(s_grow, 16)
                for c in range(4):
                    a.wait_ge(g_p, c // 2 + 1)
                    nc.scalar.activation(ssT[:, c, :], ps[:, c // 2, (c % 2) * 256:(c % 2) * 256 + 256], ACT.Sigmoid,
                                         bias=VT[:, 52 + c:53 + c]).then_inc(g_s, 1)

            @block.vector
            def _(v):
                link = chain(v, "v_chain")
                nv = nc.vector
                v.wait_ge(g_s, 4)
                nv.tensor_tensor(ssT[:], ssT[:], zT[:], ALU.mult).then_inc(g_m, 1)
                v.wait_ge(g_o, 2)
                for i in range(NT):
                    link(nv.tensor_tensor(junk[:], ps[:, 4 + 2 * i:6 + 2 * i, :].rearrange("p b c -> p (b c)"), mod[:, 2 * D:3 * D], ALU.mult))
                    link(nv.tensor_tensor(X[:, i, :], X[:, i, :], junk[:], ALU.add))
                v.wait_ge(s_grow, 80)
                nv.scalar_tensor_tensor(out=grow[:], in0=mod[:, 4 * D:5 * D], scalar=1.0, in1=grow[:], op0=ALU.add,
                                        op1=ALU.mult).then_inc(g_k, 1)
        p2b.close()
        retire_semaphores()
        n3 = Norm("n3", shift=mod[:, 3 * D:4 * D])
        n3.gains = 5
        m, acc = mixture("m2_", K_MOE2, 12, moe2_src, "w_router_2", "b_router_2", 4, False, n3, lambda sp: None, False)
        nz = Norm("nz")
        z_x, z_o = S("normed_out"), S("out_done")
        with nc.Block() as block:
            @block.scalar
            def _(a):
                a.dma_start(grow[:], A["final_g_2"].rearrange("(a d) -> a d", a=1).to_broadcast([128, D])).then_inc(s_grow, 16)
                nz.act_root(a)

            @block.vector
            def _(v):
                link = chain(v, "v_chain")
                nv = nc.vector
                for i in range(NT):
                    link(nv.tensor_tensor(acc[:, i, :], acc[:, i, :], mod[:, 5 * D:6 * D], ALU.mult))
                    link(nv.tensor_tensor(X[:, i, :], X[:, i, :], acc[:, i, :], ALU.add))
                nz.dve_stats(v, link)
                v.wait_ge(s_grow, 96)
                for i in range(NT):
                    nv.scalar_tensor_tensor(out=X[:, i, :], in0=X[:, i, :], scalar=st[:, 4 + i:5 + i], in1=grow[:],
                                            op0=ALU.mult, op1=ALU.mult).then_inc(z_x, 1)

            @block.sync
            def _(sp):
                for i in range(NT):
                    sp.wait_ge(z_x, i + 1)
                    sp.dma_start(out[0, i * 128:i * 128 + 128, :], X[:, i, :]).then_inc(z_o, 16)
                sp.wait_ge(z_o, 32)
        m.close()
        p2.close()


def kernel(**inputs):
    import numpy as _np
    import concourse.bacc as _bacc
    from concourse import mybir as _mybir
    from concourse.bass_utils import run_bass_kernel_spmd as _run

    nc = _bacc.Bacc("TRN2", target_bir_lowering=False, num_devices=1)
    arrays, args = {}, {}
    for name, a in list(inputs.items()) + [("cst", constants())]:
        a = _np.ascontiguousarray(a)
        arrays[f"in_{name}_dram"] = a
        args[name] = nc.dram_tensor(f"in_{name}_dram", a.shape, _mybir.dt.from_np(a.dtype), kind="ExternalInput").ap()
    out = nc.dram_tensor("out_0_dram", (1, T, D), _mybir.dt.float32, kind="ExternalOutput").ap()
    bass_block_pair(nc, args, out)
    r = _run(nc, [arrays], core_ids=[0])
    return r.results[0]["out_0_dram"]
```

```python
import numpy as np
import concourse.bass as bass
from concourse import mybir
from contextlib import ExitStack

F32 = mybir.dt.float32
I32 = mybir.dt.int32
ALU = mybir.AluOpType
ACT = mybir.ActivationFunctionType
AX = mybir.AxisListType

T, D = 256, 1024
NT = T // 128
KC = D // 128
EPS = 1e-6
NEG = -1e30
IN_COLS = 5400
C_KV, C_GATE, C_HQ, C_HF, C_HI, C_HG, C_MRG = 512, 1280, 1304, 1816, 2328, 2840, 3352
NCMP = 15
NE = 32
CAP = 64
ROUNDS = T // CAP
PAIRS = NE // 2
RING = 6
UNIT = 4096
LEVELS = 7

WIDTHS = [("ident", 128), ("ones", 128), ("iota", 128), ("before", 128), ("causal", 128),
          ("lvl", LEVELS * 128), ("cos", NT * 8), ("sin", NT * 8), ("ccos", 8), ("csin", 8),
          ("cadd", NT * 16), ("cmul", NT * 16), ("tie8", 64), ("tie4", 16),
          ("even", 1), ("odd", 1), ("geven", 1), ("godd", 1), ("full", 256),
          ("tie32", 1024)]
CO = {}
NCST = 0
for _n, _w in WIDTHS:
    CO[_n] = (NCST, _w)
    NCST += _w


def constants():
    c = np.zeros((128, NCST), np.float32)

    def put(name, a):
        o, w = CO[name]
        c[:, o:o + w] = np.broadcast_to(np.asarray(a, np.float32).reshape(-1, w), (128, w))

    p = np.arange(128)
    put("ident", np.eye(128))
    put("ones", np.ones((128, 128)))
    s = np.arange(128) % 64
    put("iota", s)
    put("before", p[:, None] < p[None, :])
    put("causal", np.where(p[None, :] <= p[:, None], 0.0, NEG))
    lv = []
    for l in range(LEVELS):
        half, blk = 1 << l, 2 << l
        s_, t_ = p[:, None], p[None, :]
        lv.append((s_ // blk == t_ // blk) & (s_ % blk < half) & (t_ % blk >= half))
    put("lvl", np.stack(lv, 1).reshape(128, -1))
    inv = (np.float32(500000.0) ** (-np.arange(8, dtype=np.float32) / 8)).astype(np.float32)
    pos = np.arange(T, dtype=np.float32)
    ang = (pos[:, None] * inv[None, :]).reshape(NT, 128, 8).transpose(1, 0, 2)
    put("cos", np.cos(ang).reshape(128, -1))
    put("sin", np.sin(ang).reshape(128, -1))
    cang = ((p % 32) * 16).astype(np.float32)[:, None] * inv[None, :]
    put("ccos", np.cos(cang))
    put("csin", np.sin(cang))
    tp = np.arange(T).reshape(NT, 128).T
    ok = (np.arange(16)[None, None, :] * 16 + 31 <= tp[:, :, None])
    put("cadd", np.where(ok, 0.0, NEG).reshape(128, -1))
    put("cmul", ok.reshape(128, -1))
    for n in (32, 8, 4):
        i = np.arange(n)
        put(f"tie{n}", (i[None, :] < i[:, None]).reshape(-1))
    put("even", (p < 64)[:, None])
    put("odd", (p >= 64)[:, None])
    put("geven", ((p // 16) % 2 == 0)[:, None])
    put("godd", ((p // 16) % 2 == 1)[:, None])
    put("full", np.ones(256))
    return c


def bass_block_pair(nc, A, out):
    top = ExitStack()
    with top:
        def sbuf(ctx, name, shape, dt=F32):
            return ctx.enter_context(nc.sbuf_tensor(name, shape, dt))

        sems = {}
        cleared = []
        LASTING = {"units_used", "gain_in"} | {f"ring_ready{j}" for j in range(RING)}

        def S(name):
            if name not in sems:
                sems[name] = cleared.pop() if cleared else top.enter_context(nc.semaphore(name))
            return sems[name]

        def retire_semaphores():
            old = [n for n in sems if n not in LASTING]
            with nc.Block() as block:
                @block.gpsimd
                def _(g):
                    for n in old:
                        g.sem_clear(sems[n])
            for n in old:
                cleared.append(sems.pop(n))
            chains.clear()

        CS = sbuf(top, "CS", [128, CO["tie32"][0]])
        ring = sbuf(top, "ring", [128, RING, UNIT])
        X = sbuf(top, "X", [128, NT, D])
        hn = sbuf(top, "hn", [128, NT, KC, 128])
        hT = sbuf(top, "hT", [128, KC, T])
        grow = sbuf(top, "grow", [128, D])
        st = sbuf(top, "st", [128, 8])
        junk = sbuf(top, "junk", [128, D])
        ps = top.enter_context(nc.psum_tensor("ps", [128, 8, 512], F32))

        def K(name, parts=128):
            o, w = CO[name]
            return CS[0:parts, o:o + w]

        ident = K("ident")
        ring_ready = [S(f"ring_ready{j}") for j in range(RING)]
        units_used = S("units_used")

        units = []

        def cols(w, c0, c1):
            return [(w[0].rearrange("(p t) n -> p t n", t=KC)[:, :, c0:c1], KC, c1 - c0)]

        def rows(w, t0, t1, nt):
            n = w.shape[-1]
            return [(w[0].rearrange("(t p) n -> p t n", t=nt)[:, t0:t1, :], t1 - t0, n)]

        SECT = [(C_HF, C_HI), (C_HQ, C_HF), (0, 512), (512, 1024), (1024, C_HQ), (C_HI, C_HG), (C_HG, C_MRG)] + \
               [(C_MRG + 512 * j, C_MRG + 512 * (j + 1)) for j in (2, 3, 0, 1)]
        for c0, c1 in SECT:
            units += cols(A["w_in"], c0, c1)
        K_BR = len(units)
        units += rows(A["w_br_hg"], 0, 4, 4) + rows(A["w_br_nsa"], 0, 4, 4)
        K_OUT = len(units)
        units += rows(A["w_out"], 0, 4, 8) + rows(A["w_out"], 4, 8, 8)
        K_MOE1 = len(units)
        units += [None] * (3 * NE)
        K_ADA = len(units)
        for j in range(12):
            units += cols(A["w_ada_2"], 512 * j, 512 * (j + 1))
        K_IN2 = len(units)
        for j in range(4):
            units += cols(A["w_in_2"], 512 * j, 512 * (j + 1))
        K_GLU = len(units)
        units += rows(A["w_glu_2"], 0, 4, 4)
        K_OUT2 = len(units)
        units += rows(A["w_out_2"], 0, 4, 8) + rows(A["w_out_2"], 4, 8, 8)
        K_MOE2 = len(units)
        units += [None] * (6 * NE)

        def load_unit(sp, k):
            if k >= RING:
                sp.wait_ge(units_used, k - RING + 1)
            if K_MOE1 <= k < K_ADA:
                src, dst = moe1_src(0, k - K_MOE1), ring[:, k % RING, :]
            elif k >= K_MOE2:
                src, dst = moe2_src(0, k - K_MOE2), ring[:, k % RING, :]
            else:
                src, n, w = units[k]
                dst = ring[:, k % RING, 0:n * w].rearrange("p (t n) -> p t n", t=n)
            sp.dma_start(dst, src).then_inc(ring_ready[k % RING], 16)

        def unit_arrived(pe, k):
            pe.wait_ge(ring_ready[k % RING], 16 * (k // RING + 1))

        def unit(k):
            n, w = units[k][1:]
            return ring[:, k % RING, 0:n * w].rearrange("p (t n) -> p t n", t=n)

        def moe1_src(e0, j):
            w = A[("w_gate", "w_up", "w_down")[j // 2]]
            t = 4 if j >= 4 else KC
            return w[0, bass.ds(e0 + j % 2, 1), :, :].rearrange("a (p t) n -> (a p) (t n)", t=t)

        def moe2_src(e0, j):
            e = bass.ds(e0 + j % 2, 1)
            if j < 8:
                return A["w1_2"][0, e, :, :].rearrange("a (p u t) n -> (a p) u (t n)", u=4, t=2)[:, j // 2, :]
            return A["w2_2"][0, e, :, :].rearrange("a (p u t) n -> (a p) u (t n)", u=2, t=4)[:, j // 2 - 4, :]

        def chain(eng, name):
            s, n = S(name), chains.setdefault(name, [0])

            def link(ins):
                n[0] += 1
                ins.then_inc(s, 1)
                eng.wait_ge(s, n[0])
            return link
        chains = {}

        class Norm:

            def __init__(self, tag, shift=None):
                self.tag, self.shift = tag, shift
                self.sq, self.sd, self.rt = S(tag + "_squares"), S(tag + "_variance"), S(tag + "_root")
                self.hn, self.tr, self.ev = S(tag + "_normed"), S(tag + "_transposed"), S(tag + "_hT")

            def act_root(self, a):
                a.wait_ge(self.sd, 1)
                nc.scalar.activation(st[:, 2:4], st[:, 2:4], ACT.Sqrt).then_inc(self.rt, 1)

            def act(self, a):
                self.act_root(a)
                for t in range(KC):
                    if t % 2 == 0:
                        a.wait_ge(self.tr, t // 2 + 1)
                        nc.scalar.activation(hT[:, t:t + 2, :].rearrange("p t q -> p (t q)"), ps[:, t // 2, :],
                                             ACT.Copy).then_inc(self.ev, 1)

            def dve_stats(self, v, link):
                for i in range(NT):
                    link(nc.vector.tensor_tensor_reduce(out=junk[:], in0=X[:, i, :], in1=X[:, i, :], scale=1.0,
                                                        scalar=0.0, op0=ALU.mult, op1=ALU.add,
                                                        accum_out=st[:, i:i + 1]))
                nc.vector.tensor_scalar(st[:, 2:4], st[:, 0:2], 1.0 / D, EPS, ALU.mult, ALU.add).then_inc(self.sd, 1)
                v.wait_ge(self.rt, 1)
                link(nc.vector.reciprocal(st[:, 4:6], st[:, 2:4]))

            def dve(self, v, link):
                self.dve_stats(v, link)
                for i in range(NT):
                    o = hn[:, i].rearrange("q t p -> q p t")
                    x = X[:, i, :].rearrange("q (p t) -> q p t", t=KC)
                    g = grow[:].rearrange("q (p t) -> q p t", t=KC)
                    ins = nc.vector.scalar_tensor_tensor(out=o, in0=x, scalar=st[:, 4 + i:5 + i], in1=g,
                                                         op0=ALU.mult, op1=ALU.mult)
                    if self.shift is not None:
                        link(ins)
                        b = self.shift.rearrange("q (p t) -> q p t", t=KC)
                        ins = nc.vector.tensor_tensor(o, o, b, ALU.add)
                    ins.then_inc(self.hn, 1)

            def pe(self, pe):
                for t in range(KC):
                    for i in range(NT):
                        pe.wait_ge(self.hn, i + 1)
                        ins = nc.tensor.transpose(ps[:, t // 2, (t % 2) * 256 + i * 128:(t % 2) * 256 + i * 128 + 128],
                                                  hn[:, i, t, :], ident)
                    if t % 2 == 1:
                        ins.then_inc(self.tr, 1)

        p1 = ExitStack()
        qkv = sbuf(p1, "qkv", [128, NT, C_HQ])
        hgi = sbuf(p1, "hgi", [128, NT, 512])
        hgg = sbuf(p1, "hgg", [128, NT, 512])
        mrg = sbuf(p1, "mrg", [128, NT, 2 * D])
        hqT = sbuf(p1, "hqT", [128, 4, T])
        hfT = sbuf(p1, "hfT", [128, 4, T])
        pos2 = sbuf(p1, "pos2", [32, 128])
        lbn = sbuf(p1, "lbn", [8, 128])
        hgn = sbuf(p1, "hgn", [128, 1])
        W1 = sbuf(p1, "W1", [128, 6400])
        Xf = X[:].rearrange("p i c -> p (i c)")
        mf = mrg[:].rearrange("p i c -> p (i c)")
        hnf = hn[:].rearrange("p i t q -> p (i t q)")
        hTf = hT[:].rearrange("p t q -> p (t q)")
        qT = Xf[:, 0:1024].rearrange("p (a q) -> p a q", a=4)
        kT = Xf[:, 1024:2048].rearrange("p (a q) -> p a q", a=4)
        kvT = W1[:, 4096:4608].rearrange("p (g q) -> p g q", g=2)
        kvc = W1[:, 4608:5120].rearrange("p (i g c) -> p i g c", i=2, g=2)
        PcT = W1[0:64, 4096:5120].rearrange("p (i r q) -> p i r q", i=2, r=4)
        Sc = W1[:, 5120:5376].rearrange("p (i h n) -> p i h n", i=2, h=8)
        Pc = W1[:, 5376:5888].rearrange("p (i r g n) -> p i r g n", i=2, r=4, g=2)
        rtmp = W1[:, 5120:5888]
        sm = W1[:, 5888:6400]
        kc, vcb = sm[0:64, 0:64], sm[0:64, 64:192]
        kcd = sm[0:64, 192:320]
        kcT = sm[:, 320:384]
        posT, lraw = sm[:, 384:416], sm[:, 416:424]
        wts = sm[:, 424:480]
        kdup = junk[:].rearrange("p (i a b c) -> p i a b c", i=2, a=4, b=2)
        blkT = hnf.rearrange("p (l g n) -> p l g n", l=32, g=2)
        Wc = mf[:, 2048:4096].rearrange("p (l e) -> p l e", l=32)
        P = hnf.rearrange("p (s a k) -> p s a k", s=2, a=4)
        PT = W1[:, 1024:3072].rearrange("p (b h q) -> p b h q", b=2, h=8)
        onsa = junk[:].rearrange("p (i c) -> p i c", i=2)
        onT = grow[:].rearrange("p (a q) -> p a q", a=4)
        hq, hf = hqT[:].rearrange("p h t -> p (h t)"), hfT[:].rearrange("p h t -> p (h t)")
        Dl = hf
        QK = [mf[:, 0:1024], mf[:, 1024:2048]]
        kk, bsum = W1[:, 0:1024], W1[:, 1024:2048]
        Am = [W1[:, 2048:2560], W1[:, 2560:3072], W1[:, 3072:3584]]
        hp_ = W1[:, 3584:4096]
        osq = hfT[:].rearrange("p (i a) t -> p i (a t)", i=2)
        hst = sm[:, 480:504]
        lb, oml = sm[:, 504:508], sm[:, 508:512]
        ohn = bsum.rearrange("p (i c) -> p i c", i=2)
        ohT = kk.rearrange("p (a q) -> p a q", a=4)

        n0 = Norm("n0")
        s_cst, s_x, s_grow, s_wc = S("consts_in"), S("x_in"), S("gain_in"), S("nsa_small_in")
        s_proj, s_pev, s_gate = S("proj_done"), S("proj_kept"), S("gates_ready")
        s_rope, s_tq, s_tqk, s_tv, s_tvk, s_sh, s_shk = (S(n) for n in (
            "nsa_roped", "qkT_done", "qkT_kept", "cmp_inT", "cmp_inT_kept", "shortT", "shortT_kept"))
        s_blk, s_cmp, s_kcd, s_kct, s_kctk = (S(n) for n in ("blocks_built", "compressed", "kcmp_roped", "kcmpT_done", "kcmpT_kept"))
        s_sc, s_scs, s_sce, s_pc, s_pct, s_pctk = (S(n) for n in (
            "cmp_scores", "cmp_shifted", "cmp_exp", "cmp_probs", "cmp_probsT", "cmp_probsT_kept"))
        s_s, s_mx, s_exp, s_p, s_pt, s_ptk, s_pv = (S(n) for n in (
            "scores", "scores_max", "scores_exp", "probs", "probsT", "probsT_kept", "pv_done"))
        s_o, s_oT, s_oTk = S("nsa_out_kept"), S("nsa_outT"), S("nsa_outT_kept")
        h_f, h_ln, h_d, h_e, h_qk, h_a, h_am = (S(n) for n in (
            "forget", "log_forget", "level_exponents", "level_factors", "level_operands", "level_products", "level_added"))
        h_o, h_sq, h_v, h_r, h_n, h_g, h_t, h_tk, h_lb = (S(n) for n in (
            "hg_out", "hg_squares", "hg_variance", "hg_root", "hg_normed", "hg_gated", "hg_outT", "hg_outT_kept", "hg_bound"))
        b_h, b_hm, b_m, b_mx, b_t, b_tk, b_o, b_x = (S(n) for n in (
            "hg_branch", "hg_branch_gated", "nsa_branch", "mixed", "mixedT", "mixedT_kept", "out_proj", "x1"))
        DEST = [hfT, hqT, (qkv, 0, 512), (qkv, 512, 1024), (qkv, 1024, C_HQ), (hgi, 0, 512), (hgg, 0, 512),
                (mrg, 1024, 1536), (mrg, 1536, 2048), (mrg, 0, 512), (mrg, 512, 1024)]
        STEPS = [(i, ty) for i in range(NT) for ty in range(2)]
        ORDER = "F0 F1 Hpre F2 F3 H0 F4 H1 F5 H2 F6 H3 F7 H4 F8 H5 F9 H6 Nrope F10 H7 F11 H8 Nqk F12 Ho Nkv F13 Gate Hgate Ncmp Ht " \
                "F14 Nkc F15 Nsc F16 Npc M0 F17 SigH Q0 M1 F18 Q1 M2 F19 Q2 M3 F20 F21 Bh0 SigN Q3 Bh1 Nout Bn"

        def bc(ap, shape):
            return ap.to_broadcast(shape)

        def follow(steps):
            for word in ORDER.split():
                name, n = word.rstrip("0123456789"), word.lstrip("ABCDEFGHIJKLMNOPQRSTUVWXYZabcdefghijklmnopqrstuvwxyz")
                if name in steps:
                    steps[name](int(n)) if n else steps[name]()

        def rope(eng, link, t1, t2, cos, sin, shape, tmp):
            n = int(np.prod(shape[1:]))
            names = "abcd"[:len(shape) - 1]
            pat = "p (" + " ".join(names) + ") -> p " + " ".join(names)
            kw = dict(zip(names, shape[1:]))
            b = [tmp[0:shape[0], j * n:(j + 1) * n].rearrange(pat, **kw) for j in range(4)]
            link(eng.tensor_tensor(b[0], t1, cos, ALU.mult))
            link(eng.tensor_tensor(b[1], t2, sin, ALU.mult))
            link(eng.tensor_tensor(b[2], t2, cos, ALU.mult))
            link(eng.tensor_tensor(b[3], t1, sin, ALU.mult))
            link(eng.tensor_tensor(t1, b[0], b[1], ALU.subtract))
            return eng.tensor_tensor(t2, b[2], b[3], ALU.add)

        with nc.Block() as block:
            @block.sync
            def _(sp):
                sp.dma_start(X[:], A["x"][0].rearrange("(i q) d -> q i d", i=NT)).then_inc(s_x, 16)
                for k in range(4):
                    load_unit(sp, k)
                sp.dma_start(pos2[:, 0:64], A["cmp_pos"][0]).then_inc(s_wc, 16)
                sp.dma_start(pos2[:, 64:128], A["cmp_pos"][0]).then_inc(s_wc, 16)
                sp.dma_start(lbn[:], A["hg_lb_logits"].rearrange("r (h k) -> (r h) k", h=4)).then_inc(s_wc, 16)
                sp.dma_start(Wc[0:64], A["w_cmp_k"][0].rearrange("(l d) e -> d l e", l=32)).then_inc(s_wc, 16)
                sp.dma_start(Wc[64:128], A["w_cmp_v"][0].rearrange("(l d) e -> d l e", l=32)).then_inc(s_wc, 16)
                sp.dma_start(hgn[:], A["hg_norm"].rearrange("a v -> v a")).then_inc(s_wc, 16)
                for k in range(4, K_MOE1 + RING):
                    load_unit(sp, k)

            @block.gpsimd
            def _(g):
                link = chain(g, "g_chain")
                ng = nc.gpsimd
                g.wait_ge(s_cst, 16)
                g.wait_ge(s_pev, 10)
                for i in range(NT):
                    cos = K("cos")[:, i * 8:i * 8 + 8].rearrange("p (a c) -> p a c", a=1)
                    sin = K("sin")[:, i * 8:i * 8 + 8].rearrange("p (a c) -> p a c", a=1)
                    q = qkv[:, i, 0:512].rearrange("p (h d) -> p h d", h=8)
                    link(rope(ng, link, q[:, :, 0:8], q[:, :, 8:16], bc(cos, [128, 8, 8]), bc(sin, [128, 8, 8]), [128, 8, 8], rtmp))
                    for c in (768, 1024):
                        k = qkv[:, i, c:c + 128].rearrange("p (h d) -> p h d", h=2)
                        link(rope(ng, link, k[:, :, 0:8], k[:, :, 8:16], bc(cos, [128, 2, 8]), bc(sin, [128, 2, 8]), [128, 2, 8], rtmp))
                for i in range(NT):
                    for ty in range(2):
                        src = qkv[:, i, 768 + 256 * ty:768 + 256 * ty + 128].rearrange("p (g a d) -> p g a d", g=2, a=1)
                        link(ng.tensor_copy(kdup[:, i, 2 * ty:2 * ty + 2], bc(src, [128, 2, 2, 64])))
                    src = qkv[:, i, 512:768].rearrange("p (k g d) -> p g k d", k=2, g=2)
                    link(ng.tensor_copy(kvc[:, i].rearrange("p g (k d) -> p g k d", k=2), src))
                ng.memset(hnf, 0.0).then_inc(s_rope, 1)

            @block.vector
            def _(v):
                link = chain(v, "v_chain")
                nv = nc.vector
                v.wait_ge(s_x, 16)
                v.wait_ge(s_grow, 16)
                n0.dve(v, link)

                def exponents(L):
                    half = 1 << L
                    bv = bsum.rearrange("p (n k) -> p n k", k=2 * half)
                    dv = Dl.rearrange("p (n k) -> p n k", k=2 * half)
                    ref = bc(bv[:, :, half - 1:half], [128, 512 // half, half])
                    nv.tensor_tensor(dv[:, :, half:], bv[:, :, half:], ref, ALU.subtract)
                    nv.tensor_tensor(dv[:, :, 0:half], ref, bv[:, :, 0:half], ALU.subtract).then_inc(h_d, 1)

                def Hpre():
                    v.wait_ge(s_shk, 1)
                    nv.tensor_tensor(lb, lraw[:, 0:4], lraw[:, 4:8], ALU.subtract).then_inc(h_lb, 1)
                    v.wait_ge(h_lb, 2)
                    link(nv.tensor_scalar(oml, lb, -1.0, 1.0, ALU.mult, ALU.add))
                    v.wait_ge(s_pev, 2)
                    for h in range(4):
                        ins = nv.tensor_scalar(hfT[:, h], hfT[:, h], oml[:, h:h + 1], lb[:, h:h + 1], ALU.mult, ALU.add)
                    link(ins)
                    nv.tensor_scalar(kk, hf, -1.0, 1.0, ALU.mult, ALU.add).then_inc(h_f, 1)
                    v.wait_ge(h_ln, 1)
                    for h in range(4):
                        ins = nv.tensor_tensor_scan(bsum[:, h * T:h * T + T], K("full"), hfT[:, h], 0.0, ALU.mult, ALU.add)
                    link(ins)
                    exponents(0)

                def H(n):
                    if n <= LEVELS:
                        half = 1 << n
                        dv = Dl.rearrange("p (n k) -> p n k", k=2 * half)
                        qv = QK[n % 2].rearrange("p (n k) -> p n k", k=2 * half)
                        hv = hq.rearrange("p (n k) -> p n k", k=2 * half)
                        kv = kk.rearrange("p (n k) -> p n k", k=2 * half)
                        v.wait_ge(s_pev, 4)
                        v.wait_ge(h_e, n + 1)
                        if n >= 2:
                            v.wait_ge(h_a, n)
                        nv.tensor_tensor(qv[:, :, half:], hv[:, :, half:], dv[:, :, half:], ALU.mult)
                        nv.tensor_tensor(qv[:, :, 0:half], kv[:, :, 0:half], dv[:, :, 0:half], ALU.mult).then_inc(h_qk, 1)
                    if n < LEVELS:
                        v.wait_ge(h_qk, n + 1)
                        exponents(n + 1)
                    v.wait_ge(h_a, n + 1)
                    if n > LEVELS:
                        nv.tensor_copy(Am[2], ps[:, 0, :]).then_inc(h_am, 1)
                        return
                    m = ident if n == 0 else K("lvl")[:, (n - 1) * 128:n * 128]
                    m = bc(m.rearrange("p (a t) -> p a t", a=1), [128, 4, 128])
                    for i in range(NT):
                        src = ps[:, i, :].rearrange("p (h t) -> p h t", h=4)
                        if n == 0:
                            ins = nv.tensor_tensor(Am[i].rearrange("p (h t) -> p h t", h=4), src, m, ALU.mult)
                        else:
                            link(nv.tensor_tensor(hp_.rearrange("p (h t) -> p h t", h=4), src, m, ALU.mult))
                            ins = nv.tensor_tensor(Am[i], Am[i], hp_, ALU.add)
                        if i == 0:
                            link(ins)
                    ins.then_inc(h_am, 1)
                    v.wait_ge(h_am, n + 1)

                def Ho():
                    v.wait_ge(h_sq, 2)
                    link(nv.tensor_reduce(hst[:, 0:8], osq[:].rearrange("p i (h c) -> p (i h) c", h=4), AX.X, ALU.add))
                    nv.tensor_scalar(hst[:, 8:16], hst[:, 0:8], 1.0 / 128, EPS, ALU.mult, ALU.add).then_inc(h_v, 1)
                    v.wait_ge(h_r, 1)
                    link(nv.reciprocal(hst[:, 16:24], hst[:, 8:16]))
                    for i in range(NT):
                        r = bc(hst[:, 16 + 4 * i:20 + 4 * i].rearrange("p (h n) -> p h n", n=1), [128, 4, 128])
                        o = ohn[:, i].rearrange("p (h c) -> p h c", h=4)
                        nv.tensor_tensor(o, ps[:, i, :].rearrange("p (h c) -> p h c", h=4), r, ALU.mult).then_inc(h_n, 1)

                def Hgate():
                    v.wait_ge(h_n, 2)
                    v.wait_ge(s_gate, 1)
                    nv.tensor_tensor(bsum, bsum, hgg[:].rearrange("p i c -> p (i c)"), ALU.mult).then_inc(h_g, 1)

                def Nkv():
                    v.wait_ge(s_tvk, 1)
                    v.wait_ge(s_rope, 1)
                    for g in range(2):
                        for a in range(2):
                            src = kvT[:, g, 16 * a:16 * a + 240].rearrange("p (n b) -> p b n", b=16)
                            po = posT[:, 16 * a:16 * a + 16].rearrange("p (b n) -> p b n", n=1)
                            nv.tensor_tensor(blkT[:, 16 * a:16 * a + 16, g, 0:NCMP], src, bc(po, [128, 16, NCMP]),
                                             ALU.add).then_inc(s_blk, 1)

                def Ncmp():
                    v.wait_ge(s_cmp, 1)
                    nv.tensor_copy(kc, ps[0:64, 4, 0:64])
                    link(nv.memset(vcb, 0.0))
                    nv.tensor_copy(vcb[0:32, 0:64], ps[0:32, 5, 0:64])
                    link(nv.tensor_copy(vcb[32:64, 64:128], ps[32:64, 5, 0:64]))
                    link(rope(nv, link, kc[:, 0:8], kc[:, 8:16], K("ccos", 64), K("csin", 64), [64, 8], rtmp))
                    nv.tensor_copy(kcd.rearrange("p (a d) -> p a d", a=2),
                                   bc(kc.rearrange("p (a d) -> p a d", a=1), [64, 2, 64])).then_inc(s_kcd, 1)

                def Nsc():
                    v.wait_ge(s_sc, 1)
                    for i in range(NT):
                        add = K("cadd")[:, i * 16:i * 16 + 16].rearrange("p (a n) -> p a n", a=1)
                        for par in range(2):
                            o = Sc[:, i].rearrange("p (a b) n -> p a b n", b=2)[:, :, par, :]
                            ins = nv.tensor_tensor(o, ps[:, 4 + par, i * 64:i * 64 + 64].rearrange("p (a n) -> p a n", a=4),
                                                   bc(add, [128, 4, 16]), ALU.add)
                    link(ins)
                    S16 = Sc[:].rearrange("p i h n -> p (i h) n")[:, :, 0:NCMP]
                    mx, su = wts[:, 0:16], wts[:, 16:32]
                    link(nv.tensor_reduce(mx, S16, AX.X, ALU.max))
                    nv.tensor_tensor(S16, S16, bc(mx.rearrange("p (h n) -> p h n", n=1), [128, 16, NCMP]),
                                     ALU.subtract).then_inc(s_scs, 1)
                    link(nv.memset(Pc[:, :, :, :, :], 0.0))
                    v.wait_ge(s_sce, 1)
                    link(nv.tensor_reduce(su, S16, AX.X, ALU.add))
                    link(nv.reciprocal(su, su))
                    v.wait_ge(s_gate, 1)
                    link(nv.tensor_tensor(su.rearrange("p (i h) -> p i h", i=2), su.rearrange("p (i h) -> p i h", i=2),
                                          qkv[:, :, C_GATE:C_HQ].rearrange("p i (h b) -> p i h b", b=3)[:, :, :, 0], ALU.mult))
                    link(nv.tensor_tensor(S16, S16, bc(su.rearrange("p (h n) -> p h n", n=1), [128, 16, NCMP]), ALU.mult))
                    for i in range(NT):
                        for g in range(2):
                            mul = K("cmul")[:, i * 16:i * 16 + NCMP].rearrange("p (a n) -> p a n", a=1)
                            nv.tensor_tensor(Pc[:, i, :, g, 0:NCMP], Sc[:, i, 4 * g:4 * g + 4, 0:NCMP],
                                             bc(mul, [128, 4, NCMP]), ALU.mult).then_inc(s_pc, 1)

                def M(n):
                    i, ty = STEPS[n]
                    nk = 128 * (i + 1)
                    P8 = P[:].rearrange("p s a k -> p (s a) k")[:, :, 0:nk]
                    v.wait_ge(s_s, n + 1)
                    if n:
                        v.wait_ge(s_pt, n)
                    src = ps[:, 2:6, :].rearrange("p b (a k) -> p (b a) k", a=2)
                    ca = K("causal").rearrange("p (a k) -> p a k", a=1)
                    ins = nv.tensor_tensor(P8[:, :, nk - 128:nk], src[:, :, nk - 128:nk], bc(ca, [128, 8, 128]), ALU.add)
                    if i:
                        ins = nv.tensor_copy(P8[:, :, 0:128], src[:, :, 0:128])
                    link(ins)
                    m8, w8 = wts[:, 32:40], wts[:, 48:56]
                    link(nv.tensor_reduce(m8, P8, AX.X, ALU.max))
                    nv.tensor_scalar(wts[:, 40:48], m8, -0.125, None, ALU.mult).then_inc(s_mx, 1)
                    v.wait_ge(s_exp, n + 1)
                    link(nv.reciprocal(w8, w8))
                    gate = qkv[:, i, C_GATE:C_HQ].rearrange("p (a s b) -> p s a b", s=2, b=3)[:, :, :, 1 + ty]
                    link(nv.tensor_tensor(w8.rearrange("p (s a) -> p s a", s=2), w8.rearrange("p (s a) -> p s a", s=2), gate, ALU.mult))
                    nv.tensor_tensor(P8, P8, bc(w8.rearrange("p (h n) -> p h n", n=1), [128, 8, nk]), ALU.mult).then_inc(s_p, 1)

                def Bh(i):
                    v.wait_ge(b_h, i + 1)
                    v.wait_ge(s_gate, 2)
                    nv.tensor_tensor(mrg[:, i, D:], mrg[:, i, D:], ps[:, 6:8, :].rearrange("p b c -> p (b c)"), ALU.mult).then_inc(b_hm, 1)

                def Bn():
                    v.wait_ge(s_gate, 3)
                    v.wait_ge(b_hm, 2)
                    for i in range(NT):
                        v.wait_ge(b_m, i + 1)
                        link(nv.tensor_tensor(mrg[:, i, 0:D], mrg[:, i, 0:D], ps[:, 4 + 2 * i:6 + 2 * i, :].rearrange("p b c -> p (b c)"), ALU.mult))
                        nv.tensor_tensor(mrg[:, i, 0:D], mrg[:, i, 0:D], mrg[:, i, D:2 * D], ALU.add).then_inc(b_mx, 1)
                    v.wait_ge(s_x, 32)
                    for i in range(NT):
                        v.wait_ge(b_o, i + 1)
                        nv.tensor_tensor(X[:, i, :], X[:, i, :], ps[:, 4 + 2 * i:6 + 2 * i, :].rearrange("p b c -> p (b c)"),
                                         ALU.add).then_inc(b_x, 1)

                follow(dict(Hpre=Hpre, H=H, Ho=Ho, Hgate=Hgate, Nkv=Nkv, Ncmp=Ncmp, Nsc=Nsc, M=M, Bh=Bh, Bn=Bn))

            @block.scalar
            def _(a):
                na = nc.scalar
                a.dma_start(grow[:], A["attn_norm"].to_broadcast([128, D])).then_inc(s_grow, 16)
                a.dma_start(CS[:], A["cst"][:, 0:CO["tie32"][0]]).then_inc(s_cst, 16)
                n0.act(a)

                def F(n):
                    u, h = divmod(n, 2)
                    a.wait_ge(s_proj, n + 1)
                    if n == 14:
                        a.wait_ge(h_a, LEVELS + 2)
                        a.wait_ge(s_cmp, 1)
                    src, dst = ps[:, 6 + n % 2, :], DEST[u]
                    if type(dst) is tuple:
                        ins = na.activation(dst[0][:, h, dst[1]:dst[2]], src[:, 0:dst[2] - dst[1]], ACT.Copy)
                    else:
                        ins = na.activation(dst[:, 2 * h:2 * h + 2, :].rearrange("p a b -> p (a b)"), src, ACT.Sigmoid if u == 0 else ACT.Copy)
                    ins.then_inc(s_pev, 1)
                    if h:
                        a.sem_inc(units_used, 1)

                def Hpre():
                    a.wait_ge(s_sh, 1)
                    na.activation(sm[:, 384:424], ps[:, 4, 0:40], ACT.Copy).then_inc(s_shk, 1)
                    a.wait_ge(h_lb, 1)
                    na.activation(lb, lb, ACT.Sigmoid).then_inc(h_lb, 1)
                    a.wait_ge(h_f, 1)
                    na.activation(hf, hf, ACT.Ln).then_inc(h_ln, 1)
                    a.wait_ge(h_d, 1)
                    na.activation(Dl, Dl, ACT.Exp).then_inc(h_e, 1)

                def H(n):
                    if n < LEVELS:
                        a.wait_ge(h_d, n + 2)
                        na.activation(Dl, Dl, ACT.Exp).then_inc(h_e, 1)

                def Ho():
                    a.wait_ge(h_qk, LEVELS + 1)
                    for i in range(NT):
                        a.wait_ge(h_o, i + 1)
                        na.activation(osq[:, i], ps[:, i, :], ACT.Square).then_inc(h_sq, 1)
                    a.wait_ge(h_v, 1)
                    na.activation(hst[:, 8:16], hst[:, 8:16], ACT.Sqrt).then_inc(h_r, 1)

                def Gate():
                    a.wait_ge(s_pev, 14)
                    na.activation(qkv[:, :, C_GATE:C_HQ], qkv[:, :, C_GATE:C_HQ], ACT.Sigmoid)
                    na.activation(hgg[:], hgg[:], ACT.Silu).then_inc(s_gate, 1)

                def SigH():
                    a.wait_ge(s_pev, 18)
                    na.activation(mrg[:, :, D:], mrg[:, :, D:], ACT.Sigmoid).then_inc(s_gate, 1)

                def SigN():
                    a.wait_ge(s_pev, 22)
                    na.activation(mrg[:, :, 0:D], mrg[:, :, 0:D], ACT.Sigmoid).then_inc(s_gate, 1)

                def Nqk():
                    a.wait_ge(s_tq, 1)
                    for b in range(4):
                        dst = [qT[:, 0:2], qT[:, 2:4], kT[:, 0:2], kT[:, 2:4]][b]
                        na.activation(dst, ps[:, 2 + b, :].rearrange("p (a q) -> p a q", a=2), ACT.Copy).then_inc(s_tqk, 1)

                def Nkv():
                    a.wait_ge(s_tv, 1)
                    na.activation(kvT[:], ps[:, 2, :].rearrange("p (a q) -> p a q", a=2), ACT.Copy).then_inc(s_tvk, 1)

                def Nkc():
                    a.wait_ge(s_kct, 1)
                    na.activation(kcT, ps[:, 3, 0:64], ACT.Copy).then_inc(s_kctk, 1)

                def Nsc():
                    a.wait_ge(s_scs, 1)
                    S16 = Sc[:].rearrange("p i h n -> p (i h) n")[:, :, 0:NCMP]
                    na.activation(S16, S16, ACT.Exp, scale=0.125).then_inc(s_sce, 1)

                def Npc():
                    a.wait_ge(s_pct, 1)
                    for i in range(NT):
                        na.activation(PcT[:, i], ps[0:64, 2 + i, :].rearrange("p (r q) -> p r q", r=4), ACT.Copy).then_inc(s_pctk, 1)

                def Ht():
                    a.wait_ge(h_t, 1)
                    a.wait_ge(s_wc, 96)
                    for b in range(2):
                        na.activation(ohT[:, 2 * b:2 * b + 2], ps[:, b, :].rearrange("p (a q) -> p a q", a=2), ACT.Copy,
                                      scale=hgn[:, 0:1]).then_inc(h_tk, 1)

                def M(n):
                    i, ty = STEPS[n]
                    nk = 128 * (i + 1)
                    a.wait_ge(s_mx, n + 1)
                    for h in range(8):
                        row = P[:].rearrange("p s a k -> p (s a) k")[:, h, 0:nk]
                        ins = na.activation(row, row, ACT.Exp, bias=wts[:, 40 + h:41 + h], scale=0.125,
                                            accum_out=wts[:, 48 + h:49 + h])
                    ins.then_inc(s_exp, 1)

                def Q(n):
                    i, ty = STEPS[n]
                    a.wait_ge(s_pt, n + 1)
                    a.wait_ge(h_t, 1)
                    if n:
                        a.wait_ge(s_pv, n)
                    for kb in range(i + 1):
                        na.activation(PT[:, kb], ps[:, 2 + 2 * kb:4 + 2 * kb, :].rearrange("p b (c q) -> p (b c) q", c=4),
                                      ACT.Copy).then_inc(s_ptk, 1)
                    if ty:
                        a.wait_ge(s_pv, n + 1)
                        na.activation(onsa[:, i], ps[:, i, :], ACT.Copy).then_inc(s_o, 1)
                    if n == 3:
                        a.dma_start(X[:], A["x"][0].rearrange("(i q) d -> q i d", i=NT)).then_inc(s_x, 16)

                def Nout():
                    a.wait_ge(s_oT, 1)
                    for b in range(2):
                        na.activation(onT[:, 2 * b:2 * b + 2], ps[:, 2 + b, :].rearrange("p (a q) -> p a q", a=2), ACT.Copy).then_inc(s_oTk, 1)

                def Bn():
                    a.wait_ge(b_m, 2)
                    a.dma_start(grow[:], A["ffn_norm"].to_broadcast([128, D])).then_inc(s_grow, 16)
                    for t in range(4):
                        a.wait_ge(b_t, t + 1)
                        na.activation(hT[:, 2 * t:2 * t + 2, :].rearrange("p t q -> p (t q)"), ps[:, t, :],
                                      ACT.Copy).then_inc(b_tk, 1)

                follow(dict(F=F, Hpre=Hpre, H=H, Ho=Ho, Gate=Gate, SigH=SigH, SigN=SigN, Nqk=Nqk, Nkv=Nkv, Nkc=Nkc, Nsc=Nsc,
                            Npc=Npc, Ht=Ht, M=M, Q=Q, Nout=Nout, Bn=Bn))

            @block.tensor
            def _(pe):
                nt = nc.tensor
                pe.wait_ge(s_cst, 16)
                n0.pe(pe)
                pe.wait_ge(s_wc, 96)
                nt.transpose(ps[:, 4, 0:32], pos2[:], K("ident", 32)[:, 0:32])
                nt.transpose(ps[:, 4, 32:40], lbn[:], K("ident", 8)[:, 0:8]).then_inc(s_sh, 1)
                pe.wait_ge(n0.ev, 4)

                def F(n):
                    u, h = divmod(n, 2)
                    unit_arrived(pe, u)
                    w = unit(u)
                    width = units[u][2]
                    if n >= 2:
                        pe.wait_ge(s_pev, n - 1)
                    if type(DEST[u]) is tuple:
                        for t in range(KC):
                            ins = nt.matmul(ps[:, 6 + n % 2, 0:width], hT[:, t, h * 128:h * 128 + 128],
                                            w[:, t, :], start=t == 0, stop=t == KC - 1)
                    else:
                        for cb in range(2):
                            c = (2 * h + cb) * 128
                            for t in range(KC):
                                ins = nt.matmul(ps[:, 6 + n % 2, cb * 256:cb * 256 + 256], w[:, t, c:c + 128], hT[:, t, :],
                                                start=t == 0, stop=t == KC - 1)
                    ins.then_inc(s_proj, 1)

                def H(n):
                    pe.wait_ge(h_f, 1)
                    pe.wait_ge(s_pev, 4)
                    if n:
                        pe.wait_ge(h_qk, n)
                        pe.wait_ge(h_am, n)
                    if n <= LEVELS:
                        for i in range(NT):
                            for h in range(4):
                                c = h * T + i * 128
                                kx, qx = (kk, hq) if n == 0 else (QK[(n - 1) % 2], QK[(n - 1) % 2])
                                ins = nt.matmul(ps[:, i, h * 128:h * 128 + 128], kx[:, c:c + 128], qx[:, c:c + 128],
                                                start=True, stop=True)
                    else:
                        x = QK[(n - 1) % 2]
                        for h in range(4):
                            ins = nt.matmul(ps[:, 0, h * 128:h * 128 + 128], x[:, h * T:h * T + 128], x[:, h * T + 128:h * T + 256],
                                            start=True, stop=True)
                    ins.then_inc(h_a, 1)

                def Ho():
                    pe.wait_ge(h_am, LEVELS + 2)
                    pe.wait_ge(s_pev, 12)
                    for i in range(NT):
                        for h in range(4):
                            c = slice(h * 128, h * 128 + 128)
                            if i:
                                nt.matmul(ps[:, 1, c], Am[2][:, c], hgi[:, 0, c], start=True, stop=False)
                            ins = nt.matmul(ps[:, i, c], Am[i][:, c], hgi[:, i, c], start=i == 0, stop=True)
                        ins.then_inc(h_o, 1)

                def Ht():
                    pe.wait_ge(h_g, 1)
                    for i in range(NT):
                        for h in range(4):
                            ins = nt.transpose(ps[:, h // 2, (h % 2) * 256 + i * 128:(h % 2) * 256 + i * 128 + 128],
                                               ohn[:, i, h * 128:h * 128 + 128], ident)
                    ins.then_inc(h_t, 1)

                def Nqk():
                    pe.wait_ge(s_rope, 1)
                    pe.wait_ge(s_shk, 1)
                    for i in range(NT):
                        for hp in range(4):
                            nt.transpose(ps[:, 2 + hp // 2, (hp % 2) * 256 + i * 128:(hp % 2) * 256 + i * 128 + 128],
                                         qkv[:, i, hp * 128:hp * 128 + 128], ident)
                        for x in range(4):
                            ins = nt.transpose(ps[:, 4 + x // 2, (x % 2) * 256 + i * 128:(x % 2) * 256 + i * 128 + 128],
                                               kdup[:, i, x].rearrange("p b c -> p (b c)"), ident)
                    ins.then_inc(s_tq, 1)

                def Nkv():
                    pe.wait_ge(s_tqk, 1)
                    for i in range(NT):
                        for g in range(2):
                            ins = nt.transpose(ps[:, 2, g * 256 + i * 128:g * 256 + i * 128 + 128], kvc[:, i, g, :], ident)
                    ins.then_inc(s_tv, 1)

                def Ncmp():
                    pe.wait_ge(s_blk, 4)
                    pe.wait_ge(s_tqk, 4)
                    for l in range(32):
                        nt.matmul(ps[0:64, 4, 0:64], blkT[0:64, l].rearrange("p g n -> p (g n)"), Wc[0:64, l, :],
                                  start=l == 0, stop=l == 31)
                        ins = nt.matmul(ps[0:64, 5, 0:64], blkT[64:128, l].rearrange("p g n -> p (g n)"), Wc[64:128, l, :],
                                        start=l == 0, stop=l == 31)
                    ins.then_inc(s_cmp, 1)

                def Nkc():
                    pe.wait_ge(s_kcd, 1)
                    nt.transpose(ps[:, 3, 0:64], kcd, K("ident", 64)[:, 0:64]).then_inc(s_kct, 1)

                def Nsc():
                    pe.wait_ge(s_kctk, 1)
                    for i in range(NT):
                        for h in range(8):
                            r = 64 * (h % 2)
                            ins = nt.matmul(ps[:, 4 + h % 2, i * 64 + (h // 2) * 16:i * 64 + (h // 2) * 16 + 16],
                                            qT[r:r + 64, h // 2, i * 128:i * 128 + 128], kcT[r:r + 64, (h // 4) * 32:(h // 4) * 32 + 16],
                                            start=True, stop=True)
                    ins.then_inc(s_sc, 1)

                def Npc():
                    pe.wait_ge(s_pc, 4)
                    for i in range(NT):
                        for r in range(4):
                            ins = nt.transpose(ps[0:64, 2 + i, r * 128:r * 128 + 128], Pc[:, i, r].rearrange("p g n -> p (g n)"), ident)
                    ins.then_inc(s_pct, 1)

                def M(n):
                    i, ty = STEPS[n]
                    pe.wait_ge(s_pctk, 2)
                    if n:
                        pe.wait_ge(s_ptk, [0, 1, 2, 4][n])
                    for h in range(8):
                        par, a4 = h % 2, h // 2
                        r = 64 * par
                        for kb in range(i + 1):
                            c = (a4 % 2) * 256 + kb * 128
                            ins = nt.matmul(ps[:, 2 + 2 * par + a4 // 2, c:c + 128], qT[r:r + 64, a4, i * 128:i * 128 + 128],
                                            kT[r:r + 64, 2 * ty + h // 4, kb * 128:kb * 128 + 128], start=True, stop=True)
                    ins.then_inc(s_s, 1)
                    if ty == 0:
                        pe.wait_ge(h_tk, 2)
                        for r in range(4):
                            o = ps[:, i, :].rearrange("p (g r d) -> p g r d", g=2, r=4)[:, :, r, :]
                            nt.matmul(o, PcT[:, i, r, :], vcb.rearrange("p (g d) -> p g d", g=2), start=r == 0, stop=False,
                                      skip_group_check=True)

                def Q(n):
                    i, ty = STEPS[n]
                    pe.wait_ge(s_p, n + 1)
                    for kb in range(i + 1):
                        for h in range(8):
                            ins = nt.transpose(ps[:, 2 + 2 * kb + h // 4, (h % 4) * 128:(h % 4) * 128 + 128],
                                               P[:, h // 4, h % 4, kb * 128:kb * 128 + 128], ident)
                    ins.then_inc(s_pt, 1)
                    pe.wait_ge(s_ptk, [1, 2, 4, 6][n])
                    for s8 in range(8):
                        h = 2 * (s8 % 4) + s8 // 4
                        for kb in range(i + 1):
                            c = 896 + 256 * ty + (h // 4) * 64
                            ins = nt.matmul(ps[:, i, h * 64:h * 64 + 64], PT[:, kb, s8, :], qkv[:, kb, c:c + 64],
                                            start=False, stop=(ty == 1 and s8 == 7 and kb == i), skip_group_check=True)
                    ins.then_inc(s_pv, 1)

                def Bh(i):
                    unit_arrived(pe, K_BR)
                    pe.wait_ge(s_pev, 22)
                    if i:
                        pe.wait_ge(b_hm, 1)
                    for h in range(2):
                        for c in range(4):
                            ins = nt.matmul(ps[:, 6 + h, :], ohT[:, c, i * 128:i * 128 + 128], unit(K_BR)[:, c, h * 512:h * 512 + 512],
                                            start=c == 0, stop=c == 3)
                    ins.then_inc(b_h, 1)

                def Nout():
                    pe.wait_ge(s_o, 2)
                    pe.wait_ge(s_ptk, 6)
                    for i in range(NT):
                        for c in range(4):
                            ins = nt.transpose(ps[:, 2 + c // 2, (c % 2) * 256 + i * 128:(c % 2) * 256 + i * 128 + 128],
                                               onsa[:, i, c * 128:c * 128 + 128], ident)
                    ins.then_inc(s_oT, 1)

                def Bn():
                    unit_arrived(pe, K_BR + 1)
                    pe.wait_ge(s_oTk, 2)
                    for i in range(NT):
                        if i:
                            pe.wait_ge(b_hm, 2)
                        for h in range(2):
                            for c in range(4):
                                ins = nt.matmul(ps[:, 4 + 2 * i + h, :], onT[:, c, i * 128:i * 128 + 128],
                                                unit(K_BR + 1)[:, c, h * 512:h * 512 + 512], start=c == 0, stop=c == 3)
                        ins.then_inc(b_m, 1)
                    for t in range(KC):
                        for i in range(NT):
                            pe.wait_ge(b_mx, i + 1)
                            ins = nt.transpose(ps[:, t // 2, (t % 2) * 256 + i * 128:(t % 2) * 256 + i * 128 + 128],
                                               mrg[:, i, t * 128:t * 128 + 128], ident)
                        if t % 2:
                            ins.then_inc(b_t, 1)
                    pe.sem_inc(units_used, 2)
                    for i in range(NT):
                        for k in range(2):
                            unit_arrived(pe, K_OUT + k)
                            for h in range(2):
                                for c in range(4):
                                    if i == 0 and h == 0:
                                        pe.wait_ge(b_tk, 2 * k + c // 2 + 1)
                                    ins = nt.matmul(ps[:, 4 + 2 * i + h, :], hT[:, 4 * k + c, i * 128:i * 128 + 128],
                                                    unit(K_OUT + k)[:, c, h * 512:h * 512 + 512], start=k == 0 and c == 0,
                                                    stop=k == 1 and c == 3)
                        ins.then_inc(b_o, 1)
                    pe.wait_ge(b_o, 2)
                    pe.sem_inc(units_used, 2)

                follow(dict(F=F, H=H, Ho=Ho, Ht=Ht, Nqk=Nqk, Nkv=Nkv, Ncmp=Ncmp, Nkc=Nkc, Nsc=Nsc, Npc=Npc, M=M, Q=Q,
                            Bh=Bh, Nout=Nout, Bn=Bn))
        p1.close()
        def mixture(tag, base, per_pair, w_src, router, bias, topk, first, norm, after, acc_in_x):
            m = ExitStack()
            nr = 36 if first else 32
            FT = 4 if first else 8
            UP = 6 - 2 if first else 8
            BU = 2 if first else 4
            A0, C0 = 4, 6
            def s(n):
                return S(tag + n)

            wr = sbuf(m, tag + "wr", [128, KC, nr])
            brow = sbuf(m, tag + "brow", [1, nr])
            lgE = sbuf(m, tag + "lgE", [128, NT, 32])
            ex = sbuf(m, tag + "ex", [128, NT, 36])
            rk = sbuf(m, tag + "rk", [128, NT, 36])
            sel = sbuf(m, tag + "sel", [128, NT, 32])
            comb = sbuf(m, tag + "comb", [128, NT, 32])
            posx = sbuf(m, tag + "posx", [128, NT, 34])
            rs = sbuf(m, tag + "rs", [128, 16])
            cnt = sbuf(m, tag + "cnt", [128, 1], I32)
            hTf = hT[:].rearrange("p t q -> p (t q)")
            if not first:
                b1s = sbuf(m, "b1s", [32, 2048])
                b2s = sbuf(m, "b2s", [32, D])
                cT = sbuf(m, "cT", [32, T])
                tie32 = sbuf(m, "tie32", [128, 1024])
            e3 = ex[:].rearrange("p i n -> p (i n)")
            exE, exG = e3[:, 0:64], e3[:, 64:72]
            r3 = rk[:].rearrange("p i n -> p (i n)")
            rkE, rkG = r3[:, 0:64], r3[:, 64:72]
            q_in, q_lg, q_ex, q_exd, q_sel, q_pos, q_cnt, q_bT, q_bTk, q_b2, q_acc = (
                s("router_in"), s("logits"), s("shifted"), s("exp"), s("selected"), s("positions"), s("slots"),
                s("combT"), s("combT_kept"), s("bias_out"), s("acc_set"))
            acc = X if acc_in_x else sbuf(m, "acc", [128, NT, D])
            with nc.Block() as block:
                @block.scalar
                def _(a):
                    a.dma_start(wr[:, :, 0:nr - 32], A["w_grp"][0].rearrange("(p t) n -> p t n", t=KC)).then_inc(q_in, 16) if first else None
                    a.dma_start(wr[:, :, nr - 32:nr], A[router][0].rearrange("(p t) n -> p t n", t=KC)).then_inc(q_in, 16)
                    if first:
                        a.dma_start(brow[:, 0:4], A["b_grp"]).then_inc(q_in, 16)
                    a.dma_start(brow[:, nr - 32:nr], A[bias]).then_inc(q_in, 16)
                    if not first:
                        a.dma_start(b1s[:], A["b1_2"][0]).then_inc(q_in, 16)
                        a.dma_start(b2s[:], A["b2_2"][0]).then_inc(q_in, 16)
                        a.dma_start(tie32[:], A["cst"][:, CO["tie32"][0]:]).then_inc(q_in, 16)
                    norm.act(a)
                    a.wait_ge(q_ex, 1)
                    w = 72 if first else 64
                    nc.scalar.activation(e3[:, 0:w], e3[:, 0:w], ACT.Exp).then_inc(q_exd, 1)
                    if not first:
                        a.wait_ge(q_bT, 1)
                        nc.scalar.activation(cT[:], ps[0:32, 6, 0:T], ACT.Copy).then_inc(q_bTk, 1)

                @block.vector
                def _(v):
                    link = chain(v, "v_chain")
                    nv = nc.vector
                    v.wait_ge(s_grow, 16 * norm.gains)
                    norm.dve(v, link)
                    v.wait_ge(q_lg, 1)
                    lp = ps[:, 4, 0:128].rearrange("p (i n) -> p i n", i=NT)
                    lg = lgE[:]
                    link(nv.tensor_copy(lg, lp[:, :, nr - 32:nr]))
                    n = 8 if first else 32
                    lv = lg.rearrange("p i (g n) -> p (i g) n", n=n)
                    G = 64 // n
                    mx = rs[:, 0:G]
                    link(nv.tensor_reduce(mx, lv, AX.X, ALU.max))
                    ins = nv.tensor_tensor(exE.rearrange("p (g n) -> p g n", n=n), lv,
                                           bc(mx.rearrange("p (g n) -> p g n", n=1), [128, G, n]), ALU.subtract)
                    if first:
                        lgG = rkG.rearrange("p (i n) -> p i n", i=NT)
                        link(nv.tensor_copy(lgG, lp[:, :, 0:4]))
                        link(nv.tensor_reduce(rs[:, 8:10], lgG, AX.X, ALU.max))
                        ins = nv.tensor_tensor(exG.rearrange("p (i n) -> p i n", i=NT), lgG,
                                               bc(rs[:, 8:10].rearrange("p (i n) -> p i n", n=1), [128, NT, 4]), ALU.subtract)
                    ins.then_inc(q_ex, 1)

                    def rank(out, l, g, k):
                        b1_ = hTf[:, 0:g * k * k].rearrange("p (g i j) -> p g i j", g=g, i=k)
                        b2_ = hTf[:, 1024:1024 + g * k * k].rearrange("p (g i j) -> p g i j", g=g, i=k)
                        lj = bc(l.rearrange("p g (a j) -> p g a j", a=1), [128, g, k, k])
                        li = bc(l.rearrange("p g (i a) -> p g i a", a=1), [128, g, k, k])
                        tie = bc((tie32[:] if k == 32 else K(f"tie{k}")).rearrange("p (g i j) -> p g i j", g=1, i=k), [128, g, k, k])
                        nv.tensor_tensor(b1_, lj, li, ALU.is_gt)
                        link(nv.tensor_tensor(b2_, lj, li, ALU.is_equal))
                        link(nv.tensor_tensor(b2_, b2_, tie, ALU.mult))
                        link(nv.tensor_tensor(b1_, b1_, b2_, ALU.add))
                        link(nv.tensor_reduce(out, b1_, AX.X, ALU.add))

                    if first:
                        rank(rkE.rearrange("p (g i) -> p g i", g=G), lv, G, n)
                        gl = rs[:, 0:8].rearrange("p (i n) -> p i n", i=NT)
                        link(nv.tensor_copy(gl, rkG.rearrange("p (i n) -> p i n", i=NT)))
                        rank(rkG.rearrange("p (i n) -> p i n", i=NT), gl, NT, 4)
                        link(nv.tensor_scalar(rkG, rkG, 0.5, None, ALU.is_lt))
                        link(nv.tensor_scalar(rkE, rkE, topk - 0.5, None, ALU.is_lt))
                        link(nv.tensor_tensor(sel[:].rearrange("p i (g n) -> p (i g) n", n=8), rkE.rearrange("p (g n) -> p g n", n=8),
                                              bc(rkG.rearrange("p (g n) -> p g n", n=1), [128, 8, 8]), ALU.mult))
                    else:
                        for i in range(NT):
                            rank(rkE[:, 32 * i:32 * i + 32].rearrange("p (g i) -> p g i", g=1), lv[:, i:i + 1], 1, 32)
                        link(nv.tensor_scalar(sel[:].rearrange("p i n -> p (i n)"), rkE, topk - 0.5, None, ALU.is_lt))
                    nv.nop().then_inc(q_sel, 1)
                    v.wait_ge(q_exd, 1)
                    link(nv.tensor_tensor(comb[:], sel[:], exE.rearrange("p (i n) -> p i n", i=NT), ALU.mult))
                    link(nv.tensor_reduce(rs[:, 0:2], comb[:], AX.X, ALU.add))
                    if first:
                        link(nv.tensor_reduce(rs[:, 2:4], exG.rearrange("p (i n) -> p i n", i=NT), AX.X, ALU.add))
                        link(nv.tensor_tensor(rs[:, 0:2], rs[:, 0:2], rs[:, 2:4], ALU.mult))
                    link(nv.reciprocal(rs[:, 4:6], rs[:, 0:2]))
                    nv.tensor_tensor(comb[:], comb[:], bc(rs[:, 4:6].rearrange("p (i n) -> p i n", n=1), [128, NT, 32]),
                                     ALU.mult).then_inc(q_sel, 1)
                    link(nv.memset(posx[:], -1.0))
                    v.wait_ge(q_pos, 1)
                    po = posx[:, :, 0:32]
                    link(nv.tensor_scalar(po, ps[:, 5, 0:64].rearrange("p (i n) -> p i n", i=NT), 1.0, None, ALU.add))
                    link(nv.tensor_tensor(po, po, sel[:], ALU.mult))
                    link(nv.tensor_scalar(po, po, -1.0, None, ALU.add))
                    link(nv.tensor_reduce(rs[:, 6:7], ps[:, 5, 64:96], AX.X, ALU.max))
                    nv.tensor_copy(cnt[:], rs[:, 6:7]).then_inc(q_cnt, 1)
                    if not first:
                        v.wait_ge(q_b2, 1)
                        for i in range(NT):
                            nv.tensor_copy(acc[:, i, :], ps[:, 2 * i:2 * i + 2, :].rearrange("p b c -> p (b c)")).then_inc(q_acc, 1)

                @block.tensor
                def _(pe):
                    nt = nc.tensor
                    norm.pe(pe)
                    pe.wait_ge(norm.ev, 4)
                    pe.wait_ge(q_in, 64 if first else 80)
                    for i in range(NT):
                        for t in range(KC):
                            nt.matmul(ps[:, 4, 64 * i:64 * i + nr], hT[:, t, i * 128:i * 128 + 128], wr[:, t, :], start=t == 0, stop=False)
                        ins = nt.matmul(ps[:, 4, 64 * i:64 * i + nr], K("ones", 1), brow[:], start=False, stop=True)
                    ins.then_inc(q_lg, 1)
                    pe.wait_ge(q_sel, 1)
                    nt.matmul(ps[:, 5, 0:32], K("before"), sel[:, 0, :], start=True, stop=True)
                    nt.matmul(ps[:, 5, 32:64], K("before"), sel[:, 1, :], start=True, stop=False)
                    nt.matmul(ps[:, 5, 32:64], K("ones"), sel[:, 0, :], start=False, stop=True)
                    nt.matmul(ps[:, 5, 64:96], K("ones"), sel[:, 0, :], start=True, stop=False)
                    nt.matmul(ps[:, 5, 64:96], K("ones"), sel[:, 1, :], start=False, stop=True).then_inc(q_pos, 1)
                    if not first:
                        pe.wait_ge(q_sel, 2)
                        for i in range(NT):
                            ins = nt.transpose(ps[0:32, 6, i * 128:i * 128 + 128], comb[:, i, :], ident)
                        ins.then_inc(q_bT, 1)
                        pe.wait_ge(q_bTk, 1)
                        for i in range(NT):
                            for h in range(2):
                                ins = nt.matmul(ps[:, 2 * i + h, :], cT[:, i * 128:i * 128 + 128], b2s[:, 512 * h:512 * h + 512],
                                                start=True, stop=True)
                        ins.then_inc(q_b2, 1)

            Pm = sbuf(m, tag + "Pm", [128, NT, 128])
            Pg = sbuf(m, tag + "Pg", [128, NT, 128])
            xgT = hTf[:, 0:1024].rearrange("p (t c) -> p t c", t=KC)
            GT = sbuf(m, tag + "GT", [128, NT, 128])
            sg = sbuf(m, tag + "sg", [128, 512 * BU // 2])
            hid = sbuf(m, tag + "hid", [128, FT, 128])
            hidT = sbuf(m, tag + "hidT", [128, FT, 128])
            y = hTf[:, 1024:2048]
            if not first:
                gm = sbuf(m, "gm", [128, 1024])
                um = junk
                pick = sbuf(m, "pick", [32, 128])

            def rounds(pre, used, ready_value, ready, used_base):
                def z(n):
                    return S(tag + pre + n)
                p_ready, pg_ready, pick_ready, gathered, xg_kept, gatesT, gt_kept = (
                    z("onehot_ready"), z("weighted_ready"), z("pick_ready"), z("gathered"), z("gathered_kept"), z("weightsT"), z("weightsT_kept"))
                act1, clip, hid_ready, hid_tr, hid_kept, y_act, y_dve, scat, acc_a, acc_c = (
                    z("activated"), z("clipped"), z("hidden_ready"), z("hiddenT"), z("hiddenT_kept"), z("y_low_kept"), z("y_high_kept"),
                    z("scattered"), z("added_tile0"), z("added_tile1"))

                def onehot(v, dst, p2):
                    for i in range(NT):
                        ins = nc.vector.tensor_tensor(dst[:, i, :].rearrange("p (e c) -> p e c", e=2),
                                                      K("iota").rearrange("p (e c) -> p e c", e=2),
                                                      bc(posx[:, i, p2].rearrange("p (e c) -> p e c", c=1), [128, 2, 64]), ALU.is_equal)
                    return ins

                def gather(pe):
                    for t in range(KC):
                        for i in range(NT):
                            ins = nc.tensor.matmul(ps[:, A0 + t // 4, (t % 4) * 128:(t % 4) * 128 + 128], hn[:, i, t, :], Pm[:, i, :],
                                                   start=i == 0, stop=i == NT - 1)
                    ins.then_inc(gathered, 1)

                def gather_kept(a):
                    for b in range(2):
                        ins = nc.scalar.activation(xgT[:, 4 * b:4 * b + 4, :].rearrange("p t c -> p (t c)"), ps[:, A0 + b, :], ACT.Copy)
                    ins.then_inc(xg_kept, 1)

                def up_used(it, n):
                    return it * per_pair + (used_base + n)

                def pe_credit(pe):
                    pe.sem_inc(gatesT, 1)

                def pe_start(pe, it, g):
                    pe.wait_ge(p_ready, g + 1)
                    if pre:
                        pe.wait_ge(acc_a, it + 1)
                        pe.wait_ge(gatesT, it + 1)
                    gather(pe)

                def pe_pair(pe, it, g):
                    nt = nc.tensor
                    pe.wait_ge(xg_kept, g + 1)
                    pe.wait_ge(hid_ready, it + 1)
                    if not first:
                        pe.wait_ge(pick_ready, g + 1)
                        for b in range(4):
                            nt.matmul(ps[:, b, :], pick[:], b1s[:, 512 * b:512 * b + 512], start=True, stop=False, skip_group_check=True)

                    def arrived(j):
                        pe.wait_ge(ready[(base + j) % RING], ready_value(it, j))
                    for u in range(UP // 2):
                        arrived(2 * u)
                        arrived(2 * u + 1)
                        for t in range(KC if first else 2):
                            for b in range(1 if first else 4):
                                for e in range(2):
                                    w = ring[:, (base + 2 * u + e) % RING, :]
                                    if first:
                                        ins = nt.matmul(ps[64 * e:64 * e + 64, u, :], xgT[:, t, 64 * e:64 * e + 64], w[:, 512 * t:512 * t + 512],
                                                        start=t == 0, stop=t == KC - 1, skip_group_check=True)
                                    else:
                                        c = 2048 * t + 512 * b
                                        ins = nt.matmul(ps[64 * e:64 * e + 64, b, :], xgT[:, 2 * u + t, 64 * e:64 * e + 64], w[:, c:c + 512],
                                                        start=False, stop=u == 3 and t == 1, skip_group_check=True)
                        ins.then_inc(used, 2)
                    pe.wait_ge(p_ready, g + 2)
                    pe.wait_ge(acc_a, it + 1)
                    gather(pe)
                    pe.wait_ge(xg_kept, g + 2)
                    pe.wait_ge(pg_ready, it + 1)
                    for i in range(NT):
                        ins = nt.transpose(ps[:, A0, i * 128:i * 128 + 128], Pg[:, i, :], ident)
                    ins.then_inc(gatesT, 1)
                    pe.wait_ge(hid_ready, it + 2)
                    pe.wait_ge(acc_c, it + 1)
                    for t in range(FT):
                        ins = nt.transpose(ps[:, C0 + t // 4, (t % 4) * 128:(t % 4) * 128 + 128], hid[:, t, :], ident)
                    ins.then_inc(hid_tr, 1)
                    pe.wait_ge(hid_kept, it + 1)
                    for u in range((per_pair - UP) // 2):
                        j = UP + 2 * u
                        arrived(j)
                        arrived(j + 1)
                        for t in range(4):
                            for h in range(2):
                                for e in range(2):
                                    w = ring[:, (base + j + e) % RING, :]
                                    c = 1024 * t + 512 * h
                                    ins = nt.matmul(ps[64 * e:64 * e + 64, C0 + h, :], hidT[:, 4 * u + t, 64 * e:64 * e + 64], w[:, c:c + 512],
                                                    start=u == 0 and t == 0, stop=4 * u + t == FT - 1, skip_group_check=True)
                        ins.then_inc(used, 2)
                    pe.wait_ge(y_act, it + 1)
                    pe.wait_ge(y_dve, it + 1)
                    pe.wait_ge(gt_kept, it + 1)
                    for i in range(NT):
                        for h in range(2):
                            ins = nt.matmul(ps[:, (A0, C0)[i] + h, :], GT[:, i, :], y[:, 512 * h:512 * h + 512], start=True, stop=True)
                        ins.then_inc(scat, 1)

                def act_start(a, it, g):
                    a.wait_ge(gathered, g + 1)
                    gather_kept(a)

                def act_pair(a, it, g):
                    na = nc.scalar
                    if first:
                        a.wait_ge(used, up_used(it, 2))
                        na.activation(sg[:], ps[:, 0, :], ACT.Silu).then_inc(act1, 1)
                    else:
                        a.wait_ge(clip, it + 1)
                        na.activation(sg[:], gm[:], ACT.Sigmoid, scale=1.702).then_inc(act1, 1)
                    a.wait_ge(gathered, g + 2)
                    gather_kept(a)
                    a.wait_ge(hid_tr, it + 1)
                    for b in range(FT // 4):
                        ins = na.activation(hidT[:, 4 * b:4 * b + 4, :].rearrange("p t c -> p (t c)"), ps[:, C0 + b, :], ACT.Copy)
                    ins.then_inc(hid_kept, 1)
                    a.wait_ge(used, up_used(it, per_pair))
                    na.activation(y[:, 0:512], ps[:, C0, :], ACT.Copy).then_inc(y_act, 1)

                def dve_credit(v):
                    v.sem_inc(hid_ready, 1)
                    v.sem_inc(acc_a, 1)
                    v.sem_inc(acc_c, 1)

                def dve_pick(v, p2):
                    if not first:
                        nc.vector.tensor_copy(pick[:].rearrange("p (e c) -> p e c", e=2),
                                              bc(K("ident", 32)[:, p2].rearrange("p (e c) -> p e c", c=1), [32, 2, 64])).then_inc(pick_ready, 1)

                def dve_start(v, it, g):
                    if pre:
                        v.wait_ge(acc_c, it + 1)
                    onehot(v, Pm, slice(0, 2)).then_inc(p_ready, 1)
                    dve_pick(v, slice(0, 2))

                def dve_pair(v, link, it, g, p):
                    nv = nc.vector
                    e_now = v.snap(2 * p)
                    e_next = v.snap(2 * p + 2)
                    v.wait_ge(gathered, g + 1)
                    onehot(v, Pm, bass.ds(e_next, 2)).then_inc(p_ready, 1)
                    v.wait_ge(gatesT, it + 1)
                    onehot(v, Pg, bass.ds(e_now, 2)).then_inc(s("eq"), 1)
                    v.wait_ge(s("eq"), 1)
                    v.sem_clear(s("eq"))
                    for i in range(NT):
                        pv = Pg[:, i, :].rearrange("p (e c) -> p e c", e=2)
                        ins = nv.tensor_tensor(pv, pv, bc(comb[:, i, bass.ds(e_now, 2)].rearrange("p (e c) -> p e c", c=1), [128, 2, 64]), ALU.mult)
                    ins.then_inc(pg_ready, 1)
                    hv = hid[:].rearrange("q t p -> q p t")
                    if first:
                        v.wait_ge(act1, it + 1)
                        v.wait_ge(used, up_used(it, 4))
                        nv.tensor_tensor(hv, sg[:].rearrange("q (p t) -> q p t", t=FT), ps[:, 1, :].rearrange("q (p t) -> q p t", t=FT),
                                         ALU.mult).then_inc(hid_ready, 1)
                    else:
                        v.wait_ge(used, up_used(it, 8))
                        nv.tensor_scalar(gm[:], ps[:, 0:2, :].rearrange("p b c -> p (b c)"), 7.0, None, ALU.min).then_inc(clip, 1)
                        dve_pick(v, bass.ds(e_next, 2))
                        nv.tensor_scalar(um[:], ps[:, 2:4, :].rearrange("p b c -> p (b c)"), 7.0, -7.0, ALU.min, ALU.max)
                        v.wait_ge(act1, it + 1)
                        nv.tensor_tensor(gm[:], gm[:], sg[:], ALU.mult).then_inc(s("glu"), 1)
                        v.wait_ge(s("glu"), 1)
                        v.sem_clear(s("glu"))
                        nv.scalar_tensor_tensor(out=hv, in0=um[:].rearrange("q (p t) -> q p t", t=FT), scalar=1.0,
                                                in1=gm[:].rearrange("q (p t) -> q p t", t=FT), op0=ALU.add, op1=ALU.mult).then_inc(hid_ready, 1)
                    v.wait_ge(gatesT, it + 2)
                    nv.tensor_copy(GT[:].rearrange("p i c -> p (i c)"), ps[:, A0, 0:256]).then_inc(gt_kept, 1)
                    v.wait_ge(used, up_used(it, per_pair))
                    nv.tensor_copy(y[:, 512:1024], ps[:, C0 + 1, :]).then_inc(y_dve, 1)
                    for i, (b, sm_) in enumerate(((A0, acc_a), (C0, acc_c))):
                        v.wait_ge(scat, it * 2 + (i + 1))
                        nv.tensor_tensor(acc[:, i, :], acc[:, i, :], ps[:, b:b + 2, :].rearrange("p b c -> p (b c)"), ALU.add).then_inc(sm_, 1)

                return pe_credit, pe_start, pe_pair, act_start, act_pair, dve_credit, dve_start, dve_pair

            n6 = per_pair // RING
            main = rounds("", units_used, lambda it, j: it * (16 * n6) + 16 * ((base + j) // RING + 1), ring_ready, base)
            o_used = s("more_used")
            o_ready = [s(f"more_ready{j}") for j in range(RING)]
            more = rounds("more_", o_used, lambda it, j: it * (16 * n6) + 16 * (j // RING + 1), o_ready, RING)
            full_used = base + per_pair * PAIRS

            def pairs(eng, body):
                with eng.Fori(0, PAIRS) as p:
                    body(p)

            def more_rounds(eng, credit, start, body, flag_wait=True):
                most = eng.value_load(cnt[0:1, 0:1], min_val=0, max_val=T)
                with eng.If(most > CAP):
                    credit()
                    with eng.Fori(0, ROUNDS - 1) as r:
                        start(r)
                        if body is not None:
                            with eng.Fori(0, PAIRS) as p:
                                body(eng.snap(r * PAIRS + p), eng.snap(r * (PAIRS + 1) + p), p)

            with nc.Block() as block:
                @block.sync
                def _(sp):
                    def load(sem_ready, sem_used, k_used, e0, j):
                        e0 = sp.snap(e0)
                        sp.wait_ge(sem_used, k_used)
                        sp.dma_start(ring[:, (base + j) % RING, :], w_src(e0, j)).then_inc(sem_ready[(base + j) % RING], 16)
                    with sp.Fori(0, PAIRS - 1) as p:
                        for j in range(RING, per_pair):
                            load(ring_ready, units_used, sp.snap(p * per_pair + (base + j - RING + 1)), 2 * p, j)
                        for j in range(RING):
                            load(ring_ready, units_used, sp.snap(p * per_pair + (base + per_pair + j - RING + 1)), 2 * p + 2, j)
                    for j in range(RING, per_pair):
                        k = base + (PAIRS - 1) * per_pair + j
                        sp.wait_ge(units_used, k - RING + 1)
                        sp.dma_start(ring[:, k % RING, :], w_src(2 * PAIRS - 2, j)).then_inc(ring_ready[k % RING], 16)
                    sp.wait_ge(units_used, full_used)
                    most = sp.value_load(cnt[0:1, 0:1], min_val=0, max_val=T)
                    with sp.If(most > CAP):
                        with sp.Fori(0, ROUNDS - 1) as r:
                            with sp.Fori(0, PAIRS) as p:
                                for j in range(per_pair):
                                    load(o_ready, o_used, sp.snap(r * (PAIRS * per_pair) + p * per_pair + (j + 1)), 2 * p, j)
                        for j in range(RING):
                            sp.wait_ge(o_used, RING + (ROUNDS - 1) * PAIRS * per_pair)
                    after(sp)

                @block.tensor
                def _(pe):
                    credit, start, pair = main[0:3]
                    credit(pe)
                    start(pe, 0, 0)
                    pairs(pe, lambda p: pair(pe, p, p))
                    credit_, start_, pair_ = more[0:3]

                    def credit_more():
                        pe.wait_ge(units_used, full_used)
                        credit_(pe)
                        pe.sem_inc(o_used, RING)
                    more_rounds(pe, credit_more, lambda r: start_(pe, pe.snap(r * PAIRS), pe.snap(r * (PAIRS + 1))),
                                lambda it, g, p: pair_(pe, it, g))

                @block.scalar
                def _(a):
                    main[3](a, 0, 0)
                    pairs(a, lambda p: main[4](a, p, p))
                    more_rounds(a, lambda: None, lambda r: more[3](a, r * PAIRS, a.snap(r * (PAIRS + 1))),
                                lambda it, g, p: more[4](a, it, g))

                @block.vector
                def _(v):
                    link = None
                    main[5](v)
                    main[6](v, 0, 0)
                    pairs(v, lambda p: main[7](v, link, p, p, p))
                    lv = chain(v, "v_chain")

                    def next_round(r):
                        v.wait_ge(S(tag + "more_added_tile1"), v.snap(r * PAIRS + 1))
                        nc.vector.tensor_scalar(posx[:], posx[:], -float(CAP), None, ALU.add).then_inc(S(tag + "round_set"), 1)
                        v.wait_ge(S(tag + "round_set"), r + 1)
                        more[6](v, v.snap(r * PAIRS), v.snap(r * (PAIRS + 1)))
                    more_rounds(v, lambda: more[5](v), next_round, lambda it, g, p: more[7](v, link, it, g, p))
            return m, acc

        n1 = Norm("n1")
        n1.gains = 2

        def after1(sp):
            for k in range(K_ADA, K_ADA + RING):
                load_unit(sp, k)
        m, _ = mixture("m1_", K_MOE1, 6, moe1_src, "w_rtr", "b_rtr", 2, True, n1, after1, True)
        m.close()
        retire_semaphores()
        p2 = ExitStack()
        mod = sbuf(p2, "mod", [128, 6 * D])
        p2b = ExitStack()
        SV = sbuf(p2b, "SV", [57, 128])
        ldr = sbuf(p2b, "ldr", [48, 2])
        VT = sbuf(p2b, "VT", [128, 57])
        lqk = sbuf(p2b, "lqk", [128, 4, 64])
        Bn = sbuf(p2b, "Bn", [128, 2, 16, 16])
        Cn = sbuf(p2b, "Cn", [128, 2, 4, 64])
        cv = sbuf(p2b, "cv", [128, KC])
        cwide = hnf[:, 0:1024].rearrange("p (t c) -> p t c", t=KC)
        f_in, f_c, f_cw, f_ada, f_adak, f_sv, f_ld = (S("mod_in"), S("cond_activated"), S("cond_wide"), S("mod_done"), S("mod_kept"),
                                                S("short_in"), S("dt_spread"))
        nf = Norm("nf")
        nA = Norm("nA", shift=mod[:, 0:D])
        nA.gains = 4
        x3_done, gain_ready = S("x3"), S("gain_ready")
        with nc.Block() as block:
            @block.sync
            def _(sp):
                for k in range(K_ADA + RING, K_IN2 + RING):
                    load_unit(sp, k)

            @block.scalar
            def _(a):
                a.dma_start(grow[:], A["final_norm"].rearrange("(a d) -> a d", a=1).to_broadcast([128, D])).then_inc(s_grow, 16)
                a.dma_start(cv[:], A["c_2"][0].rearrange("(p t) -> p t", t=KC)).then_inc(f_in, 16)
                a.dma_start(mod[:], A["b_ada_2"].to_broadcast([128, 6 * D])).then_inc(f_in, 16)
                for r0, n, ap in ((0, 16, A["ssm_a_re_2"][0].rearrange("(j g) p -> j (g p)", j=16)),
                                  (16, 16, A["ssm_a_im_2"][0].rearrange("(j g) p -> j (g p)", j=16)),
                                  (48, 4, A["ssm_d_2"][0].rearrange("(j c) -> j c", j=4)),
                                  (52, 4, A["b_glu_2"][0].rearrange("(j c) -> j c", j=4)),
                                  (56, 1, A["subln_g_2"])):
                    a.dma_start(SV[r0:r0 + n, :], ap).then_inc(f_sv, 16)
                a.dma_start(ldr[32:48, :], A["ssm_log_dt_2"][0].rearrange("(j g) -> j g", j=16)).then_inc(f_sv, 16)
                for i, n in enumerate(("lq1_2", "lk1_2", "lq2_2", "lk2_2")):
                    a.dma_start(lqk[:, i, :], A[n].to_broadcast([128, 64])).then_inc(f_sv, 16)
                for i, n in enumerate(("ssm_b_re_2", "ssm_b_im_2")):
                    a.dma_start(Bn[:, i], A[n][0].rearrange("(j g) p c -> (g p) j c", j=16)).then_inc(f_sv, 16)
                for i, n in enumerate(("ssm_c_re_2", "ssm_c_im_2")):
                    a.dma_start(Cn[:, i], A[n][0].rearrange("(j g) c p -> (g c) j p", j=4)).then_inc(f_sv, 16)
                a.wait_ge(f_in, 32)
                nc.scalar.activation(cv[:], cv[:], ACT.Silu).then_inc(f_c, 1)
                nf.act_root(a)
                a.wait_ge(x3_done, 2)
                a.dma_start(grow[:], A["norm1_g_2"].to_broadcast([128, D])).then_inc(s_grow, 16)

            @block.vector
            def _(v):
                link = chain(v, "v_chain")
                nv = nc.vector
                v.wait_ge(f_c, 1)
                nv.tensor_copy(cwide, bc(cv[:].rearrange("p (t c) -> p t c", c=1), [128, KC, 128])).then_inc(f_cw, 1)
                v.wait_ge(s_grow, 48)
                nf.dve_stats(v, link)
                for i in range(NT):
                    nv.scalar_tensor_tensor(out=X[:, i, :], in0=X[:, i, :], scalar=st[:, 4 + i:5 + i], in1=grow[:],
                                            op0=ALU.mult, op1=ALU.mult).then_inc(x3_done, 1)
                v.wait_ge(f_sv, 16 * 14)
                nv.tensor_copy(SV[32:48, :].rearrange("j (g p) -> j g p", g=2),
                               bc(ldr[32:48, :].rearrange("j (g p) -> j g p", p=1), [16, 2, 64])).then_inc(f_ld, 1)
                for j in range(12):
                    v.wait_ge(f_ada, j + 1)
                    c = slice(512 * j, 512 * j + 512)
                    nv.tensor_tensor(mod[:, c], mod[:, c], ps[:, 4 + j % 4, :], ALU.add).then_inc(f_adak, 1)
                v.wait_ge(f_adak, 12)
                v.wait_ge(s_grow, 64)
                nv.scalar_tensor_tensor(out=grow[:], in0=mod[:, D:2 * D], scalar=1.0, in1=grow[:], op0=ALU.add,
                                        op1=ALU.mult).then_inc(gain_ready, 1)

            @block.tensor
            def _(pe):
                nt = nc.tensor
                pe.wait_ge(f_cw, 1)
                for j in range(12):
                    unit_arrived(pe, K_ADA + j)
                    if j >= 4:
                        pe.wait_ge(f_adak, j - 3)
                    w = unit(K_ADA + j)
                    for t in range(KC):
                        ins = nt.matmul(ps[:, 4 + j % 4, :], cwide[:, t, :], w[:, t, :], start=t == 0, stop=t == KC - 1)
                    ins.then_inc(f_ada, 1)
                    pe.wait_ge(f_ada, j + 1)
                    pe.sem_inc(units_used, 1)


        q2T = sbuf(p2b, "q2T", [128, 4, T])
        k2T = sbuf(p2b, "k2T", [128, 4, T])
        v2 = sbuf(p2b, "v2", [128, NT, 512])
        uT = sbuf(p2b, "uT", [128, 4, T])
        aT = sbuf(p2b, "aT", [128, 4, T])
        zc = sbuf(p2b, "zc", [128, 12, 16])
        lam = sbuf(p2b, "lam", [128, 8])
        BT = sbuf(p2b, "BT", [128, 2, 4, 128])
        CT = sbuf(p2b, "CT", [128, 2, 4, 128])
        Bp = junk[:].rearrange("p (k j g c) -> p k j g c", k=2, j=16, g=2)
        s2_proj, s2_pev, s2_vt, s2_vtk, s2_e, s2_ek, s2_b, s2_bt, s2_btk, s2_l, s2_lk = (
            S("proj2_done"), S("proj2_kept"), S("shortT"), S("shortT_kept"), S("lam_ready"), S("lam_acted"),
            S("bc_built"), S("bcT"), S("bcT_kept"), S("lam_dots"), S("lam_exps"))
        zr_, zi_, dec, sn, cs_, re, im, cr, ci, t1_, t2_, dt_ = (zc[:, i, :] for i in range(12))
        TWO_PI = 2 * np.pi
        with nc.Block() as block:
            @block.sync
            def _(sp):
                for k in range(K_IN2 + RING, K_IN2 + 4 + RING):
                    load_unit(sp, k)

            @block.scalar
            def _(a):
                na = nc.scalar
                nA.act(a)
                a.wait_ge(s2_vt, 1)
                na.activation(VT[:], ps[:, 4, 0:57], ACT.Copy).then_inc(s2_vtk, 1)
                a.wait_ge(s2_vtk, 1)
                na.activation(dt_, VT[:, 32:48], ACT.Exp).then_inc(s2_vtk, 1)
                a.wait_ge(s2_e, 1)
                na.activation(dec, zr_, ACT.Exp).then_inc(s2_ek, 1)
                a.wait_ge(s2_l, 1)
                na.activation(lam[:, 2:4], lam[:, 0:2], ACT.Exp).then_inc(s2_lk, 1)
                a.wait_ge(s2_e, 2)
                na.activation(sn, t1_, ACT.Sin).then_inc(s2_ek, 1)
                na.activation(cs_, t2_, ACT.Sin).then_inc(s2_ek, 1)
                for u in range(4):
                    for h in range(2):
                        n = 2 * u + h
                        a.wait_ge(s2_proj, n + 1)
                        src = ps[:, 4 + n % 4, :]
                        if u == 2:
                            ins = na.activation(v2[:, h, :], src, ACT.Copy)
                        else:
                            dst = {0: q2T, 1: k2T, 3: uT}[u]
                            ins = na.activation(dst[:, 2 * h:2 * h + 2, :].rearrange("p a b -> p (a b)"), src, ACT.Copy)
                        ins.then_inc(s2_pev, 1)
                a.wait_ge(s2_bt, 1)
                for k in range(2):
                    na.activation(BT[:, k].rearrange("p j c -> p (j c)"), ps[:, k, :], ACT.Copy).then_inc(s2_btk, 1)
                    na.activation(CT[:, k].rearrange("p j c -> p (j c)"), ps[:, 2 + k, :], ACT.Copy,
                                  scale=(1.0, -1.0)[k]).then_inc(s2_btk, 1)

            @block.vector
            def _(v):
                link = chain(v, "v_chain")
                nv = nc.vector
                nA.dve(v, link)
                v.wait_ge(s2_vtk, 2)
                link(nv.tensor_scalar(re, VT[:, 0:16], -1e-4, None, ALU.min))
                link(nv.tensor_copy(im, VT[:, 16:32]))
                link(nv.tensor_tensor(zi_, im, dt_, ALU.mult))
                nv.tensor_tensor(zr_, re, dt_, ALU.mult).then_inc(s2_e, 1)
                link(nv.tensor_scalar(t1_, zi_, 1.0 / TWO_PI, 12582912.0, ALU.mult, ALU.add))
                link(nv.tensor_scalar(t1_, t1_, -12582912.0, None, ALU.add))
                for c in (6.28125, 0.0019350051879882812, TWO_PI - 6.28125 - 0.0019350051879882812):
                    link(nv.scalar_tensor_tensor(out=zi_, in0=t1_, scalar=-c, in1=zi_, op0=ALU.mult, op1=ALU.add))
                link(nv.tensor_scalar(t1_, zi_, 3.1415925, -3.1415925, ALU.min, ALU.max))
                link(nv.tensor_scalar(t2_, t1_, -1.0, None, ALU.mult))
                link(nv.tensor_tensor(t2_, t2_, t1_, ALU.max))
                nv.tensor_scalar(t2_, t2_, -1.0, float(np.pi / 2), ALU.mult, ALU.add).then_inc(s2_e, 1)
                prod = junk[:, 0:128]
                for i in range(2):
                    ins = nv.tensor_tensor_reduce(out=prod[:, 64 * i:64 * i + 64], in0=lqk[:, 2 * i, :], in1=lqk[:, 2 * i + 1, :],
                                                  scale=1.0, scalar=0.0, op0=ALU.mult, op1=ALU.add, accum_out=lam[:, i:i + 1])
                ins.then_inc(s2_l, 1)
                v.wait_ge(s2_lk, 1)
                link(nv.tensor_tensor(lam[:, 4:5], lam[:, 3:4], lam[:, 2:3], ALU.subtract))
                link(nv.tensor_scalar(lam[:, 4:5], lam[:, 4:5], -0.2, None, ALU.add))
                link(nv.tensor_scalar(lam[:, 5:6], VT[:, 56:57], 0.8, None, ALU.mult))
                v.wait_ge(s2_ek, 3)
                link(nv.tensor_tensor(cr, dec, cs_, ALU.mult))
                link(nv.tensor_scalar(cr, cr, -1.0, None, ALU.add))
                link(nv.tensor_tensor(ci, dec, sn, ALU.mult))
                link(nv.tensor_tensor(t1_, re, re, ALU.mult))
                link(nv.tensor_tensor(t2_, im, im, ALU.mult))
                link(nv.tensor_tensor(t1_, t1_, t2_, ALU.add))
                link(nv.reciprocal(dt_, t1_))
                link(nv.tensor_tensor(t1_, cr, re, ALU.mult))
                link(nv.tensor_tensor(t2_, ci, im, ALU.mult))
                link(nv.tensor_tensor(zr_, t1_, t2_, ALU.add))
                link(nv.tensor_tensor(t1_, ci, re, ALU.mult))
                link(nv.tensor_tensor(t2_, cr, im, ALU.mult))
                link(nv.tensor_tensor(zi_, t1_, t2_, ALU.subtract))
                link(nv.tensor_tensor(zr_, zr_, dt_, ALU.mult))
                link(nv.tensor_tensor(zi_, zi_, dt_, ALU.mult))
                zrb = bc(zr_.rearrange("p (j c) -> p j c", c=1), [128, 16, 16])
                zib = bc(zi_.rearrange("p (j c) -> p j c", c=1), [128, 16, 16])
                tmp = hnf[:, 0:512].rearrange("p (k j c) -> p k j c", k=2, j=16)
                for k, (x, y_, op) in enumerate(((0, 1, ALU.subtract), (1, 0, ALU.add))):
                    nv.tensor_tensor(tmp[:, 0], Bn[:, x], zrb, ALU.mult)
                    link(nv.tensor_tensor(tmp[:, 1], Bn[:, y_], zib, ALU.mult))
                    link(nv.tensor_tensor(tmp[:, 0], tmp[:, 0], tmp[:, 1], op))
                    nv.tensor_scalar(Bp[:, k, :, 0, :], tmp[:, 0], K("even"), None, ALU.mult)
                    link(nv.tensor_scalar(Bp[:, k, :, 1, :], tmp[:, 0], K("odd"), None, ALU.mult))
                Cp = hnf[:, 1024:2048].rearrange("p (k j r) -> p k j r", k=2, j=4)
                for k in range(2):
                    nv.tensor_scalar(Cp[:, k, :, 0:64], Cn[:, k], K("geven"), None, ALU.mult)
                    ins = nv.tensor_scalar(Cp[:, k, :, 64:128], Cn[:, k], K("godd"), None, ALU.mult)
                ins.then_inc(s2_b, 1)

            @block.tensor
            def _(pe):
                nt = nc.tensor
                nt.transpose(ps[:, 4, 0:57], SV[:], K("ident", 57)[:, 0:57]).then_inc(s2_vt, 1)
                nA.pe(pe)
                pe.wait_ge(nA.ev, 4)
                pe.wait_ge(s2_vtk, 1)
                for u in range(4):
                    unit_arrived(pe, K_IN2 + u)
                    w = unit(K_IN2 + u)
                    for h in range(2):
                        n = 2 * u + h
                        if n >= 4:
                            pe.wait_ge(s2_pev, n - 3)
                        if u == 2:
                            for t in range(KC):
                                ins = nt.matmul(ps[:, 4 + n % 4, :], hT[:, t, h * 128:h * 128 + 128], w[:, t, :], start=t == 0, stop=t == KC - 1)
                        else:
                            for cb in range(2):
                                c = (2 * h + cb) * 128
                                for t in range(KC):
                                    ins = nt.matmul(ps[:, 4 + n % 4, cb * 256:cb * 256 + 256], w[:, t, c:c + 128], hT[:, t, :],
                                                    start=t == 0, stop=t == KC - 1)
                        ins.then_inc(s2_proj, 1)
                    pe.wait_ge(s2_proj, 2 * u + 2)
                    pe.sem_inc(units_used, 1)
                pe.wait_ge(s2_b, 1)
                Cp = hnf[:, 1024:2048].rearrange("p (k j r) -> p k j r", k=2, j=4)
                for k in range(2):
                    for q in range(4):
                        nt.transpose(ps[:, k, q * 128:q * 128 + 128], Bp[:, k, 4 * q:4 * q + 4].rearrange("p j g c -> p (j g c)"), ident)
                        ins = nt.transpose(ps[:, 2 + k, q * 128:q * 128 + 128], Cp[:, k, q, :], ident)
                ins.then_inc(s2_bt, 1)

        P2 = hnf.rearrange("p (s k) -> p s k", s=8)
        PT2 = hTf.rearrange("p (b h q) -> p b h q", b=2, h=8)
        w2s = sbuf(p2b, "w2s", [128, 48])
        osq2 = junk[:].rearrange("p (i c) -> p i c", i=NT)
        d_s, d_mx, d_exp, d_p, d_t, d_tk, d_o, d_sq, d_v, d_r, d_n, d_nt, d_ntk = (
            S(n) for n in ("a2_scores", "a2_max", "a2_exp", "a2_probs", "a2_probsT", "a2_probsT_kept", "a2_out", "a2_squares",
                           "a2_variance", "a2_root", "a2_normed", "a2_outT", "a2_outT_kept"))
        with nc.Block() as block:
            @block.vector
            def _(v):
                link = chain(v, "v_chain")
                nv = nc.vector
                for i in range(NT):
                    nk = 128 * (i + 1)
                    P8 = P2[:, :, 0:nk]
                    v.wait_ge(d_s, i + 1)
                    if i:
                        v.wait_ge(d_t, i)
                    src = ps[:, 2:6, :].rearrange("p b (a k) -> p (b a) k", a=2)
                    ca = K("causal").rearrange("p (a k) -> p a k", a=1)
                    link(nv.tensor_tensor(P8[:, :, nk - 128:nk], src[:, :, nk - 128:nk], bc(ca, [128, 8, 128]), ALU.add))
                    if i:
                        link(nv.tensor_copy(P8[:, :, 0:128], src[:, :, 0:128]))
                    link(nv.tensor_reduce(w2s[:, 0:8], P8, AX.X, ALU.max))
                    nv.tensor_scalar(w2s[:, 8:16], w2s[:, 0:8], -0.125, None, ALU.mult).then_inc(d_mx, 1)
                    v.wait_ge(d_exp, i + 1)
                    w8 = w2s[:, 16:24]
                    link(nv.reciprocal(w8, w8))
                    link(nv.tensor_scalar(w2s[:, 20:24], w2s[:, 20:24], lam[:, 4:5], None, ALU.mult))
                    link(nv.tensor_tensor(P8, P8, bc(w8.rearrange("p (h n) -> p h n", n=1), [128, 8, nk]), ALU.mult))
                    nv.tensor_tensor(P2[:, 0:4, 0:nk], P2[:, 0:4, 0:nk], P2[:, 4:8, 0:nk], ALU.add).then_inc(d_p, 1)
                v.wait_ge(d_sq, 2)
                link(nv.tensor_reduce(w2s[:, 24:32], osq2.rearrange("p i (h c) -> p (i h) c", h=4), AX.X, ALU.add))
                nv.tensor_scalar(w2s[:, 32:40], w2s[:, 24:32], 1.0 / 128, EPS, ALU.mult, ALU.add).then_inc(d_v, 1)
                v.wait_ge(d_r, 1)
                link(nv.reciprocal(w2s[:, 40:48], w2s[:, 32:40]))
                for i in range(NT):
                    r = bc(w2s[:, 40 + 4 * i:44 + 4 * i].rearrange("p (h n) -> p h n", n=1), [128, 4, 128])
                    nv.tensor_tensor(osq2[:, i].rearrange("p (h c) -> p h c", h=4), ps[:, 6 + i, :].rearrange("p (h c) -> p h c", h=4),
                                     r, ALU.mult).then_inc(d_n, 1)

            @block.scalar
            def _(a):
                na = nc.scalar
                for i in range(NT):
                    nk = 128 * (i + 1)
                    a.wait_ge(d_mx, i + 1)
                    for h in range(8):
                        ins = na.activation(P2[:, h, 0:nk], P2[:, h, 0:nk], ACT.Exp, bias=w2s[:, 8 + h:9 + h], scale=0.125,
                                            accum_out=w2s[:, 16 + h:17 + h])
                    ins.then_inc(d_exp, 1)
                    a.wait_ge(d_t, i + 1)
                    if i:
                        a.wait_ge(d_o, i)
                    for kb in range(i + 1):
                        na.activation(PT2[:, kb, 0:4], ps[:, 2 + kb, :].rearrange("p (c q) -> p c q", c=4), ACT.Copy).then_inc(d_tk, 1)
                for i in range(NT):
                    a.wait_ge(d_o, i + 1)
                    na.activation(osq2[:, i], ps[:, 6 + i, :], ACT.Square).then_inc(d_sq, 1)
                a.wait_ge(d_v, 1)
                na.activation(w2s[:, 32:40], w2s[:, 32:40], ACT.Sqrt).then_inc(d_r, 1)
                a.wait_ge(d_nt, 1)
                for b in range(2):
                    na.activation(aT[:, 2 * b:2 * b + 2], ps[:, b, :].rearrange("p (a q) -> p a q", a=2), ACT.Copy,
                                  scale=lam[:, 5:6]).then_inc(d_ntk, 1)

            @block.tensor
            def _(pe):
                nt = nc.tensor
                for i in range(NT):
                    if i:
                        pe.wait_ge(d_tk, 1)
                    for h in range(4):
                        for m_ in range(2):
                            r = 64 * m_
                            for kb in range(i + 1):
                                c = (h % 2) * 256 + kb * 128
                                ins = nt.matmul(ps[:, 2 + 2 * m_ + h // 2, c:c + 128], q2T[r:r + 64, h, i * 128:i * 128 + 128],
                                                k2T[r:r + 64, h, kb * 128:kb * 128 + 128], start=True, stop=True)
                    ins.then_inc(d_s, 1)
                    pe.wait_ge(d_p, i + 1)
                    for kb in range(i + 1):
                        for h in range(4):
                            ins = nt.transpose(ps[:, 2 + kb, h * 128:h * 128 + 128], P2[:, h, kb * 128:kb * 128 + 128], ident)
                    ins.then_inc(d_t, 1)
                    pe.wait_ge(d_tk, [1, 3][i])
                    for h in range(4):
                        for kb in range(i + 1):
                            ins = nt.matmul(ps[:, 6 + i, h * 128:h * 128 + 128], PT2[:, kb, h, :], v2[:, kb, h * 128:h * 128 + 128],
                                            start=kb == 0, stop=kb == i)
                    ins.then_inc(d_o, 1)
                pe.wait_ge(d_n, 2)
                for i in range(NT):
                    for h in range(4):
                        ins = nt.transpose(ps[:, h // 2, (h % 2) * 256 + i * 128:(h % 2) * 256 + i * 128 + 128],
                                           osq2[:, i, h * 128:h * 128 + 128], ident)
                ins.then_inc(d_nt, 1)

        Wp = sbuf(p2b, "Wp", [128, 2, 4, T])
        sq_ = sbuf(p2b, "sq_", [128, 3, 16])
        w4 = k2T[:, 0:2, :]
        Z = [hnf[:, 0:1024], hnf[:, 1024:2048]]
        Y1, Y2 = hTf[:, 0:1024], hTf[:, 1024:2048]
        xs = [hTf[:, 0:1024], junk[:]]
        dk = grow[:]
        zT = q2T
        e_h = S("ssm_input_half")
        e_bu, e_x, e_y, e_y1, e_sg, e_z = (S(n) for n in ("ssm_input", "ssm_states", "ssm_out", "ssm_gelu_arg", "ssm_gelu_sig", "ssm_gelu"))
        with nc.Block() as block:
            @block.tensor
            def _(pe):
                nt = nc.tensor
                for q in range(4):
                    if q:
                        pe.wait_ge(e_x, q)
                    for jj in (0, 2, 1, 3):
                        if jj == 1:
                            ins.then_inc(e_h, 1)
                            pe.wait_ge(e_h, q + 1)
                        for k in range(2):
                            r = 32 * jj
                            ins = nt.matmul(ps[:, 2 * k + jj // 2, (jj % 2) * 256:(jj % 2) * 256 + 256], BT[r:r + 32, k, q, :], uT[r:r + 32, q, :],
                                            start=True, stop=True, tile_position=(r, 0))
                    ins.then_inc(e_bu, 1)
                    pe.wait_ge(e_x, q + 1)
                    for jj in range(4):
                        for k in range(2):
                            ins = nt.matmul(ps[32 * jj:32 * jj + 32, 4 + q % 2, 0:256], CT[:, k, q, 32 * jj:32 * jj + 32],
                                            xs[k][:, jj * 256:jj * 256 + 256], start=k == 0, stop=k == 1, tile_position=(0, 32 * jj))
                    ins.then_inc(e_y, 1)

            @block.scalar
            def _(a):
                for q in range(4):
                    a.wait_ge(e_y1, q + 1)
                    nc.scalar.activation(w4[:, 1], w4[:, 1], ACT.Sigmoid, scale=1.5957691216057308).then_inc(e_sg, 1)

            @block.vector
            def _(v):
                link = chain(v, "v_chain")
                nv = nc.vector
                for q in range(4):
                    j4 = slice(4 * q, 4 * q + 4)

                    def col(ap, n):
                        return bc(ap.rearrange("p (j n) -> p j n", n=1), [128, 4, n])
                    link(nv.memset(Wp[:, 0, :, 0:1], 1.0))
                    link(nv.memset(Wp[:, 1, :, 0:1], 0.0))
                    wr_, wi_ = sq_[:, 0, 0:4], sq_[:, 1, 0:4]
                    link(nv.tensor_copy(wr_, cs_[:, j4]))
                    link(nv.tensor_copy(wi_, sn[:, j4]))
                    n = 1
                    while n < T:
                        a_r, a_i = Wp[:, 0, :, 0:n], Wp[:, 1, :, 0:n]
                        o_r, o_i = Wp[:, 0, :, n:2 * n], Wp[:, 1, :, n:2 * n]
                        t_ = [Z[0][:, 0:4 * n].rearrange("p (j t) -> p j t", j=4), Z[1][:, 0:4 * n].rearrange("p (j t) -> p j t", j=4)]
                        nv.tensor_tensor(o_r, a_r, col(wr_, n), ALU.mult)
                        nv.tensor_tensor(t_[0], a_i, col(wi_, n), ALU.mult)
                        nv.tensor_tensor(o_i, a_r, col(wi_, n), ALU.mult)
                        link(nv.tensor_tensor(t_[1], a_i, col(wr_, n), ALU.mult))
                        nv.tensor_tensor(o_r, o_r, t_[0], ALU.subtract)
                        link(nv.tensor_tensor(o_i, o_i, t_[1], ALU.add))
                        n *= 2
                        if n < T:
                            x_, y_, w_ = sq_[:, 2, 0:4], sq_[:, 2, 4:8], sq_[:, 2, 8:12]
                            nv.tensor_tensor(x_, wr_, wr_, ALU.mult)
                            nv.tensor_tensor(y_, wi_, wi_, ALU.mult)
                            link(nv.tensor_tensor(w_, wr_, wi_, ALU.mult))
                            link(nv.tensor_tensor(wr_, x_, y_, ALU.subtract))
                            link(nv.tensor_tensor(wi_, w_, w_, ALU.add))
                    W_r, W_i = Wp[:, 0].rearrange("p j t -> p (j t)"), Wp[:, 1].rearrange("p j t -> p (j t)")
                    link(nv.tensor_copy(dk.rearrange("p (j t) -> p j t", j=4), col(dec[:, j4], 256)))
                    v.wait_ge(e_bu, q + 1)
                    if q:
                        v.wait_ge(e_y, q)
                    b_r = ps[:, 0:2, :].rearrange("p b c -> p (b c)")
                    b_i = ps[:, 2:4, :].rearrange("p b c -> p (b c)")
                    nv.tensor_tensor(Y1, b_r, W_r, ALU.mult)
                    nv.tensor_tensor(Z[0], b_i, W_i, ALU.mult)
                    nv.tensor_tensor(Y2, b_i, W_r, ALU.mult)
                    link(nv.tensor_tensor(Z[1], b_r, W_i, ALU.mult))
                    nv.tensor_tensor(Y1, Y1, Z[0], ALU.add)
                    link(nv.tensor_tensor(Y2, Y2, Z[1], ALU.subtract))
                    for jj in range(4):
                        c = slice(256 * jj, 256 * jj + 256)
                        nv.tensor_tensor_scan(Z[0][:, c], dk[:, c], Y1[:, c], 0.0, ALU.mult, ALU.add)
                        ins = nv.tensor_tensor_scan(Z[1][:, c], dk[:, c], Y2[:, c], 0.0, ALU.mult, ALU.add)
                    link(ins)
                    nv.tensor_tensor(xs[0], Z[0], W_r, ALU.mult)
                    nv.tensor_tensor(Y2, Z[1], W_i, ALU.mult)
                    nv.tensor_tensor(xs[1], Z[0], W_i, ALU.mult)
                    link(nv.tensor_tensor(Z[1], Z[1], W_r, ALU.mult))
                    nv.tensor_tensor(xs[0], xs[0], Y2, ALU.subtract)
                    nv.tensor_tensor(xs[1], xs[1], Z[1], ALU.add).then_inc(e_x, 1)
                    v.wait_ge(e_y, q + 1)
                    yq = w4[:, 0]
                    link(nv.scalar_tensor_tensor(out=yq, in0=uT[:, q, :], scalar=VT[:, 48 + q:49 + q], in1=ps[:, 4 + q % 2, 0:256],
                                                 op0=ALU.mult, op1=ALU.add))
                    link(nv.tensor_tensor(w4[:, 1], yq, yq, ALU.mult))
                    link(nv.tensor_scalar(w4[:, 1], w4[:, 1], 0.044715, 1.0, ALU.mult, ALU.add))
                    nv.tensor_tensor(w4[:, 1], w4[:, 1], yq, ALU.mult).then_inc(e_y1, 1)
                    v.wait_ge(e_sg, q + 1)
                    nv.tensor_tensor(zT[:, q, :], yq, w4[:, 1], ALU.mult).then_inc(e_z, 1)

        g_p, g_s, g_m, g_o, g_k = (S(n) for n in ("glu_done", "glu_sig", "ssm_gated", "mix_done", "gain2_set"))
        ssT = k2T
        with nc.Block() as block:
            @block.sync
            def _(sp):
                for k in range(K_IN2 + 4 + RING, K_MOE2 + RING):
                    load_unit(sp, k)

            @block.tensor
            def _(pe):
                nt = nc.tensor
                unit_arrived(pe, K_GLU)
                w = unit(K_GLU)
                for b in range(2):
                    for cb in range(2):
                        for c in range(4):
                            col_ = (2 * b + cb) * 128
                            ins = nt.matmul(ps[:, b, cb * 256:cb * 256 + 256], w[:, c, col_:col_ + 128], zT[:, c, :], start=c == 0, stop=c == 3)
                    ins.then_inc(g_p, 1)
                pe.wait_ge(g_p, 2)
                pe.sem_inc(units_used, 1)
                for k, src in enumerate((aT, ssT)):
                    unit_arrived(pe, K_OUT2 + k)
                    if k:
                        pe.wait_ge(g_m, 1)
                    for i in range(NT):
                        for h in range(2):
                            for c in range(4):
                                ins = nt.matmul(ps[:, 4 + 2 * i + h, :], src[:, c, i * 128:i * 128 + 128],
                                                unit(K_OUT2 + k)[:, c, h * 512:h * 512 + 512], start=k == 0 and c == 0, stop=k == 1 and c == 3)
                    ins.then_inc(g_o, 1)
                pe.wait_ge(g_o, 2)
                pe.sem_inc(units_used, 2)

            @block.scalar
            def _(a):
                a.dma_start(grow[:], A["norm2_g_2"].to_broadcast([128, D])).then_inc(s_grow, 16)
                for c in range(4):
                    a.wait_ge(g_p, c // 2 + 1)
                    nc.scalar.activation(ssT[:, c, :], ps[:, c // 2, (c % 2) * 256:(c % 2) * 256 + 256], ACT.Sigmoid,
                                         bias=VT[:, 52 + c:53 + c]).then_inc(g_s, 1)

            @block.vector
            def _(v):
                link = chain(v, "v_chain")
                nv = nc.vector
                v.wait_ge(g_s, 4)
                nv.tensor_tensor(ssT[:], ssT[:], zT[:], ALU.mult).then_inc(g_m, 1)
                v.wait_ge(g_o, 2)
                for i in range(NT):
                    link(nv.tensor_tensor(junk[:], ps[:, 4 + 2 * i:6 + 2 * i, :].rearrange("p b c -> p (b c)"), mod[:, 2 * D:3 * D], ALU.mult))
                    link(nv.tensor_tensor(X[:, i, :], X[:, i, :], junk[:], ALU.add))
                v.wait_ge(s_grow, 80)
                nv.scalar_tensor_tensor(out=grow[:], in0=mod[:, 4 * D:5 * D], scalar=1.0, in1=grow[:], op0=ALU.add,
                                        op1=ALU.mult).then_inc(g_k, 1)
        p2b.close()
        retire_semaphores()
        n3 = Norm("n3", shift=mod[:, 3 * D:4 * D])
        n3.gains = 5
        m, acc = mixture("m2_", K_MOE2, 12, moe2_src, "w_router_2", "b_router_2", 4, False, n3, lambda sp: None, False)
        nz = Norm("nz")
        z_x, z_o = S("normed_out"), S("out_done")
        with nc.Block() as block:
            @block.scalar
            def _(a):
                a.dma_start(grow[:], A["final_g_2"].rearrange("(a d) -> a d", a=1).to_broadcast([128, D])).then_inc(s_grow, 16)
                nz.act_root(a)

            @block.vector
            def _(v):
                link = chain(v, "v_chain")
                nv = nc.vector
                for i in range(NT):
                    link(nv.tensor_tensor(acc[:, i, :], acc[:, i, :], mod[:, 5 * D:6 * D], ALU.mult))
                    link(nv.tensor_tensor(X[:, i, :], X[:, i, :], acc[:, i, :], ALU.add))
                nz.dve_stats(v, link)
                v.wait_ge(s_grow, 96)
                for i in range(NT):
                    nv.scalar_tensor_tensor(out=X[:, i, :], in0=X[:, i, :], scalar=st[:, 4 + i:5 + i], in1=grow[:],
                                            op0=ALU.mult, op1=ALU.mult).then_inc(z_x, 1)

            @block.sync
            def _(sp):
                for i in range(NT):
                    sp.wait_ge(z_x, i + 1)
                    sp.dma_start(out[0, i * 128:i * 128 + 128, :], X[:, i, :]).then_inc(z_o, 16)
                sp.wait_ge(z_o, 32)
        m.close()
        p2.close()


def kernel(**inputs):
    import numpy as _np
    import concourse.bacc as _bacc
    from concourse import mybir as _mybir
    from concourse.bass_utils import run_bass_kernel_spmd as _run

    nc = _bacc.Bacc("TRN2", target_bir_lowering=False, num_devices=1)
    arrays, args = {}, {}
    for name, a in list(inputs.items()) + [("cst", constants())]:
        a = _np.ascontiguousarray(a)
        arrays[f"in_{name}_dram"] = a
        args[name] = nc.dram_tensor(f"in_{name}_dram", a.shape, _mybir.dt.from_np(a.dtype), kind="ExternalInput").ap()
    out = nc.dram_tensor("out_0_dram", (1, T, D), _mybir.dt.float32, kind="ExternalOutput").ap()
    bass_block_pair(nc, args, out)
    r = _run(nc, [arrays], core_ids=[0])
    return r.results[0]["out_0_dram"]
```

```python
import numpy as np
import concourse.bass as bass
from concourse import mybir
from contextlib import ExitStack

F32 = mybir.dt.float32
I32 = mybir.dt.int32
ALU = mybir.AluOpType
ACT = mybir.ActivationFunctionType
AX = mybir.AxisListType

T, D = 256, 1024
NT = T // 128
KC = D // 128
EPS = 1e-6
NEG = -1e30
IN_COLS = 5400
C_KV, C_GATE, C_HQ, C_HF, C_HI, C_HG, C_MRG = 512, 1280, 1304, 1816, 2328, 2840, 3352
NCMP = 15
NE = 32
CAP = 64
ROUNDS = T // CAP
PAIRS = NE // 2
RING = 6
UNIT = 4096
LEVELS = 7

WIDTHS = [("ident", 128), ("ones", 128), ("iota", 128), ("before", 128), ("causal", 128),
          ("cos", NT * 8), ("sin", NT * 8), ("ccos", 8), ("csin", 8),
          ("cadd", NT * 16), ("cmul", NT * 16), ("tie8", 64), ("tie4", 16),
          ("even", 1), ("odd", 1), ("geven", 1), ("godd", 1),
          ("lvl", LEVELS * 128), ("tie32", 1024)]
CO = {}
NCST = 0
for _n, _w in WIDTHS:
    CO[_n] = (NCST, _w)
    NCST += _w


def constants():
    c = np.zeros((128, NCST), np.float32)

    def put(name, a):
        o, w = CO[name]
        c[:, o:o + w] = np.broadcast_to(np.asarray(a, np.float32).reshape(-1, w), (128, w))

    p = np.arange(128)
    put("ident", np.eye(128))
    put("ones", np.ones((128, 128)))
    s = np.arange(128) % 64
    put("iota", s)
    put("before", p[:, None] < p[None, :])
    put("causal", np.where(p[None, :] <= p[:, None], 0.0, NEG))
    lv = []
    for l in range(LEVELS):
        half, blk = 1 << l, 2 << l
        s_, t_ = p[:, None], p[None, :]
        lv.append((s_ // blk == t_ // blk) & (s_ % blk < half) & (t_ % blk >= half))
    put("lvl", np.stack(lv, 1).reshape(128, -1))
    inv = (np.float32(500000.0) ** (-np.arange(8, dtype=np.float32) / 8)).astype(np.float32)
    pos = np.arange(T, dtype=np.float32)
    ang = (pos[:, None] * inv[None, :]).reshape(NT, 128, 8).transpose(1, 0, 2)
    put("cos", np.cos(ang).reshape(128, -1))
    put("sin", np.sin(ang).reshape(128, -1))
    cang = ((p % 32) * 16).astype(np.float32)[:, None] * inv[None, :]
    put("ccos", np.cos(cang))
    put("csin", np.sin(cang))
    tp = np.arange(T).reshape(NT, 128).T
    ok = (np.arange(16)[None, None, :] * 16 + 31 <= tp[:, :, None])
    put("cadd", np.where(ok, 0.0, NEG).reshape(128, -1))
    put("cmul", ok.reshape(128, -1))
    for n in (32, 8, 4):
        i = np.arange(n)
        put(f"tie{n}", (i[None, :] < i[:, None]).reshape(-1))
    put("even", (p < 64)[:, None])
    put("odd", (p >= 64)[:, None])
    put("geven", ((p // 16) % 2 == 0)[:, None])
    put("godd", ((p // 16) % 2 == 1)[:, None])
    return c


def bass_block_pair(nc, A, out):
    top = ExitStack()
    with top:
        def sbuf(ctx, name, shape, dt=F32):
            return ctx.enter_context(nc.sbuf_tensor(name, shape, dt))

        sems = {}
        cleared = []
        LASTING = {"units_used", "gain_in", "v_chain"} | {f"ring_ready{j}" for j in range(RING)}

        def S(name):
            if name not in sems:
                sems[name] = cleared.pop() if cleared else top.enter_context(nc.semaphore(name))
            return sems[name]

        def finished():
            return [n for n in sems if n not in LASTING]

        def clear(g, names):
            for n in names:
                g.sem_clear(sems[n])

        def retire(names):
            for n in names:
                cleared.append(sems.pop(n))

        CS = sbuf(top, "CS", [128, CO["lvl"][0]])
        ring = sbuf(top, "ring", [128, RING, UNIT])
        X = sbuf(top, "X", [128, NT, D])
        hn = sbuf(top, "hn", [128, NT, KC, 128])
        hT = sbuf(top, "hT", [128, KC, T])
        grow = sbuf(top, "grow", [128, D])
        st = sbuf(top, "st", [128, 8])
        junk = sbuf(top, "junk", [128, D])
        ps = top.enter_context(nc.psum_tensor("ps", [128, 8, 512], F32))

        def K(name, parts=128):
            o, w = CO[name]
            return CS[0:parts, o:o + w]

        ident = K("ident")
        ring_ready = [S(f"ring_ready{j}") for j in range(RING)]
        units_used = S("units_used")

        units = []

        def cols(w, c0, c1):
            return [(w[0].rearrange("(p t) n -> p t n", t=KC)[:, :, c0:c1], KC, c1 - c0)]

        def rows(w, t0, t1, nt):
            n = w.shape[-1]
            return [(w[0].rearrange("(t p) n -> p t n", t=nt)[:, t0:t1, :], t1 - t0, n)]

        SECT = [(C_HF, C_HI), (C_HQ, C_HF), (0, 512), (512, 1024), (1024, C_HQ), (C_HI, C_HG), (C_HG, C_MRG)] + \
               [(C_MRG + 512 * j, C_MRG + 512 * (j + 1)) for j in (2, 3, 0, 1)]
        ORDER = "A0 A1 F0 F1 Hpre F2 F3 H0 F4 H1 F5 H2 F6 H3 F7 H4 F8 H5 F9 H6 Nrope F10 H7 F11 H8 Nqk F12 Ho Nkv F13 A2 Gate Hgate " \
                "Ncmp Ht F14 Nkc F15 Nsc A3 F16 Npc M0 F17 SigH Q0 A4 M1 F18 Q1 M2 F19 A5 Q2 A6 M3 F20 F21 Bh0 SigN Q3 Bh1 A7 Nout A8 A9 A10 A11 Bn"
        FILL = [w for w in ORDER.split() if w[0] in "FA" and w[1].isdigit()]
        PLACE = {}
        for w in ORDER.split():
            if w == "Bh0":
                K_BR_HG = len(units)
                units += rows(A["w_br_hg"], 0, 4, 4)
            elif w not in FILL:
                continue
            elif w[0] == "A":
                PLACE[w] = len(units)
                units += cols(A["w_ada_2"], 512 * int(w[1:]), 512 * (int(w[1:]) + 1))
            elif int(w[1:]) % 2 == 0:
                PLACE[w] = PLACE[f"F{int(w[1:]) + 1}"] = len(units)
                c0, c1 = SECT[int(w[1:]) // 2]
                units += cols(A["w_in"], c0, c1)

        def kept(w):
            return FILL.index(w) + 1
        K_BR_NSA = len(units)
        units += rows(A["w_br_nsa"], 0, 4, 4)
        K_OUT = len(units)
        units += rows(A["w_out"], 0, 4, 8) + rows(A["w_out"], 4, 8, 8)
        K_MOE1 = len(units)
        units += [None] * (3 * NE)
        K_IN2 = len(units)
        units += cols(A["w_in_2"], 1536, 2048) + [None]
        for j in range(3):
            units += cols(A["w_in_2"], 512 * j, 512 * (j + 1))
        K_GLU = len(units)
        units += rows(A["w_glu_2"], 0, 4, 4)
        K_OUT2 = len(units)
        units += rows(A["w_out_2"], 0, 4, 8) + [None] + rows(A["w_out_2"], 4, 8, 8)
        K_SCRATCH = (K_IN2 + 1, K_OUT2 + 1)
        K_MOE2 = len(units)
        units += [None] * (6 * NE)

        def load_unit(sp, k):
            if k >= RING:
                sp.wait_ge(units_used, k - RING + 1)
            if k in K_SCRATCH:
                if k >= RING:
                    sp.wait_ge(ring_ready[k % RING], 16 * (k // RING))
                sp.sem_inc(ring_ready[k % RING], 16)
                return
            if K_MOE1 <= k < K_IN2:
                src, dst = moe1_src(0, k - K_MOE1), ring[:, k % RING, :]
            elif k >= K_MOE2:
                src, dst = moe2_src(0, k - K_MOE2), ring[:, k % RING, :]
            else:
                src, n, w = units[k]
                dst = ring[:, k % RING, 0:n * w].rearrange("p (t n) -> p t n", t=n)
            sp.dma_start(dst, src).then_inc(ring_ready[k % RING], 16)

        def unit_arrived(pe, k):
            pe.wait_ge(ring_ready[k % RING], 16 * (k // RING + 1))

        def unit(k):
            n, w = units[k][1:]
            return ring[:, k % RING, 0:n * w].rearrange("p (t n) -> p t n", t=n)

        def moe1_src(e0, j):
            w = A[("w_gate", "w_up", "w_down")[j // 2]]
            t = 4 if j >= 4 else KC
            return w[0, bass.ds(e0 + j % 2, 1), :, :].rearrange("a (p t) n -> (a p) (t n)", t=t)

        def moe2_src(e0, j):
            e = bass.ds(e0 + j % 2, 1)
            if j < 8:
                return A["w1_2"][0, e, :, :].rearrange("a (p u t) n -> (a p) u (t n)", u=4, t=2)[:, j // 2, :]
            return A["w2_2"][0, e, :, :].rearrange("a (p u t) n -> (a p) u (t n)", u=2, t=4)[:, j // 2 - 4, :]

        def chain(eng, name):
            s, n = S(name), chains.setdefault(name, [0])

            def link(ins):
                n[0] += 1
                ins.then_inc(s, 1)
                eng.wait_ge(s, n[0])
            return link
        chains = {}

        class Norm:

            def __init__(self, tag, shift=None):
                self.tag, self.shift = tag, shift
                self.sq, self.sd, self.rt = S(tag + "_squares"), S(tag + "_variance"), S(tag + "_root")
                self.hn, self.tr, self.ev = S(tag + "_normed"), S(tag + "_transposed"), S(tag + "_hT")

            def act_root(self, a):
                a.wait_ge(self.sd, 1)
                nc.scalar.activation(st[:, 2:4], st[:, 2:4], ACT.Sqrt).then_inc(self.rt, 1)

            def act(self, a):
                self.act_root(a)
                for t in range(KC):
                    if t % 2 == 0:
                        a.wait_ge(self.tr, t // 2 + 1)
                        nc.scalar.activation(hT[:, t:t + 2, :].rearrange("p t q -> p (t q)"), ps[:, t // 2, :],
                                             ACT.Copy).then_inc(self.ev, 1)

            def dve_stats(self, v, link):
                for i in range(NT):
                    link(nc.vector.tensor_tensor_reduce(out=junk[:], in0=X[:, i, :], in1=X[:, i, :], scale=1.0,
                                                        scalar=0.0, op0=ALU.mult, op1=ALU.add,
                                                        accum_out=st[:, i:i + 1]))
                nc.vector.tensor_scalar(st[:, 2:4], st[:, 0:2], 1.0 / D, EPS, ALU.mult, ALU.add).then_inc(self.sd, 1)
                v.wait_ge(self.rt, 1)
                link(nc.vector.reciprocal(st[:, 4:6], st[:, 2:4]))

            def dve(self, v, link):
                self.dve_stats(v, link)
                for i in range(NT):
                    o = hn[:, i].rearrange("q t p -> q p t")
                    x = X[:, i, :].rearrange("q (p t) -> q p t", t=KC)
                    g = grow[:].rearrange("q (p t) -> q p t", t=KC)
                    ins = nc.vector.scalar_tensor_tensor(out=o, in0=x, scalar=st[:, 4 + i:5 + i], in1=g,
                                                         op0=ALU.mult, op1=ALU.mult)
                    if self.shift is not None:
                        link(ins)
                        b = self.shift.rearrange("q (p t) -> q p t", t=KC)
                        ins = nc.vector.tensor_tensor(o, o, b, ALU.add)
                    ins.then_inc(self.hn, 1)

            def pe(self, pe):
                for t in range(KC):
                    for i in range(NT):
                        pe.wait_ge(self.hn, i + 1)
                        ins = nc.tensor.transpose(ps[:, t // 2, (t % 2) * 256 + i * 128:(t % 2) * 256 + i * 128 + 128],
                                                  hn[:, i, t, :], ident)
                    if t % 2 == 1:
                        ins.then_inc(self.tr, 1)

        modrow = sbuf(top, "modrow", [128, 12, 128])

        p1 = ExitStack()
        qkv = sbuf(p1, "qkv", [128, NT, C_HQ])
        hgi = sbuf(p1, "hgi", [128, NT, 512])
        hgg = sbuf(p1, "hgg", [128, NT, 512])
        mrg = sbuf(p1, "mrg", [128, NT, 2 * D])
        hqT = sbuf(p1, "hqT", [128, 4, T])
        hfT = sbuf(p1, "hfT", [128, 4, T])
        lvl = sbuf(p1, "lvl", [128, LEVELS * 128])
        cv = sbuf(p1, "cv", [128, KC])
        cwide = sbuf(p1, "cwide", [128, KC, 32])
        hgn = sbuf(p1, "hgn", [128, 1])
        W1 = sbuf(p1, "W1", [128, 5888])
        Xf = X[:].rearrange("p i c -> p (i c)")
        mf = mrg[:].rearrange("p i c -> p (i c)")
        pos2, lbn = mf[0:32, 0:128], mf[0:8, 128:256]
        hnf = hn[:].rearrange("p i t q -> p (i t q)")
        hTf = hT[:].rearrange("p t q -> p (t q)")
        qT = Xf[:, 0:1024].rearrange("p (a q) -> p a q", a=4)
        kT = Xf[:, 1024:2048].rearrange("p (a q) -> p a q", a=4)
        kvT = W1[:, 4096:4608].rearrange("p (g q) -> p g q", g=2)
        kvc = grow[:, 0:512].rearrange("p (i g c) -> p i g c", i=2, g=2)
        PcT = grow[0:64, :].rearrange("p (i r q) -> p i r q", i=2, r=4)
        Sc = W1[:, 4608:4864].rearrange("p (i h n) -> p i h n", i=2, h=8)
        Pc = W1[:, 4864:5376].rearrange("p (i r g n) -> p i r g n", i=2, r=4, g=2)
        rtmp = W1[:, 4608:5376]
        sm = W1[:, 5376:5888]
        kc, vcb = sm[0:64, 0:64], sm[0:64, 64:192]
        kcd = sm[0:64, 192:320]
        kcT = sm[:, 320:384]
        posT, lraw = sm[:, 384:416], sm[:, 416:424]
        wts = sm[:, 424:480]
        kdup = junk[:].rearrange("p (i a b c) -> p i a b c", i=2, a=4, b=2)
        blkT = hnf.rearrange("p (l g n) -> p l g n", l=32, g=2)
        Wc = mf[:, 2048:4096].rearrange("p (l e) -> p l e", l=32)
        P = hnf.rearrange("p (s a k) -> p s a k", s=2, a=4)
        PT = W1[:, 1024:3072].rearrange("p (b h q) -> p b h q", b=2, h=8)
        onsa = junk[:].rearrange("p (i c) -> p i c", i=2)
        onT = grow[:].rearrange("p (a q) -> p a q", a=4)
        hq, hf = hqT[:].rearrange("p h t -> p (h t)"), hfT[:].rearrange("p h t -> p (h t)")
        Dl = hf
        QK = [mf[:, 0:1024], mf[:, 1024:2048]]
        kk, bsum = W1[:, 0:1024], W1[:, 1024:2048]
        Am = [W1[:, 2048:2560], W1[:, 2560:3072], W1[:, 3072:3584]]
        hp_ = W1[:, 3584:4096]
        osq = hfT[:].rearrange("p (i a) t -> p i (a t)", i=2)
        hst = sm[:, 480:504]
        lb, oml = sm[:, 504:508], sm[:, 508:512]
        ohn = bsum.rearrange("p (i c) -> p i c", i=2)
        ohT = kk.rearrange("p (a q) -> p a q", a=4)

        n0 = Norm("n0")
        s_short, s_lvl = S("short_vectors_in"), S("level_masks_in")
        s_c, s_ca, s_cw = S("cond_in"), S("cond_activated"), S("cond_wide")
        s_cst, s_x, s_grow, s_wc = S("consts_in"), S("x_in"), S("gain_in"), S("cmp_weights_in")
        s_proj, s_pev, s_gate = S("proj_done"), S("proj_kept"), S("gates_ready")
        s_rope, s_tq, s_tqk, s_tv, s_tvk, s_sh, s_shk = (S(n) for n in (
            "nsa_roped", "qkT_done", "qkT_kept", "cmp_inT", "cmp_inT_kept", "shortT", "shortT_kept"))
        s_blk, s_cmp, s_kcd, s_kct, s_kctk = (S(n) for n in ("blocks_built", "compressed", "kcmp_roped", "kcmpT_done", "kcmpT_kept"))
        s_sc, s_scs, s_sce, s_pc, s_pct, s_pctk = (S(n) for n in (
            "cmp_scores", "cmp_shifted", "cmp_exp", "cmp_probs", "cmp_probsT", "cmp_probsT_kept"))
        s_s, s_mx, s_exp, s_p, s_pt, s_ptk, s_pv = (S(n) for n in (
            "scores", "scores_max", "scores_exp", "probs", "probsT", "probsT_kept", "pv_done"))
        s_o, s_oT, s_oTk = S("nsa_out_kept"), S("nsa_outT"), S("nsa_outT_kept")
        h_f, h_ln, h_d, h_e, h_qk, h_a, h_am = (S(n) for n in (
            "forget", "log_forget", "level_exponents", "level_factors", "level_operands", "level_products", "level_added"))
        h_o, h_sq, h_v, h_r, h_n, h_g, h_t, h_tk, h_lb = (S(n) for n in (
            "hg_out", "hg_squares", "hg_variance", "hg_root", "hg_normed", "hg_gated", "hg_outT", "hg_outT_kept", "hg_bound"))
        b_h, b_hm, b_m, b_mx, b_t, b_tk, b_o, b_x = (S(n) for n in (
            "hg_branch", "hg_branch_gated", "nsa_branch", "mixed", "mixedT", "mixedT_kept", "out_proj", "x1"))
        DEST = [hfT, hqT, (qkv, 0, 512), (qkv, 512, 1024), (qkv, 1024, C_HQ), (hgi, 0, 512), (hgg, 0, 512),
                (mrg, 1024, 1536), (mrg, 1536, 2048), (mrg, 0, 512), (mrg, 512, 1024)]
        STEPS = [(i, ty) for i in range(NT) for ty in range(2)]

        def bc(ap, shape):
            return ap.to_broadcast(shape)

        def follow(steps, order=ORDER):
            for word in order.split():
                name, n = word.rstrip("0123456789"), word.lstrip("ABCDEFGHIJKLMNOPQRSTUVWXYZabcdefghijklmnopqrstuvwxyz")
                if name in steps:
                    steps[name](int(n)) if n else steps[name]()

        def rope(eng, link, t1, t2, cos, sin, shape, tmp):
            n = int(np.prod(shape[1:]))
            names = "abcd"[:len(shape) - 1]
            pat = "p (" + " ".join(names) + ") -> p " + " ".join(names)
            kw = dict(zip(names, shape[1:]))
            b = [tmp[0:shape[0], j * n:(j + 1) * n].rearrange(pat, **kw) for j in range(4)]
            link(eng.tensor_tensor(b[0], t1, cos, ALU.mult))
            link(eng.tensor_tensor(b[1], t2, sin, ALU.mult))
            link(eng.tensor_tensor(b[2], t2, cos, ALU.mult))
            link(eng.tensor_tensor(b[3], t1, sin, ALU.mult))
            link(eng.tensor_tensor(t1, b[0], b[1], ALU.subtract))
            return eng.tensor_tensor(t2, b[2], b[3], ALU.add)

        with nc.Block() as block:
            @block.sync
            def _(sp):
                sp.dma_start(X[:], A["x"][0].rearrange("(i q) d -> q i d", i=NT)).then_inc(s_x, 16)
                sp.dma_start(pos2[:, 0:64], A["cmp_pos"][0]).then_inc(s_short, 16)
                sp.dma_start(pos2[:, 64:128], A["cmp_pos"][0]).then_inc(s_short, 16)
                sp.dma_start(lbn, A["hg_lb_logits"].rearrange("r (h k) -> (r h) k", h=4)).then_inc(s_short, 16)
                sp.dma_start(hgn[:], A["hg_norm"].rearrange("a v -> v a")).then_inc(s_short, 16)
                for k in range(5):
                    load_unit(sp, k)
                sp.dma_start(Wc[0:64], A["w_cmp_k"][0].rearrange("(l d) e -> d l e", l=32)).then_inc(s_wc, 16)
                sp.dma_start(Wc[64:128], A["w_cmp_v"][0].rearrange("(l d) e -> d l e", l=32)).then_inc(s_wc, 16)
                for k in range(5, K_MOE1 + 4):
                    load_unit(sp, k)

            @block.gpsimd
            def _(g):
                link = chain(g, "g_chain")
                ng = nc.gpsimd
                g.wait_ge(s_ca, 1)
                ng.tensor_copy(cwide[:], bc(cv[:].rearrange("p (t c) -> p t c", c=1), [128, KC, 32])).then_inc(s_cw, 1)
                g.wait_ge(s_cst, 16)
                g.wait_ge(s_pev, kept("F9"))
                for i in range(NT):
                    cos = K("cos")[:, i * 8:i * 8 + 8].rearrange("p (a c) -> p a c", a=1)
                    sin = K("sin")[:, i * 8:i * 8 + 8].rearrange("p (a c) -> p a c", a=1)
                    q = qkv[:, i, 0:512].rearrange("p (h d) -> p h d", h=8)
                    link(rope(ng, link, q[:, :, 0:8], q[:, :, 8:16], bc(cos, [128, 8, 8]), bc(sin, [128, 8, 8]), [128, 8, 8], rtmp))
                    for c in (768, 1024):
                        k = qkv[:, i, c:c + 128].rearrange("p (h d) -> p h d", h=2)
                        link(rope(ng, link, k[:, :, 0:8], k[:, :, 8:16], bc(cos, [128, 2, 8]), bc(sin, [128, 2, 8]), [128, 2, 8], rtmp))
                for i in range(NT):
                    for ty in range(2):
                        src = qkv[:, i, 768 + 256 * ty:768 + 256 * ty + 128].rearrange("p (g a d) -> p g a d", g=2, a=1)
                        link(ng.tensor_copy(kdup[:, i, 2 * ty:2 * ty + 2], bc(src, [128, 2, 2, 64])))
                    src = qkv[:, i, 512:768].rearrange("p (k g d) -> p g k d", k=2, g=2)
                    link(ng.tensor_copy(kvc[:, i].rearrange("p g (k d) -> p g k d", k=2), src))
                ng.memset(hnf, 0.0).then_inc(s_rope, 1)

            @block.vector
            def _(v):
                link = chain(v, "v_chain")
                nv = nc.vector
                v.wait_ge(s_x, 16)
                v.wait_ge(s_grow, 16)
                n0.dve(v, link)

                def exponents(L):
                    half = 1 << L
                    bv = bsum.rearrange("p (n k) -> p n k", k=2 * half)
                    dv = Dl.rearrange("p (n k) -> p n k", k=2 * half)
                    ref = bc(bv[:, :, half - 1:half], [128, 512 // half, half])
                    nv.tensor_tensor(dv[:, :, half:], bv[:, :, half:], ref, ALU.subtract)
                    nv.tensor_tensor(dv[:, :, 0:half], ref, bv[:, :, 0:half], ALU.subtract).then_inc(h_d, 1)

                def Hpre():
                    v.wait_ge(s_lvl, 16)
                    v.wait_ge(s_shk, 1)
                    nv.tensor_tensor(lb, lraw[:, 0:4], lraw[:, 4:8], ALU.subtract).then_inc(h_lb, 1)
                    v.wait_ge(h_lb, 2)
                    link(nv.tensor_scalar(oml, lb, -1.0, 1.0, ALU.mult, ALU.add))
                    v.wait_ge(s_pev, kept("F1"))
                    for h in range(4):
                        ins = nv.tensor_scalar(hfT[:, h], hfT[:, h], oml[:, h:h + 1], lb[:, h:h + 1], ALU.mult, ALU.add)
                    link(ins)
                    nv.tensor_scalar(kk, hf, -1.0, 1.0, ALU.mult, ALU.add).then_inc(h_f, 1)
                    v.wait_ge(h_ln, 1)
                    for h in range(4):
                        ins = nv.tensor_tensor_scan(bsum[:, h * T:h * T + T], bc(K("ones")[:, 0:1], [128, T]), hfT[:, h], 0.0, ALU.mult, ALU.add)
                    link(ins)
                    exponents(0)

                def H(n):
                    if n <= LEVELS:
                        half = 1 << n
                        dv = Dl.rearrange("p (n k) -> p n k", k=2 * half)
                        qv = QK[n % 2].rearrange("p (n k) -> p n k", k=2 * half)
                        hv = hq.rearrange("p (n k) -> p n k", k=2 * half)
                        kv = kk.rearrange("p (n k) -> p n k", k=2 * half)
                        v.wait_ge(s_pev, kept("F3"))
                        v.wait_ge(h_e, n + 1)
                        if n >= 2:
                            v.wait_ge(h_a, n)
                        nv.tensor_tensor(qv[:, :, half:], hv[:, :, half:], dv[:, :, half:], ALU.mult)
                        nv.tensor_tensor(qv[:, :, 0:half], kv[:, :, 0:half], dv[:, :, 0:half], ALU.mult).then_inc(h_qk, 1)
                    if n < LEVELS:
                        v.wait_ge(h_qk, n + 1)
                        exponents(n + 1)
                    v.wait_ge(h_a, n + 1)
                    if n > LEVELS:
                        nv.tensor_copy(Am[2], ps[:, 0, :]).then_inc(h_am, 1)
                        return
                    m = ident if n == 0 else lvl[:, (n - 1) * 128:n * 128]
                    m = bc(m.rearrange("p (a t) -> p a t", a=1), [128, 4, 128])
                    for i in range(NT):
                        src = ps[:, i, :].rearrange("p (h t) -> p h t", h=4)
                        if n == 0:
                            ins = nv.tensor_tensor(Am[i].rearrange("p (h t) -> p h t", h=4), src, m, ALU.mult)
                        else:
                            link(nv.tensor_tensor(hp_.rearrange("p (h t) -> p h t", h=4), src, m, ALU.mult))
                            ins = nv.tensor_tensor(Am[i], Am[i], hp_, ALU.add)
                        if i == 0:
                            link(ins)
                    ins.then_inc(h_am, 1)
                    v.wait_ge(h_am, n + 1)

                def Ho():
                    v.wait_ge(h_sq, 2)
                    link(nv.tensor_reduce(hst[:, 0:8], osq[:].rearrange("p i (h c) -> p (i h) c", h=4), AX.X, ALU.add))
                    nv.tensor_scalar(hst[:, 8:16], hst[:, 0:8], 1.0 / 128, EPS, ALU.mult, ALU.add).then_inc(h_v, 1)
                    v.wait_ge(h_r, 1)
                    link(nv.reciprocal(hst[:, 16:24], hst[:, 8:16]))
                    for i in range(NT):
                        r = bc(hst[:, 16 + 4 * i:20 + 4 * i].rearrange("p (h n) -> p h n", n=1), [128, 4, 128])
                        o = ohn[:, i].rearrange("p (h c) -> p h c", h=4)
                        nv.tensor_tensor(o, ps[:, i, :].rearrange("p (h c) -> p h c", h=4), r, ALU.mult).then_inc(h_n, 1)

                def Hgate():
                    v.wait_ge(h_n, 2)
                    v.wait_ge(s_gate, 1)
                    nv.tensor_tensor(bsum, bsum, hgg[:].rearrange("p i c -> p (i c)"), ALU.mult).then_inc(h_g, 1)

                def Nkv():
                    v.wait_ge(s_tvk, 1)
                    v.wait_ge(s_rope, 1)
                    for g in range(2):
                        for a in range(2):
                            src = kvT[:, g, 16 * a:16 * a + 240].rearrange("p (n b) -> p b n", b=16)
                            po = posT[:, 16 * a:16 * a + 16].rearrange("p (b n) -> p b n", n=1)
                            nv.tensor_tensor(blkT[:, 16 * a:16 * a + 16, g, 0:NCMP], src, bc(po, [128, 16, NCMP]),
                                             ALU.add).then_inc(s_blk, 1)

                def Ncmp():
                    v.wait_ge(s_cmp, 1)
                    nv.tensor_copy(kc, ps[0:64, 4, 0:64])
                    link(nv.memset(vcb, 0.0))
                    nv.tensor_copy(vcb[0:32, 0:64], ps[0:32, 5, 0:64])
                    link(nv.tensor_copy(vcb[32:64, 64:128], ps[32:64, 5, 0:64]))
                    link(rope(nv, link, kc[:, 0:8], kc[:, 8:16], K("ccos", 64), K("csin", 64), [64, 8], rtmp))
                    nv.tensor_copy(kcd.rearrange("p (a d) -> p a d", a=2),
                                   bc(kc.rearrange("p (a d) -> p a d", a=1), [64, 2, 64])).then_inc(s_kcd, 1)

                def Nsc():
                    v.wait_ge(s_sc, 1)
                    for i in range(NT):
                        add = K("cadd")[:, i * 16:i * 16 + 16].rearrange("p (a n) -> p a n", a=1)
                        for par in range(2):
                            o = Sc[:, i].rearrange("p (a b) n -> p a b n", b=2)[:, :, par, :]
                            ins = nv.tensor_tensor(o, ps[:, 4 + par, i * 64:i * 64 + 64].rearrange("p (a n) -> p a n", a=4),
                                                   bc(add, [128, 4, 16]), ALU.add)
                    link(ins)
                    S16 = Sc[:].rearrange("p i h n -> p (i h) n")[:, :, 0:NCMP]
                    mx, su = wts[:, 0:16], wts[:, 16:32]
                    link(nv.tensor_reduce(mx, S16, AX.X, ALU.max))
                    nv.tensor_tensor(S16, S16, bc(mx.rearrange("p (h n) -> p h n", n=1), [128, 16, NCMP]),
                                     ALU.subtract).then_inc(s_scs, 1)
                    link(nv.memset(Pc[:, :, :, :, :], 0.0))
                    v.wait_ge(s_sce, 1)
                    link(nv.tensor_reduce(su, S16, AX.X, ALU.add))
                    link(nv.reciprocal(su, su))
                    v.wait_ge(s_gate, 1)
                    link(nv.tensor_tensor(su.rearrange("p (i h) -> p i h", i=2), su.rearrange("p (i h) -> p i h", i=2),
                                          qkv[:, :, C_GATE:C_HQ].rearrange("p i (h b) -> p i h b", b=3)[:, :, :, 0], ALU.mult))
                    link(nv.tensor_tensor(S16, S16, bc(su.rearrange("p (h n) -> p h n", n=1), [128, 16, NCMP]), ALU.mult))
                    for i in range(NT):
                        for g in range(2):
                            mul = K("cmul")[:, i * 16:i * 16 + NCMP].rearrange("p (a n) -> p a n", a=1)
                            nv.tensor_tensor(Pc[:, i, :, g, 0:NCMP], Sc[:, i, 4 * g:4 * g + 4, 0:NCMP],
                                             bc(mul, [128, 4, NCMP]), ALU.mult).then_inc(s_pc, 1)

                def M(n):
                    i, ty = STEPS[n]
                    nk = 128 * (i + 1)
                    P8 = P[:].rearrange("p s a k -> p (s a) k")[:, :, 0:nk]
                    v.wait_ge(s_s, n + 1)
                    if n:
                        v.wait_ge(s_pt, n)
                    src = ps[:, 2:6, :].rearrange("p b (a k) -> p (b a) k", a=2)
                    ca = K("causal").rearrange("p (a k) -> p a k", a=1)
                    ins = nv.tensor_tensor(P8[:, :, nk - 128:nk], src[:, :, nk - 128:nk], bc(ca, [128, 8, 128]), ALU.add)
                    if i:
                        ins = nv.tensor_copy(P8[:, :, 0:128], src[:, :, 0:128])
                    link(ins)
                    m8, w8 = wts[:, 32:40], wts[:, 48:56]
                    link(nv.tensor_reduce(m8, P8, AX.X, ALU.max))
                    nv.tensor_scalar(wts[:, 40:48], m8, -0.125, None, ALU.mult).then_inc(s_mx, 1)
                    v.wait_ge(s_exp, n + 1)
                    link(nv.reciprocal(w8, w8))
                    gate = qkv[:, i, C_GATE:C_HQ].rearrange("p (a s b) -> p s a b", s=2, b=3)[:, :, :, 1 + ty]
                    link(nv.tensor_tensor(w8.rearrange("p (s a) -> p s a", s=2), w8.rearrange("p (s a) -> p s a", s=2), gate, ALU.mult))
                    nv.tensor_tensor(P8, P8, bc(w8.rearrange("p (h n) -> p h n", n=1), [128, 8, nk]), ALU.mult).then_inc(s_p, 1)

                def Bh(i):
                    v.wait_ge(b_h, i + 1)
                    v.wait_ge(s_gate, 2)
                    nv.tensor_tensor(mrg[:, i, D:], mrg[:, i, D:], ps[:, 6:8, :].rearrange("p b c -> p (b c)"), ALU.mult).then_inc(b_hm, 1)

                def Bn():
                    v.wait_ge(s_gate, 3)
                    v.wait_ge(b_hm, 2)
                    for i in range(NT):
                        v.wait_ge(b_m, i + 1)
                        link(nv.tensor_tensor(mrg[:, i, 0:D], mrg[:, i, 0:D], ps[:, 4 + 2 * i:6 + 2 * i, :].rearrange("p b c -> p (b c)"), ALU.mult))
                        nv.tensor_tensor(mrg[:, i, 0:D], mrg[:, i, 0:D], mrg[:, i, D:2 * D], ALU.add).then_inc(b_mx, 1)
                    v.wait_ge(s_x, 32)
                    for i in range(NT):
                        v.wait_ge(b_o, i + 1)
                        nv.tensor_tensor(X[:, i, :], X[:, i, :], ps[:, 4 + 2 * i:6 + 2 * i, :].rearrange("p b c -> p (b c)"),
                                         ALU.add).then_inc(b_x, 1)

                follow(dict(Hpre=Hpre, H=H, Ho=Ho, Hgate=Hgate, Nkv=Nkv, Ncmp=Ncmp, Nsc=Nsc, M=M, Bh=Bh, Bn=Bn))

            @block.scalar
            def _(a):
                na = nc.scalar
                a.dma_start(grow[:], A["attn_norm"].to_broadcast([128, D])).then_inc(s_grow, 16)
                a.dma_start(cv[:], A["c_2"][0].rearrange("(p t) -> p t", t=KC)).then_inc(s_c, 16)
                a.dma_start(CS[:], A["cst"][:, 0:CO["lvl"][0]]).then_inc(s_cst, 16)
                a.dma_start(lvl[:], A["cst"][:, CO["lvl"][0]:CO["tie32"][0]]).then_inc(s_lvl, 16)
                a.wait_ge(s_c, 16)
                na.activation(cv[:], cv[:], ACT.Silu).then_inc(s_ca, 1)
                n0.act(a)

                def Ada(j):
                    m = kept(f"A{j}")
                    a.wait_ge(s_proj, m)
                    na.activation(modrow[:, j, :], ps[:, 6 + m % 2, 0:128], ACT.Copy).then_inc(s_pev, 1)
                    a.sem_inc(units_used, 1)

                def F(n):
                    u, h = divmod(n, 2)
                    m = kept(f"F{n}")
                    a.wait_ge(s_proj, m)
                    if n == 14:
                        a.wait_ge(h_a, LEVELS + 2)
                        a.wait_ge(s_cmp, 1)
                    src, dst = ps[:, 6 + m % 2, :], DEST[u]
                    if type(dst) is tuple:
                        ins = na.activation(dst[0][:, h, dst[1]:dst[2]], src[:, 0:dst[2] - dst[1]], ACT.Copy)
                    else:
                        ins = na.activation(dst[:, 2 * h:2 * h + 2, :].rearrange("p a b -> p (a b)"), src, ACT.Sigmoid if u == 0 else ACT.Copy)
                    ins.then_inc(s_pev, 1)
                    if h:
                        a.sem_inc(units_used, 1)

                def Hpre():
                    a.wait_ge(s_sh, 1)
                    na.activation(sm[:, 384:424], ps[:, 4, 0:40], ACT.Copy).then_inc(s_shk, 1)
                    a.wait_ge(h_lb, 1)
                    na.activation(lb, lb, ACT.Sigmoid).then_inc(h_lb, 1)
                    a.wait_ge(h_f, 1)
                    na.activation(hf, hf, ACT.Ln).then_inc(h_ln, 1)
                    a.wait_ge(h_d, 1)
                    na.activation(Dl, Dl, ACT.Exp).then_inc(h_e, 1)

                def H(n):
                    if n < LEVELS:
                        a.wait_ge(h_d, n + 2)
                        na.activation(Dl, Dl, ACT.Exp).then_inc(h_e, 1)

                def Ho():
                    a.wait_ge(h_qk, LEVELS + 1)
                    for i in range(NT):
                        a.wait_ge(h_o, i + 1)
                        na.activation(osq[:, i], ps[:, i, :], ACT.Square).then_inc(h_sq, 1)
                    a.wait_ge(h_v, 1)
                    na.activation(hst[:, 8:16], hst[:, 8:16], ACT.Sqrt).then_inc(h_r, 1)

                def Gate():
                    a.wait_ge(s_pev, kept("F13"))
                    na.activation(qkv[:, :, C_GATE:C_HQ], qkv[:, :, C_GATE:C_HQ], ACT.Sigmoid)
                    na.activation(hgg[:], hgg[:], ACT.Silu).then_inc(s_gate, 1)

                def SigH():
                    a.wait_ge(s_pev, kept("F17"))
                    na.activation(mrg[:, :, D:], mrg[:, :, D:], ACT.Sigmoid).then_inc(s_gate, 1)

                def SigN():
                    a.wait_ge(s_pev, kept("F21"))
                    na.activation(mrg[:, :, 0:D], mrg[:, :, 0:D], ACT.Sigmoid).then_inc(s_gate, 1)

                def Nqk():
                    a.wait_ge(s_tq, 1)
                    for b in range(4):
                        dst = [qT[:, 0:2], qT[:, 2:4], kT[:, 0:2], kT[:, 2:4]][b]
                        na.activation(dst, ps[:, 2 + b, :].rearrange("p (a q) -> p a q", a=2), ACT.Copy).then_inc(s_tqk, 1)

                def Nkv():
                    a.wait_ge(s_tv, 1)
                    na.activation(kvT[:], ps[:, 2, :].rearrange("p (a q) -> p a q", a=2), ACT.Copy).then_inc(s_tvk, 1)

                def Nkc():
                    a.wait_ge(s_kct, 1)
                    na.activation(kcT, ps[:, 3, 0:64], ACT.Copy).then_inc(s_kctk, 1)

                def Nsc():
                    a.wait_ge(s_scs, 1)
                    S16 = Sc[:].rearrange("p i h n -> p (i h) n")[:, :, 0:NCMP]
                    na.activation(S16, S16, ACT.Exp, scale=0.125).then_inc(s_sce, 1)

                def Npc():
                    a.wait_ge(s_pct, 1)
                    for i in range(NT):
                        na.activation(PcT[:, i], ps[0:64, 2 + i, :].rearrange("p (r q) -> p r q", r=4), ACT.Copy).then_inc(s_pctk, 1)

                def Ht():
                    a.wait_ge(h_t, 1)
                    a.wait_ge(s_short, 64)
                    for b in range(2):
                        na.activation(ohT[:, 2 * b:2 * b + 2], ps[:, b, :].rearrange("p (a q) -> p a q", a=2), ACT.Copy,
                                      scale=hgn[:, 0:1]).then_inc(h_tk, 1)

                def M(n):
                    i, ty = STEPS[n]
                    nk = 128 * (i + 1)
                    a.wait_ge(s_mx, n + 1)
                    for h in range(8):
                        row = P[:].rearrange("p s a k -> p (s a) k")[:, h, 0:nk]
                        ins = na.activation(row, row, ACT.Exp, bias=wts[:, 40 + h:41 + h], scale=0.125,
                                            accum_out=wts[:, 48 + h:49 + h])
                    ins.then_inc(s_exp, 1)

                def Q(n):
                    i, ty = STEPS[n]
                    a.wait_ge(s_pt, n + 1)
                    a.wait_ge(h_t, 1)
                    if n:
                        a.wait_ge(s_pv, n)
                    for kb in range(i + 1):
                        na.activation(PT[:, kb], ps[:, 2 + 2 * kb:4 + 2 * kb, :].rearrange("p b (c q) -> p (b c) q", c=4),
                                      ACT.Copy).then_inc(s_ptk, 1)
                    if ty:
                        a.wait_ge(s_pv, n + 1)
                        na.activation(onsa[:, i], ps[:, i, :], ACT.Copy).then_inc(s_o, 1)
                    if n == 3:
                        a.dma_start(X[:], A["x"][0].rearrange("(i q) d -> q i d", i=NT)).then_inc(s_x, 16)

                def Nout():
                    a.wait_ge(s_oT, 1)
                    for b in range(2):
                        na.activation(onT[:, 2 * b:2 * b + 2], ps[:, 2 + b, :].rearrange("p (a q) -> p a q", a=2), ACT.Copy).then_inc(s_oTk, 1)

                def Bn():
                    a.wait_ge(b_m, 2)
                    a.dma_start(grow[:], A["ffn_norm"].to_broadcast([128, D])).then_inc(s_grow, 16)
                    for t in range(4):
                        a.wait_ge(b_t, t + 1)
                        na.activation(hT[:, 2 * t:2 * t + 2, :].rearrange("p t q -> p (t q)"), ps[:, t, :],
                                      ACT.Copy).then_inc(b_tk, 1)

                follow(dict(F=F, A=Ada, Hpre=Hpre, H=H, Ho=Ho, Gate=Gate, SigH=SigH, SigN=SigN, Nqk=Nqk, Nkv=Nkv, Nkc=Nkc, Nsc=Nsc,
                            Npc=Npc, Ht=Ht, M=M, Q=Q, Nout=Nout, Bn=Bn))

            @block.tensor
            def _(pe):
                nt = nc.tensor
                def Ada(j):
                    m = kept(f"A{j}")
                    unit_arrived(pe, PLACE[f"A{j}"])
                    pe.wait_ge(s_cw, 1)
                    if m > kept("F21"):
                        pe.wait_ge(b_hm, 2)
                    if m > 2:
                        pe.wait_ge(s_pev, m - 2)
                    w = unit(PLACE[f"A{j}"])
                    for t in range(KC):
                        for g in range(4):
                            ins = nt.matmul(ps[32 * g:32 * g + 32, 6 + m % 2, 0:128], cwide[:, t, :], w[:, t, 128 * g:128 * g + 128],
                                            start=t == 0, stop=t == KC - 1, tile_position=(0, 32 * g), skip_group_check=True)
                    ins.then_inc(s_proj, 1)

                def norm():
                    pe.wait_ge(s_cst, 16)
                    n0.pe(pe)
                    pe.wait_ge(s_short, 64)
                    nt.transpose(ps[:, 4, 0:32], pos2, K("ident", 32)[:, 0:32])
                    nt.transpose(ps[:, 4, 32:40], lbn, K("ident", 8)[:, 0:8]).then_inc(s_sh, 1)
                    pe.wait_ge(n0.ev, 4)

                def F(n):
                    if n == 0:
                        norm()
                    u, h = divmod(n, 2)
                    m = kept(f"F{n}")
                    k = PLACE[f"F{n}"]
                    unit_arrived(pe, k)
                    w = unit(k)
                    width = units[k][2]
                    if m > 2:
                        pe.wait_ge(s_pev, m - 2)
                    if type(DEST[u]) is tuple:
                        for t in range(KC):
                            ins = nt.matmul(ps[:, 6 + m % 2, 0:width], hT[:, t, h * 128:h * 128 + 128],
                                            w[:, t, :], start=t == 0, stop=t == KC - 1)
                    else:
                        for cb in range(2):
                            c = (2 * h + cb) * 128
                            for t in range(KC):
                                ins = nt.matmul(ps[:, 6 + m % 2, cb * 256:cb * 256 + 256], w[:, t, c:c + 128], hT[:, t, :],
                                                start=t == 0, stop=t == KC - 1)
                    ins.then_inc(s_proj, 1)

                def H(n):
                    pe.wait_ge(h_f, 1)
                    pe.wait_ge(s_pev, kept("F3"))
                    if n:
                        pe.wait_ge(h_qk, n)
                        pe.wait_ge(h_am, n)
                    if n <= LEVELS:
                        for i in range(NT):
                            for h in range(4):
                                c = h * T + i * 128
                                kx, qx = (kk, hq) if n == 0 else (QK[(n - 1) % 2], QK[(n - 1) % 2])
                                ins = nt.matmul(ps[:, i, h * 128:h * 128 + 128], kx[:, c:c + 128], qx[:, c:c + 128],
                                                start=True, stop=True)
                    else:
                        x = QK[(n - 1) % 2]
                        for h in range(4):
                            ins = nt.matmul(ps[:, 0, h * 128:h * 128 + 128], x[:, h * T:h * T + 128], x[:, h * T + 128:h * T + 256],
                                            start=True, stop=True)
                    ins.then_inc(h_a, 1)

                def Ho():
                    pe.wait_ge(h_am, LEVELS + 2)
                    pe.wait_ge(s_pev, kept("F11"))
                    for i in range(NT):
                        for h in range(4):
                            c = slice(h * 128, h * 128 + 128)
                            if i:
                                nt.matmul(ps[:, 1, c], Am[2][:, c], hgi[:, 0, c], start=True, stop=False)
                            ins = nt.matmul(ps[:, i, c], Am[i][:, c], hgi[:, i, c], start=i == 0, stop=True)
                        ins.then_inc(h_o, 1)

                def Ht():
                    pe.wait_ge(h_g, 1)
                    for i in range(NT):
                        for h in range(4):
                            ins = nt.transpose(ps[:, h // 2, (h % 2) * 256 + i * 128:(h % 2) * 256 + i * 128 + 128],
                                               ohn[:, i, h * 128:h * 128 + 128], ident)
                    ins.then_inc(h_t, 1)

                def Nqk():
                    pe.wait_ge(s_rope, 1)
                    pe.wait_ge(s_shk, 1)
                    for i in range(NT):
                        for hp in range(4):
                            nt.transpose(ps[:, 2 + hp // 2, (hp % 2) * 256 + i * 128:(hp % 2) * 256 + i * 128 + 128],
                                         qkv[:, i, hp * 128:hp * 128 + 128], ident)
                        for x in range(4):
                            ins = nt.transpose(ps[:, 4 + x // 2, (x % 2) * 256 + i * 128:(x % 2) * 256 + i * 128 + 128],
                                               kdup[:, i, x].rearrange("p b c -> p (b c)"), ident)
                    ins.then_inc(s_tq, 1)

                def Nkv():
                    pe.wait_ge(s_tqk, 1)
                    for i in range(NT):
                        for g in range(2):
                            ins = nt.transpose(ps[:, 2, g * 256 + i * 128:g * 256 + i * 128 + 128], kvc[:, i, g, :], ident)
                    ins.then_inc(s_tv, 1)

                def Ncmp():
                    pe.wait_ge(s_blk, 4)
                    pe.wait_ge(s_wc, 32)
                    pe.wait_ge(s_tqk, 4)
                    for l in range(32):
                        nt.matmul(ps[0:64, 4, 0:64], blkT[0:64, l].rearrange("p g n -> p (g n)"), Wc[0:64, l, :],
                                  start=l == 0, stop=l == 31)
                        ins = nt.matmul(ps[0:64, 5, 0:64], blkT[64:128, l].rearrange("p g n -> p (g n)"), Wc[64:128, l, :],
                                        start=l == 0, stop=l == 31)
                    ins.then_inc(s_cmp, 1)

                def Nkc():
                    pe.wait_ge(s_kcd, 1)
                    nt.transpose(ps[:, 3, 0:64], kcd, K("ident", 64)[:, 0:64]).then_inc(s_kct, 1)

                def Nsc():
                    pe.wait_ge(s_kctk, 1)
                    for i in range(NT):
                        for h in range(8):
                            r = 64 * (h % 2)
                            ins = nt.matmul(ps[:, 4 + h % 2, i * 64 + (h // 2) * 16:i * 64 + (h // 2) * 16 + 16],
                                            qT[r:r + 64, h // 2, i * 128:i * 128 + 128], kcT[r:r + 64, (h // 4) * 32:(h // 4) * 32 + 16],
                                            start=True, stop=True)
                    ins.then_inc(s_sc, 1)

                def Npc():
                    pe.wait_ge(s_pc, 4)
                    for i in range(NT):
                        for r in range(4):
                            ins = nt.transpose(ps[0:64, 2 + i, r * 128:r * 128 + 128], Pc[:, i, r].rearrange("p g n -> p (g n)"), ident)
                    ins.then_inc(s_pct, 1)

                def M(n):
                    i, ty = STEPS[n]
                    pe.wait_ge(s_pctk, 2)
                    if n:
                        pe.wait_ge(s_ptk, [0, 1, 2, 4][n])
                    for h in range(8):
                        par, a4 = h % 2, h // 2
                        r = 64 * par
                        for kb in range(i + 1):
                            c = (a4 % 2) * 256 + kb * 128
                            ins = nt.matmul(ps[:, 2 + 2 * par + a4 // 2, c:c + 128], qT[r:r + 64, a4, i * 128:i * 128 + 128],
                                            kT[r:r + 64, 2 * ty + h // 4, kb * 128:kb * 128 + 128], start=True, stop=True)
                    ins.then_inc(s_s, 1)
                    if ty == 0:
                        pe.wait_ge(h_tk, 2)
                        for r in range(4):
                            o = ps[:, i, :].rearrange("p (g r d) -> p g r d", g=2, r=4)[:, :, r, :]
                            nt.matmul(o, PcT[:, i, r, :], vcb.rearrange("p (g d) -> p g d", g=2), start=r == 0, stop=False,
                                      skip_group_check=True)

                def Q(n):
                    i, ty = STEPS[n]
                    pe.wait_ge(s_p, n + 1)
                    for kb in range(i + 1):
                        for h in range(8):
                            ins = nt.transpose(ps[:, 2 + 2 * kb + h // 4, (h % 4) * 128:(h % 4) * 128 + 128],
                                               P[:, h // 4, h % 4, kb * 128:kb * 128 + 128], ident)
                    ins.then_inc(s_pt, 1)
                    pe.wait_ge(s_ptk, [1, 2, 4, 6][n])
                    for s8 in range(8):
                        h = 2 * (s8 % 4) + s8 // 4
                        for kb in range(i + 1):
                            c = 896 + 256 * ty + (h // 4) * 64
                            ins = nt.matmul(ps[:, i, h * 64:h * 64 + 64], PT[:, kb, s8, :], qkv[:, kb, c:c + 64],
                                            start=False, stop=(ty == 1 and s8 == 7 and kb == i), skip_group_check=True)
                    ins.then_inc(s_pv, 1)

                def Bh(i):
                    unit_arrived(pe, K_BR_HG)
                    pe.wait_ge(s_pev, kept("F21"))
                    if i:
                        pe.wait_ge(b_hm, 1)
                    for h in range(2):
                        for c in range(4):
                            ins = nt.matmul(ps[:, 6 + h, :], ohT[:, c, i * 128:i * 128 + 128], unit(K_BR_HG)[:, c, h * 512:h * 512 + 512],
                                            start=c == 0, stop=c == 3)
                    ins.then_inc(b_h, 1)
                    if i:
                        pe.wait_ge(b_h, 2)
                        pe.wait_ge(units_used, K_BR_HG)
                        pe.sem_inc(units_used, 1)

                def Nout():
                    pe.wait_ge(s_o, 2)
                    pe.wait_ge(s_ptk, 6)
                    for i in range(NT):
                        for c in range(4):
                            ins = nt.transpose(ps[:, 2 + c // 2, (c % 2) * 256 + i * 128:(c % 2) * 256 + i * 128 + 128],
                                               onsa[:, i, c * 128:c * 128 + 128], ident)
                    ins.then_inc(s_oT, 1)

                def Bn():
                    unit_arrived(pe, K_BR_NSA)
                    pe.wait_ge(s_oTk, 2)
                    pe.wait_ge(s_pev, len(FILL))
                    for i in range(NT):
                        if i:
                            pe.wait_ge(b_hm, 2)
                        for h in range(2):
                            for c in range(4):
                                ins = nt.matmul(ps[:, 4 + 2 * i + h, :], onT[:, c, i * 128:i * 128 + 128],
                                                unit(K_BR_NSA)[:, c, h * 512:h * 512 + 512], start=c == 0, stop=c == 3)
                        ins.then_inc(b_m, 1)
                    for t in range(KC):
                        for i in range(NT):
                            pe.wait_ge(b_mx, i + 1)
                            ins = nt.transpose(ps[:, t // 2, (t % 2) * 256 + i * 128:(t % 2) * 256 + i * 128 + 128],
                                               mrg[:, i, t * 128:t * 128 + 128], ident)
                        if t % 2:
                            ins.then_inc(b_t, 1)
                    pe.wait_ge(units_used, K_BR_NSA)
                    pe.sem_inc(units_used, 1)
                    for i in range(NT):
                        for k in range(2):
                            unit_arrived(pe, K_OUT + k)
                            for h in range(2):
                                for c in range(4):
                                    if i == 0 and h == 0:
                                        pe.wait_ge(b_tk, 2 * k + c // 2 + 1)
                                    ins = nt.matmul(ps[:, 4 + 2 * i + h, :], hT[:, 4 * k + c, i * 128:i * 128 + 128],
                                                    unit(K_OUT + k)[:, c, h * 512:h * 512 + 512], start=k == 0 and c == 0,
                                                    stop=k == 1 and c == 3)
                        ins.then_inc(b_o, 1)
                    pe.wait_ge(b_o, 2)
                    pe.sem_inc(units_used, 2)

                follow(dict(F=F, A=Ada, H=H, Ho=Ho, Ht=Ht, Nqk=Nqk, Nkv=Nkv, Ncmp=Ncmp, Nkc=Nkc, Nsc=Nsc, Npc=Npc, M=M, Q=Q,
                            Bh=Bh, Nout=Nout, Bn=Bn))
        p1.close()
        def mixture(tag, base, per_pair, w_src, router, bias, topk, first, norm, after, acc_in_x, beside={}):
            m = ExitStack()
            nr = 36 if first else 32
            FT = 4 if first else 8
            UP = 6 - 2 if first else 8
            BU = 2 if first else 4
            A0, C0 = 4, 6
            def s(n):
                return S(tag + n)

            wr = sbuf(m, tag + "wr", [128, KC, nr])
            brow = sbuf(m, tag + "brow", [1, nr])
            lgE = sbuf(m, tag + "lgE", [128, NT, 32])
            ex = sbuf(m, tag + "ex", [128, NT, 36])
            rk = sbuf(m, tag + "rk", [128, NT, 36])
            sel = sbuf(m, tag + "sel", [128, NT, 32])
            comb = sbuf(m, tag + "comb", [128, NT, 32])
            posx = sbuf(m, tag + "posx", [128, NT, 34])
            rs = sbuf(m, tag + "rs", [128, 16])
            cnt = sbuf(m, tag + "cnt", [128, 1], I32)
            hTf = hT[:].rearrange("p t q -> p (t q)")
            if not first:
                b1s = sbuf(m, "b1s", [32, 2048])
                b2s = wf[0:32, 3072:4096]
                cT = sbuf(m, "cT", [32, T])
                tie32 = wf[:, 4096:5120]
            e3 = ex[:].rearrange("p i n -> p (i n)")
            exE, exG = e3[:, 0:64], e3[:, 64:72]
            r3 = rk[:].rearrange("p i n -> p (i n)")
            rkE, rkG = r3[:, 0:64], r3[:, 64:72]
            q_in, q_lg, q_ex, q_exd, q_sel, q_pos, q_cnt, q_bT, q_bTk, q_b2, q_acc = (
                s("router_in"), s("logits"), s("shifted"), s("exp"), s("selected"), s("positions"), s("slots"),
                s("combT"), s("combT_kept"), s("bias_out"), s("acc_set"))
            acc = X if acc_in_x else wf[:, 0:2048].rearrange("p (i d) -> p i d", i=NT)
            def also(part, eng):
                if part in beside:
                    beside[part](eng)

            with nc.Block() as block:
                @block.sync
                def _(sp):
                    also("router_sync", sp)
                    sp.wait_ge(q_in, 64 if first else 80)
                    for k in range(base + (4 if first else 3), base + RING):
                        load_unit(sp, k)

                @block.gpsimd
                def _(g):
                    also("router_gpsimd", g)

                @block.scalar
                def _(a):
                    a.dma_start(wr[:, :, 0:nr - 32], A["w_grp"][0].rearrange("(p t) n -> p t n", t=KC)).then_inc(q_in, 16) if first else None
                    a.dma_start(wr[:, :, nr - 32:nr], A[router][0].rearrange("(p t) n -> p t n", t=KC)).then_inc(q_in, 16)
                    if first:
                        a.dma_start(brow[:, 0:4], A["b_grp"]).then_inc(q_in, 16)
                    a.dma_start(brow[:, nr - 32:nr], A[bias]).then_inc(q_in, 16)
                    if not first:
                        a.dma_start(b1s[:], A["b1_2"][0]).then_inc(q_in, 16)
                        a.dma_start(b2s, A["b2_2"][0]).then_inc(q_in, 16)
                        a.dma_start(tie32, A["cst"][:, CO["tie32"][0]:]).then_inc(q_in, 16)
                    norm.act(a)
                    also("router_act", a)
                    a.wait_ge(q_ex, 1)
                    w = 72 if first else 64
                    nc.scalar.activation(e3[:, 0:w], e3[:, 0:w], ACT.Exp).then_inc(q_exd, 1)
                    if not first:
                        a.wait_ge(q_bT, 1)
                        nc.scalar.activation(cT[:], ps[0:32, 6, 0:T], ACT.Copy).then_inc(q_bTk, 1)
                    also("router_act_end", a)

                @block.vector
                def _(v):
                    link = chain(v, "v_chain")
                    nv = nc.vector
                    v.wait_ge(s_grow, 16 * norm.gains)
                    norm.dve(v, link)
                    v.wait_ge(q_lg, 1)
                    lp = ps[:, 4, 0:128].rearrange("p (i n) -> p i n", i=NT)
                    lg = lgE[:]
                    link(nv.tensor_copy(lg, lp[:, :, nr - 32:nr]))
                    n = 8 if first else 32
                    lv = lg.rearrange("p i (g n) -> p (i g) n", n=n)
                    G = 64 // n
                    mx = rs[:, 0:G]
                    link(nv.tensor_reduce(mx, lv, AX.X, ALU.max))
                    ins = nv.tensor_tensor(exE.rearrange("p (g n) -> p g n", n=n), lv,
                                           bc(mx.rearrange("p (g n) -> p g n", n=1), [128, G, n]), ALU.subtract)
                    if first:
                        lgG = rkG.rearrange("p (i n) -> p i n", i=NT)
                        link(nv.tensor_copy(lgG, lp[:, :, 0:4]))
                        link(nv.tensor_reduce(rs[:, 8:10], lgG, AX.X, ALU.max))
                        ins = nv.tensor_tensor(exG.rearrange("p (i n) -> p i n", i=NT), lgG,
                                               bc(rs[:, 8:10].rearrange("p (i n) -> p i n", n=1), [128, NT, 4]), ALU.subtract)
                    ins.then_inc(q_ex, 1)

                    def rank(out, l, g, k):
                        b1_ = hTf[:, 0:g * k * k].rearrange("p (g i j) -> p g i j", g=g, i=k)
                        b2_ = hTf[:, 1024:1024 + g * k * k].rearrange("p (g i j) -> p g i j", g=g, i=k)
                        lj = bc(l.rearrange("p g (a j) -> p g a j", a=1), [128, g, k, k])
                        li = bc(l.rearrange("p g (i a) -> p g i a", a=1), [128, g, k, k])
                        tie = bc((tie32 if k == 32 else K(f"tie{k}")).rearrange("p (g i j) -> p g i j", g=1, i=k), [128, g, k, k])
                        nv.tensor_tensor(b1_, lj, li, ALU.is_gt)
                        link(nv.tensor_tensor(b2_, lj, li, ALU.is_equal))
                        link(nv.tensor_tensor(b2_, b2_, tie, ALU.mult))
                        link(nv.tensor_tensor(b1_, b1_, b2_, ALU.add))
                        link(nv.tensor_reduce(out, b1_, AX.X, ALU.add))

                    if first:
                        rank(rkE.rearrange("p (g i) -> p g i", g=G), lv, G, n)
                        gl = rs[:, 0:8].rearrange("p (i n) -> p i n", i=NT)
                        link(nv.tensor_copy(gl, rkG.rearrange("p (i n) -> p i n", i=NT)))
                        rank(rkG.rearrange("p (i n) -> p i n", i=NT), gl, NT, 4)
                        link(nv.tensor_scalar(rkG, rkG, 0.5, None, ALU.is_lt))
                        link(nv.tensor_scalar(rkE, rkE, topk - 0.5, None, ALU.is_lt))
                        link(nv.tensor_tensor(sel[:].rearrange("p i (g n) -> p (i g) n", n=8), rkE.rearrange("p (g n) -> p g n", n=8),
                                              bc(rkG.rearrange("p (g n) -> p g n", n=1), [128, 8, 8]), ALU.mult))
                    else:
                        for i in range(NT):
                            rank(rkE[:, 32 * i:32 * i + 32].rearrange("p (g i) -> p g i", g=1), lv[:, i:i + 1], 1, 32)
                        link(nv.tensor_scalar(sel[:].rearrange("p i n -> p (i n)"), rkE, topk - 0.5, None, ALU.is_lt))
                    nv.nop().then_inc(q_sel, 1)
                    v.wait_ge(q_exd, 1)
                    link(nv.tensor_tensor(comb[:], sel[:], exE.rearrange("p (i n) -> p i n", i=NT), ALU.mult))
                    link(nv.tensor_reduce(rs[:, 0:2], comb[:], AX.X, ALU.add))
                    if first:
                        link(nv.tensor_reduce(rs[:, 2:4], exG.rearrange("p (i n) -> p i n", i=NT), AX.X, ALU.add))
                        link(nv.tensor_tensor(rs[:, 0:2], rs[:, 0:2], rs[:, 2:4], ALU.mult))
                    link(nv.reciprocal(rs[:, 4:6], rs[:, 0:2]))
                    nv.tensor_tensor(comb[:], comb[:], bc(rs[:, 4:6].rearrange("p (i n) -> p i n", n=1), [128, NT, 32]),
                                     ALU.mult).then_inc(q_sel, 1)
                    link(nv.memset(posx[:], -1.0))
                    v.wait_ge(q_pos, 1)
                    po = posx[:, :, 0:32]
                    link(nv.tensor_scalar(po, ps[:, 5, 0:64].rearrange("p (i n) -> p i n", i=NT), 1.0, None, ALU.add))
                    link(nv.tensor_tensor(po, po, sel[:], ALU.mult))
                    link(nv.tensor_scalar(po, po, -1.0, None, ALU.add))
                    link(nv.tensor_reduce(rs[:, 6:7], ps[:, 5, 64:96], AX.X, ALU.max))
                    nv.tensor_copy(cnt[:], rs[:, 6:7]).then_inc(q_cnt, 1)
                    if not first:
                        v.wait_ge(q_b2, 1)
                        for i in range(NT):
                            nv.tensor_copy(acc[:, i, :], ps[:, 2 * i:2 * i + 2, :].rearrange("p b c -> p (b c)")).then_inc(q_acc, 1)
                    also("router_vector_end", v)

                @block.tensor
                def _(pe):
                    nt = nc.tensor
                    norm.pe(pe)
                    also("router_pe", pe)
                    pe.wait_ge(norm.ev, 4)
                    pe.wait_ge(q_in, 64 if first else 80)
                    for i in range(NT):
                        for t in range(KC):
                            nt.matmul(ps[:, 4, 64 * i:64 * i + nr], hT[:, t, i * 128:i * 128 + 128], wr[:, t, :], start=t == 0, stop=False)
                        ins = nt.matmul(ps[:, 4, 64 * i:64 * i + nr], K("ones", 1), brow[:], start=False, stop=True)
                    ins.then_inc(q_lg, 1)
                    pe.wait_ge(q_sel, 1)
                    nt.matmul(ps[:, 5, 0:32], K("before"), sel[:, 0, :], start=True, stop=True)
                    nt.matmul(ps[:, 5, 32:64], K("before"), sel[:, 1, :], start=True, stop=False)
                    nt.matmul(ps[:, 5, 32:64], K("ones"), sel[:, 0, :], start=False, stop=True)
                    nt.matmul(ps[:, 5, 64:96], K("ones"), sel[:, 0, :], start=True, stop=False)
                    nt.matmul(ps[:, 5, 64:96], K("ones"), sel[:, 1, :], start=False, stop=True).then_inc(q_pos, 1)
                    if not first:
                        pe.wait_ge(q_sel, 2)
                        for i in range(NT):
                            ins = nt.transpose(ps[0:32, 6, i * 128:i * 128 + 128], comb[:, i, :], ident)
                        ins.then_inc(q_bT, 1)
                        pe.wait_ge(q_bTk, 1)
                        for i in range(NT):
                            for h in range(2):
                                ins = nt.matmul(ps[:, 2 * i + h, :], cT[:, i * 128:i * 128 + 128], b2s[:, 512 * h:512 * h + 512],
                                                start=True, stop=True)
                        ins.then_inc(q_b2, 1)

            Pm = sbuf(m, tag + "Pm", [128, NT, 128])
            Pg = sbuf(m, tag + "Pg", [128, NT, 128])
            xgT = hTf[:, 0:1024].rearrange("p (t c) -> p t c", t=KC)
            GT = sbuf(m, tag + "GT", [128, NT, 128])
            sg = sbuf(m, tag + "sg", [128, 512 * BU // 2])
            hid = sbuf(m, tag + "hid", [128, FT, 128])
            hidT = sbuf(m, tag + "hidT", [128, FT, 128])
            y = hTf[:, 1024:2048]
            if not first:
                gm = wf[:, 2048:3072]
                um = junk
                pick = sbuf(m, "pick", [32, 128])

            def rounds(pre, used, ready_value, ready, used_base):
                def z(n):
                    return S(tag + pre + n)
                p_ready, pg_ready, pick_ready, gathered, xg_kept, gatesT, gt_kept = (
                    z("onehot_ready"), z("weighted_ready"), z("pick_ready"), z("gathered"), z("gathered_kept"), z("weightsT"), z("weightsT_kept"))
                act1, clip, hid_ready, hid_tr, hid_kept, y_act, y_dve, scat, acc_a, acc_c = (
                    z("activated"), z("clipped"), z("hidden_ready"), z("hiddenT"), z("hiddenT_kept"), z("y_low_kept"), z("y_high_kept"),
                    z("scattered"), z("added_tile0"), z("added_tile1"))

                def onehot(v, dst, p2):
                    for i in range(NT):
                        ins = nc.vector.tensor_tensor(dst[:, i, :].rearrange("p (e c) -> p e c", e=2),
                                                      K("iota").rearrange("p (e c) -> p e c", e=2),
                                                      bc(posx[:, i, p2].rearrange("p (e c) -> p e c", c=1), [128, 2, 64]), ALU.is_equal)
                    return ins

                def gather(pe):
                    for t in range(KC):
                        for i in range(NT):
                            ins = nc.tensor.matmul(ps[:, A0 + t // 4, (t % 4) * 128:(t % 4) * 128 + 128], hn[:, i, t, :], Pm[:, i, :],
                                                   start=i == 0, stop=i == NT - 1)
                    ins.then_inc(gathered, 1)

                def gather_kept(a):
                    for b in range(2):
                        ins = nc.scalar.activation(xgT[:, 4 * b:4 * b + 4, :].rearrange("p t c -> p (t c)"), ps[:, A0 + b, :], ACT.Copy)
                    ins.then_inc(xg_kept, 1)

                def up_used(it, n):
                    return it * per_pair + (used_base + n)

                def pe_credit(pe):
                    pe.sem_inc(gatesT, 1)

                def pe_start(pe, it, g):
                    pe.wait_ge(p_ready, g + 1)
                    if pre:
                        pe.wait_ge(acc_a, it + 1)
                        pe.wait_ge(gatesT, it + 1)
                    gather(pe)

                def pe_pair(pe, it, g):
                    nt = nc.tensor
                    pe.wait_ge(xg_kept, g + 1)
                    pe.wait_ge(hid_ready, it + 1)
                    if not first:
                        pe.wait_ge(pick_ready, g + 1)
                        for b in range(4):
                            nt.matmul(ps[:, b, :], pick[:], b1s[:, 512 * b:512 * b + 512], start=True, stop=False, skip_group_check=True)

                    def arrived(j):
                        pe.wait_ge(ready[(base + j) % RING], ready_value(it, j))
                    for u in range(UP // 2):
                        arrived(2 * u)
                        arrived(2 * u + 1)
                        for t in range(KC if first else 2):
                            for b in range(1 if first else 4):
                                for e in range(2):
                                    w = ring[:, (base + 2 * u + e) % RING, :]
                                    if first:
                                        ins = nt.matmul(ps[64 * e:64 * e + 64, u, :], xgT[:, t, 64 * e:64 * e + 64], w[:, 512 * t:512 * t + 512],
                                                        start=t == 0, stop=t == KC - 1, skip_group_check=True)
                                    else:
                                        c = 2048 * t + 512 * b
                                        ins = nt.matmul(ps[64 * e:64 * e + 64, b, :], xgT[:, 2 * u + t, 64 * e:64 * e + 64], w[:, c:c + 512],
                                                        start=False, stop=u == 3 and t == 1, skip_group_check=True)
                        ins.then_inc(used, 2)
                    pe.wait_ge(p_ready, g + 2)
                    pe.wait_ge(acc_a, it + 1)
                    gather(pe)
                    pe.wait_ge(xg_kept, g + 2)
                    pe.wait_ge(pg_ready, it + 1)
                    for i in range(NT):
                        ins = nt.transpose(ps[:, A0, i * 128:i * 128 + 128], Pg[:, i, :], ident)
                    ins.then_inc(gatesT, 1)
                    pe.wait_ge(hid_ready, it + 2)
                    pe.wait_ge(acc_c, it + 1)
                    for t in range(FT):
                        ins = nt.transpose(ps[:, C0 + t // 4, (t % 4) * 128:(t % 4) * 128 + 128], hid[:, t, :], ident)
                    ins.then_inc(hid_tr, 1)
                    pe.wait_ge(hid_kept, it + 1)
                    for u in range((per_pair - UP) // 2):
                        j = UP + 2 * u
                        arrived(j)
                        arrived(j + 1)
                        for t in range(4):
                            for h in range(2):
                                for e in range(2):
                                    w = ring[:, (base + j + e) % RING, :]
                                    c = 1024 * t + 512 * h
                                    ins = nt.matmul(ps[64 * e:64 * e + 64, C0 + h, :], hidT[:, 4 * u + t, 64 * e:64 * e + 64], w[:, c:c + 512],
                                                    start=u == 0 and t == 0, stop=4 * u + t == FT - 1, skip_group_check=True)
                        ins.then_inc(used, 2)
                    pe.wait_ge(y_act, it + 1)
                    pe.wait_ge(y_dve, it + 1)
                    pe.wait_ge(gt_kept, it + 1)
                    for i in range(NT):
                        for h in range(2):
                            ins = nt.matmul(ps[:, (A0, C0)[i] + h, :], GT[:, i, :], y[:, 512 * h:512 * h + 512], start=True, stop=True)
                        ins.then_inc(scat, 1)

                def act_start(a, it, g):
                    a.wait_ge(gathered, g + 1)
                    gather_kept(a)

                def act_pair(a, it, g):
                    na = nc.scalar
                    if first:
                        a.wait_ge(used, up_used(it, 2))
                        na.activation(sg[:], ps[:, 0, :], ACT.Silu).then_inc(act1, 1)
                    else:
                        a.wait_ge(clip, it + 1)
                        na.activation(sg[:], gm, ACT.Sigmoid, scale=1.702).then_inc(act1, 1)
                    a.wait_ge(gathered, g + 2)
                    gather_kept(a)
                    a.wait_ge(hid_tr, it + 1)
                    for b in range(FT // 4):
                        ins = na.activation(hidT[:, 4 * b:4 * b + 4, :].rearrange("p t c -> p (t c)"), ps[:, C0 + b, :], ACT.Copy)
                    ins.then_inc(hid_kept, 1)
                    a.wait_ge(used, up_used(it, per_pair))
                    na.activation(y[:, 0:512], ps[:, C0, :], ACT.Copy).then_inc(y_act, 1)

                def dve_credit(v):
                    v.sem_inc(hid_ready, 1)
                    v.sem_inc(acc_a, 1)
                    v.sem_inc(acc_c, 1)

                def dve_pick(v, p2):
                    if not first:
                        nc.vector.tensor_copy(pick[:].rearrange("p (e c) -> p e c", e=2),
                                              bc(K("ident", 32)[:, p2].rearrange("p (e c) -> p e c", c=1), [32, 2, 64])).then_inc(pick_ready, 1)

                def dve_start(v, it, g):
                    if pre:
                        v.wait_ge(acc_c, it + 1)
                    onehot(v, Pm, slice(0, 2)).then_inc(p_ready, 1)
                    dve_pick(v, slice(0, 2))

                def dve_pair(v, link, it, g, p):
                    nv = nc.vector
                    e_now = v.snap(2 * p)
                    e_next = v.snap(2 * p + 2)
                    v.wait_ge(gathered, g + 1)
                    onehot(v, Pm, bass.ds(e_next, 2)).then_inc(p_ready, 1)
                    v.wait_ge(gatesT, it + 1)
                    onehot(v, Pg, bass.ds(e_now, 2)).then_inc(s("eq"), 1)
                    v.wait_ge(s("eq"), 1)
                    v.sem_clear(s("eq"))
                    for i in range(NT):
                        pv = Pg[:, i, :].rearrange("p (e c) -> p e c", e=2)
                        ins = nv.tensor_tensor(pv, pv, bc(comb[:, i, bass.ds(e_now, 2)].rearrange("p (e c) -> p e c", c=1), [128, 2, 64]), ALU.mult)
                    ins.then_inc(pg_ready, 1)
                    hv = hid[:].rearrange("q t p -> q p t")
                    if first:
                        v.wait_ge(act1, it + 1)
                        v.wait_ge(used, up_used(it, 4))
                        nv.tensor_tensor(hv, sg[:].rearrange("q (p t) -> q p t", t=FT), ps[:, 1, :].rearrange("q (p t) -> q p t", t=FT),
                                         ALU.mult).then_inc(hid_ready, 1)
                    else:
                        v.wait_ge(used, up_used(it, 8))
                        nv.tensor_scalar(gm, ps[:, 0:2, :].rearrange("p b c -> p (b c)"), 7.0, None, ALU.min).then_inc(clip, 1)
                        dve_pick(v, bass.ds(e_next, 2))
                        nv.tensor_scalar(um[:], ps[:, 2:4, :].rearrange("p b c -> p (b c)"), 7.0, -7.0, ALU.min, ALU.max)
                        v.wait_ge(act1, it + 1)
                        nv.tensor_tensor(gm, gm, sg[:], ALU.mult).then_inc(s("glu"), 1)
                        v.wait_ge(s("glu"), 1)
                        v.sem_clear(s("glu"))
                        nv.scalar_tensor_tensor(out=hv, in0=um[:].rearrange("q (p t) -> q p t", t=FT), scalar=1.0,
                                                in1=gm.rearrange("q (p t) -> q p t", t=FT), op0=ALU.add, op1=ALU.mult).then_inc(hid_ready, 1)
                    v.wait_ge(gatesT, it + 2)
                    nv.tensor_copy(GT[:].rearrange("p i c -> p (i c)"), ps[:, A0, 0:256]).then_inc(gt_kept, 1)
                    v.wait_ge(used, up_used(it, per_pair))
                    nv.tensor_copy(y[:, 512:1024], ps[:, C0 + 1, :]).then_inc(y_dve, 1)
                    for i, (b, sm_) in enumerate(((A0, acc_a), (C0, acc_c))):
                        v.wait_ge(scat, it * 2 + (i + 1))
                        nv.tensor_tensor(acc[:, i, :], acc[:, i, :], ps[:, b:b + 2, :].rearrange("p b c -> p (b c)"), ALU.add).then_inc(sm_, 1)

                return pe_credit, pe_start, pe_pair, act_start, act_pair, dve_credit, dve_start, dve_pair

            n6 = per_pair // RING
            main = rounds("", units_used, lambda it, j: it * (16 * n6) + 16 * ((base + j) // RING + 1), ring_ready, base)
            o_used = s("more_used")
            o_ready = [s(f"more_ready{j}") for j in range(RING)]
            more = rounds("more_", o_used, lambda it, j: it * (16 * n6) + 16 * (j // RING + 1), o_ready, RING)
            full_used = base + per_pair * PAIRS

            def pairs(eng, body):
                with eng.Fori(0, PAIRS) as p:
                    body(p)

            def more_rounds(eng, credit, start, body, flag_wait=True):
                most = eng.value_load(cnt[0:1, 0:1], min_val=0, max_val=T)
                with eng.If(most > CAP):
                    credit()
                    with eng.Fori(0, ROUNDS - 1) as r:
                        start(r)
                        if body is not None:
                            with eng.Fori(0, PAIRS) as p:
                                body(eng.snap(r * PAIRS + p), eng.snap(r * (PAIRS + 1) + p), p)

            with nc.Block() as block:
                @block.sync
                def _(sp):
                    def load(sem_ready, sem_used, k_used, e0, j):
                        e0 = sp.snap(e0)
                        sp.wait_ge(sem_used, k_used)
                        sp.dma_start(ring[:, (base + j) % RING, :], w_src(e0, j)).then_inc(sem_ready[(base + j) % RING], 16)
                    with sp.Fori(0, PAIRS - 1) as p:
                        for j in range(RING, per_pair):
                            load(ring_ready, units_used, sp.snap(p * per_pair + (base + j - RING + 1)), 2 * p, j)
                        for j in range(RING):
                            load(ring_ready, units_used, sp.snap(p * per_pair + (base + per_pair + j - RING + 1)), 2 * p + 2, j)
                    for j in range(RING, per_pair):
                        k = base + (PAIRS - 1) * per_pair + j
                        sp.wait_ge(units_used, k - RING + 1)
                        sp.dma_start(ring[:, k % RING, :], w_src(2 * PAIRS - 2, j)).then_inc(ring_ready[k % RING], 16)
                    sp.wait_ge(units_used, full_used)
                    most = sp.value_load(cnt[0:1, 0:1], min_val=0, max_val=T)
                    with sp.If(most > CAP):
                        with sp.Fori(0, ROUNDS - 1) as r:
                            with sp.Fori(0, PAIRS) as p:
                                for j in range(per_pair):
                                    load(o_ready, o_used, sp.snap(r * (PAIRS * per_pair) + p * per_pair + (j + 1)), 2 * p, j)
                        for j in range(RING):
                            sp.wait_ge(o_used, RING + (ROUNDS - 1) * PAIRS * per_pair)
                    after(sp)

                @block.gpsimd
                def _(g):
                    also("experts_gpsimd", g)

                @block.tensor
                def _(pe):
                    credit, start, pair = main[0:3]
                    credit(pe)
                    start(pe, 0, 0)
                    pairs(pe, lambda p: pair(pe, p, p))
                    credit_, start_, pair_ = more[0:3]

                    def credit_more():
                        pe.wait_ge(units_used, full_used)
                        credit_(pe)
                        pe.sem_inc(o_used, RING)
                    more_rounds(pe, credit_more, lambda r: start_(pe, pe.snap(r * PAIRS), pe.snap(r * (PAIRS + 1))),
                                lambda it, g, p: pair_(pe, it, g))

                @block.scalar
                def _(a):
                    main[3](a, 0, 0)
                    pairs(a, lambda p: main[4](a, p, p))
                    more_rounds(a, lambda: None, lambda r: more[3](a, r * PAIRS, a.snap(r * (PAIRS + 1))),
                                lambda it, g, p: more[4](a, it, g))

                @block.vector
                def _(v):
                    link = None
                    main[5](v)
                    main[6](v, 0, 0)
                    pairs(v, lambda p: main[7](v, link, p, p, p))
                    lv = chain(v, "v_chain")

                    def next_round(r):
                        v.wait_ge(S(tag + "more_added_tile1"), v.snap(r * PAIRS + 1))
                        nc.vector.tensor_scalar(posx[:], posx[:], -float(CAP), None, ALU.add).then_inc(S(tag + "round_set"), 1)
                        v.wait_ge(S(tag + "round_set"), r + 1)
                        more[6](v, v.snap(r * PAIRS), v.snap(r * (PAIRS + 1)))
                    more_rounds(v, lambda: more[5](v), next_round, lambda it, g, p: more[7](v, link, it, g, p))
            return m, acc

        first_block = finished()
        s5 = ExitStack()
        VT = sbuf(s5, "VT", [128, 57])
        zc = sbuf(s5, "zc", [128, 12, 16])
        BT = sbuf(s5, "BT", [128, 2, 4, 128])
        CT = sbuf(s5, "CT", [128, 2, 4, 128])
        Wp = sbuf(s5, "Wp", [128, 2, 16, T])
        wf = Wp[:].rearrange("p k j t -> p (k j t)")
        mod2 = wf[:, 5120:8192]
        p2 = ExitStack()
        mod = sbuf(p2, "mod", [128, 3 * D])
        f_in = S("mod_bias_in")
        s5t = ExitStack()
        SV = sbuf(s5t, "SV", [57, 128])
        ldr = sbuf(s5t, "ldr", [48, 2])
        Bn = sbuf(s5t, "Bn", [128, 2, 16, 16])
        Cn = sbuf(s5t, "Cn", [128, 2, 4, 64])
        Bp = BT[:].rearrange("p k q c -> p (k q c)").rearrange("p (k j g c) -> p k j g c", k=2, j=16, g=2)
        Cp = CT
        zr_, zi_, dec, sn, cs_, re, im, cr, ci, t1_, t2_, dt_ = (zc[:, i, :] for i in range(12))
        TWO_PI = 2 * np.pi
        f_sv, f_ld, z_vt, z_vtk, z_e, z_ek, z_den, z_rec, z_bc = (S(n) for n in (
            "ssm_vectors_in", "dt_spread", "ssm_vectorsT", "ssm_vectorsT_kept", "lam_ready", "lam_acted", "lam_square", "lam_inverse", "bc_built"))

        def z_loads(sp):
            for r0, n, ap in ((0, 16, A["ssm_a_re_2"][0].rearrange("(j g) p -> j (g p)", j=16)),
                              (16, 16, A["ssm_a_im_2"][0].rearrange("(j g) p -> j (g p)", j=16)),
                              (48, 4, A["ssm_d_2"][0].rearrange("(j c) -> j c", j=4)),
                              (52, 4, A["b_glu_2"][0].rearrange("(j c) -> j c", j=4)),
                              (56, 1, A["subln_g_2"])):
                sp.dma_start(SV[r0:r0 + n, :], ap).then_inc(f_sv, 16)
            sp.dma_start(mod[:], A["b_ada_2"][:, 0:3 * D].to_broadcast([128, 3 * D])).then_inc(f_in, 16)
            sp.dma_start(ldr[32:48, :], A["ssm_log_dt_2"][0].rearrange("(j g) -> j g", j=16)).then_inc(f_sv, 16)
            for i, n in enumerate(("ssm_b_re_2", "ssm_b_im_2")):
                sp.dma_start(Bn[:, i], A[n][0].rearrange("(j g) p c -> (g p) j c", j=16)).then_inc(f_sv, 16)
            for i, n in enumerate(("ssm_c_re_2", "ssm_c_im_2")):
                sp.dma_start(Cn[:, i], A[n][0].rearrange("(j g) c p -> (g c) j p", j=4)).then_inc(f_sv, 16)

        def z_pe(pe):
            pe.wait_ge(f_ld, 1)
            nc.tensor.transpose(ps[:, 6, 0:57], SV[:], K("ident", 57)[:, 0:57]).then_inc(z_vt, 1)

        def z_act(a):
            a.wait_ge(z_vt, 1)
            nc.scalar.activation(VT[:], ps[:, 6, 0:57], ACT.Copy).then_inc(z_vtk, 1)
            a.wait_ge(z_vtk, 1)
            nc.scalar.activation(dt_, VT[:, 32:48], ACT.Exp).then_inc(z_vtk, 1)

        def z_act_end(a):
            na = nc.scalar
            a.wait_ge(z_e, 1)
            na.activation(dec, zr_, ACT.Exp).then_inc(z_ek, 1)
            a.wait_ge(z_e, 2)
            na.activation(sn, t1_, ACT.Sin).then_inc(z_ek, 1)
            na.activation(cs_, t1_, ACT.Sin, scale=0.5).then_inc(z_ek, 1)

        def z_gpsimd(g):
            link = chain(g, "zg_chain")
            ng = nc.gpsimd
            g.wait_ge(f_sv, 16 * 10)
            ng.tensor_copy(SV[32:48, :].rearrange("j (g p) -> j g p", g=2),
                           bc(ldr[32:48, :].rearrange("j (g p) -> j g p", p=1), [16, 2, 64])).then_inc(f_ld, 1)
            g.wait_ge(z_vtk, 2)
            link(ng.tensor_scalar(re, VT[:, 0:16], -1e-4, None, ALU.min))
            link(ng.tensor_copy(im, VT[:, 16:32]))
            link(ng.tensor_tensor(zi_, im, dt_, ALU.mult))
            ng.tensor_tensor(zr_, re, dt_, ALU.mult).then_inc(z_e, 1)
            link(ng.tensor_scalar(t1_, zi_, 1.0 / TWO_PI, 12582912.0, ALU.mult, ALU.add))
            link(ng.tensor_scalar(t1_, t1_, -12582912.0, None, ALU.add))
            for c in (6.28125, 0.0019350051879882812, TWO_PI - 6.28125 - 0.0019350051879882812):
                link(ng.tensor_scalar(t2_, t1_, -c, None, ALU.mult))
                link(ng.tensor_tensor(zi_, zi_, t2_, ALU.add))
            ng.tensor_scalar(t1_, zi_, 3.1415925, -3.1415925, ALU.min, ALU.max).then_inc(z_e, 1)
            g.wait_ge(z_ek, 3)
            link(ng.tensor_tensor(cs_, cs_, cs_, ALU.mult))
            link(ng.tensor_scalar(cs_, cs_, -2.0, 1.0, ALU.mult, ALU.add))
            link(ng.tensor_tensor(t1_, re, re, ALU.mult))
            link(ng.tensor_tensor(t2_, im, im, ALU.mult))
            ng.tensor_tensor(t1_, t1_, t2_, ALU.add).then_inc(z_den, 1)

        def z_vector_end(v):
            v.wait_ge(z_den, 1)
            nc.vector.reciprocal(dt_, t1_).then_inc(z_rec, 1)

        def z_tables(g):
            clear(g, first_block)
            link = chain(g, "zg_chain")
            ng = nc.gpsimd
            g.wait_ge(z_rec, 1)
            link(ng.tensor_tensor(cr, dec, cs_, ALU.mult))
            link(ng.tensor_scalar(cr, cr, -1.0, None, ALU.add))
            link(ng.tensor_tensor(ci, dec, sn, ALU.mult))
            link(ng.tensor_tensor(t1_, cr, re, ALU.mult))
            link(ng.tensor_tensor(t2_, ci, im, ALU.mult))
            link(ng.tensor_tensor(zr_, t1_, t2_, ALU.add))
            link(ng.tensor_tensor(t1_, ci, re, ALU.mult))
            link(ng.tensor_tensor(t2_, cr, im, ALU.mult))
            link(ng.tensor_tensor(zi_, t1_, t2_, ALU.subtract))
            link(ng.tensor_tensor(zr_, zr_, dt_, ALU.mult))
            link(ng.tensor_tensor(zi_, zi_, dt_, ALU.mult))
            zrb = bc(zr_.rearrange("p (j c) -> p j c", c=1), [128, 16, 16])
            zib = bc(zi_.rearrange("p (j c) -> p j c", c=1), [128, 16, 16])
            tmp = junk[:, 0:512].rearrange("p (k j c) -> p k j c", k=2, j=16)
            for k, (x, y_, op) in enumerate(((0, 1, ALU.subtract), (1, 0, ALU.add))):
                ng.tensor_tensor(tmp[:, 0], Bn[:, x], zrb, ALU.mult)
                link(ng.tensor_tensor(tmp[:, 1], Bn[:, y_], zib, ALU.mult))
                link(ng.tensor_tensor(tmp[:, 0], tmp[:, 0], tmp[:, 1], op))
                ng.tensor_scalar(Bp[:, k, :, 0, :], tmp[:, 0], K("even"), None, ALU.mult)
                link(ng.tensor_scalar(Bp[:, k, :, 1, :], tmp[:, 0], K("odd"), None, ALU.mult))
            for k in range(2):
                ng.tensor_scalar(Cp[:, k, :, 0:64], Cn[:, k], K("geven"), None, ALU.mult)
                link(ng.tensor_scalar(Cp[:, k, :, 64:128], Cn[:, k], K("godd"), None, ALU.mult))
            for j8 in (slice(0, 8), slice(8, 16)):
                def col(ap, n):
                    return bc(ap.rearrange("p (j n) -> p j n", n=1), [128, 8, n])
                wr_, wi_ = cs_[:, j8], sn[:, j8]
                x_, y_, w_ = t1_[:, 0:8], t2_[:, 0:8], dt_[:, 0:8]
                ng.memset(Wp[:, 0, j8, 0:1], 1.0)
                link(ng.memset(Wp[:, 1, j8, 0:1], 0.0))
                n = 1
                while n < T:
                    a_r, a_i = Wp[:, 0, j8, 0:n], Wp[:, 1, j8, 0:n]
                    o_r, o_i = Wp[:, 0, j8, n:2 * n], Wp[:, 1, j8, n:2 * n]
                    u_ = [b[:, 0:8 * n].rearrange("p (j t) -> p j t", j=8) for b in (junk, grow)]
                    ng.tensor_tensor(o_r, a_r, col(wr_, n), ALU.mult)
                    ng.tensor_tensor(u_[0], a_i, col(wi_, n), ALU.mult)
                    ng.tensor_tensor(o_i, a_r, col(wi_, n), ALU.mult)
                    link(ng.tensor_tensor(u_[1], a_i, col(wr_, n), ALU.mult))
                    ng.tensor_tensor(o_r, o_r, u_[0], ALU.subtract)
                    link(ng.tensor_tensor(o_i, o_i, u_[1], ALU.add))
                    n *= 2
                    if n < T:
                        ng.tensor_tensor(x_, wr_, wr_, ALU.mult)
                        ng.tensor_tensor(y_, wi_, wi_, ALU.mult)
                        link(ng.tensor_tensor(w_, wr_, wi_, ALU.mult))
                        link(ng.tensor_tensor(wr_, x_, y_, ALU.subtract))
                        link(ng.tensor_tensor(wi_, w_, w_, ALU.add))
            ng.nop().then_inc(z_bc, 1)

        n1 = Norm("n1")
        n1.gains = 2

        def after1(sp):
            sp.wait_ge(z_bc, 1)
            sp.dma_start(grow[:], A["final_norm"].rearrange("(a d) -> a d", a=1).to_broadcast([128, D])).then_inc(s_grow, 16)
            for k in range(K_IN2, K_IN2 + 3):
                load_unit(sp, k)
        m, _ = mixture("m1_", K_MOE1, 6, moe1_src, "w_rtr", "b_rtr", 2, True, n1, after1, True,
                       dict(router_sync=z_loads, router_pe=z_pe, router_act=z_act, router_act_end=z_act_end, router_gpsimd=z_gpsimd,
                            router_vector_end=z_vector_end, experts_gpsimd=z_tables))
        m.close()
        s5t.close()
        retire(first_block)
        p2b = ExitStack()
        lqk = sbuf(p2b, "lqk", [128, 4, 64])
        f_ada, f_adak, f_lq, z_t, z_tk = (S(n) for n in ("mod_spread", "mod_kept", "lambda_in", "ssm_matricesT",
                                                               "ssm_matricesT_kept"))
        nf = Norm("nf")
        nA = Norm("nA", shift=mod[:, 0:D])
        nA.gains = 4

        PARTS = ((0, 4), (4, 2))

        def spread_mod_pe(pe, half, n, done):
            j0, w = PARTS[n]
            for g in range(4):
                ins = nc.tensor.matmul(ps[:, g, 0:128 * w], K("ones")[32 * g:32 * g + 1, :],
                                       modrow[32 * g:32 * g + 1, 6 * half + j0:6 * half + j0 + w, :].rearrange("p j c -> p (j c)"),
                                       start=True, stop=True, tile_position=(32 * g, 0))
            ins.then_inc(done, 1)

        def spread_mod(v, dst_, bias_in, done, added):
            v.wait_ge(bias_in, 16)
            for n, (j0, w) in enumerate(PARTS):
                v.wait_ge(done, n + 1)
                dst = dst_[:, 512 * j0:512 * (j0 + w)].rearrange("p (j g c) -> p g j c", j=w, g=4)
                for g in range(4):
                    nc.vector.tensor_tensor(dst[:, g], dst[:, g], ps[:, g, 0:128 * w].rearrange("p (j c) -> p j c", j=w),
                                            ALU.add).then_inc(added, 1)
            v.wait_ge(added, 8)
        x3_done, gain_ready = S("x3"), S("gain_ready")
        with nc.Block() as block:
            @block.sync
            def _(sp):
                sp.wait_ge(s_grow, 64)
                for k in range(K_IN2 + 3, K_IN2 + RING):
                    load_unit(sp, k)

            @block.scalar
            def _(a):
                for i, n in enumerate(("lq1_2", "lk1_2", "lq2_2", "lk2_2")):
                    a.dma_start(lqk[:, i, :], A[n].to_broadcast([128, 64])).then_inc(f_lq, 16)
                nf.act_root(a)
                a.wait_ge(z_t, 1)
                for k in range(2):
                    nc.scalar.activation(BT[:, k].rearrange("p j c -> p (j c)"), ps[:, 4 + k, :], ACT.Copy).then_inc(z_tk, 1)
                    nc.scalar.activation(CT[:, k].rearrange("p j c -> p (j c)"), ps[:, 6 + k, :], ACT.Copy,
                                         scale=(1.0, -1.0)[k]).then_inc(z_tk, 1)
                a.wait_ge(x3_done, 2)
                a.dma_start(grow[:], A["norm1_g_2"].to_broadcast([128, D])).then_inc(s_grow, 16)

            @block.vector
            def _(v):
                link = chain(v, "v_chain")
                nv = nc.vector
                v.wait_ge(s_grow, 48)
                nf.dve_stats(v, link)
                for i in range(NT):
                    nv.scalar_tensor_tensor(out=X[:, i, :], in0=X[:, i, :], scalar=st[:, 4 + i:5 + i], in1=grow[:],
                                            op0=ALU.mult, op1=ALU.mult).then_inc(x3_done, 1)
                spread_mod(v, mod, f_in, f_ada, f_adak)
                v.wait_ge(s_grow, 64)
                nv.scalar_tensor_tensor(out=grow[:], in0=mod[:, D:2 * D], scalar=1.0, in1=grow[:], op0=ALU.add,
                                        op1=ALU.mult).then_inc(gain_ready, 1)

            @block.tensor
            def _(pe):
                nt = nc.tensor
                for k in range(2):
                    for q in range(4):
                        nt.transpose(ps[:, 4 + k, q * 128:q * 128 + 128], Bp[:, k, 4 * q:4 * q + 4].rearrange("p j g c -> p (j g c)"), ident)
                        ins = nt.transpose(ps[:, 6 + k, q * 128:q * 128 + 128], Cp[:, k, q, :], ident)
                ins.then_inc(z_t, 1)
                spread_mod_pe(pe, 0, 0, f_ada)
                pe.wait_ge(f_adak, 4)
                spread_mod_pe(pe, 0, 1, f_ada)


        q2T = sbuf(p2b, "q2T", [128, 4, T])
        k2T = sbuf(p2b, "k2T", [128, 4, T])
        v2 = sbuf(p2b, "v2", [128, NT, 512])
        uT = sbuf(p2b, "uT", [128, 4, T])
        lam = sbuf(p2b, "lam", [128, 8])
        w2s = sbuf(p2b, "w2s", [128, 48])
        aT = q2T
        zT = uT
        P2 = hnf.rearrange("p (s k) -> p s k", s=8)
        PT2 = hTf[:, 0:1024].rearrange("p (b h q) -> p b h q", b=2, h=4)
        osq2 = hTf[:, 1024:2048].rearrange("p (i c) -> p i c", i=NT)
        slot = K_SCRATCH[0] % RING
        U = [ring[:, slot, 1024 * k:1024 * k + 1024] for k in (0, 1)]
        Y = [ring[:, slot, 1024 * k:1024 * k + 1024] for k in (2, 3)]
        Z = [junk[:], grow[:]]

        def table(q, k):
            return Wp[:, k, 4 * q:4 * q + 4].rearrange("p j t -> p (j t)")

        def w4(q, n):
            return Wp[:, 0, 4 * q + n, :]
        ssT = Wp[:, 1, 0:4, :]
        s2_proj, s2_pev, s2_l, s2_lk = S("proj2_done"), S("proj2_kept"), S("lam_dots"), S("lam_exps")
        d_s, d_mx, d_exp, d_p, d_t, d_tk, d_o, d_sq, d_v, d_r, d_n, d_nt, d_ntk = (
            S(n) for n in ("a2_scores", "a2_max", "a2_exp", "a2_probs", "a2_probsT", "a2_probsT_kept", "a2_out", "a2_squares",
                           "a2_variance", "a2_root", "a2_normed", "a2_outT", "a2_outT_kept"))
        e_h, e_bu, e_u, e_ri, e_zi, e_pr, e_pi, e_y, e_y1, e_sg, e_z = (S(n) for n in (
            "ssm_input_half", "ssm_input", "ssm_input_kept", "ssm_imag_rotated", "ssm_scanned", "ssm_real_products",
            "ssm_imag_products", "ssm_out", "ssm_gelu_arg", "ssm_gelu_sig", "ssm_gelu"))
        k_in, k_sp, k_ad, k_g = (S(n) for n in ("mod2_bias_in", "mod2_spread", "mod2_kept", "gain2_set"))
        g_p, g_s, g_m, g_o = (S(n) for n in ("glu_done", "glu_sig", "ssm_gated", "mix_done"))
        first_mixture = [n for n in finished() if n.startswith("m1_")]
        UNITS2 = [K_IN2, K_IN2 + 2, K_IN2 + 3, K_IN2 + 4]
        ORDER2 = "P0 P1 I0 R0 P2 P3 C0 I1 R1 P4 P5 C1 I2 R2 S0 E0 P6 C2 I3 R3 P7 T0 O0 S1 C3 G3 E1 T1 O1 H3 N Glu Out"

        with nc.Block() as block:
            @block.sync
            def _(sp):
                for k in range(K_IN2 + RING, K_MOE2 + 3):
                    load_unit(sp, k)

            @block.tensor
            def _(pe):
                nt = nc.tensor
                nA.pe(pe)
                pe.wait_ge(nA.ev, 4)

                def P(n):
                    u, h = divmod(n, 2)
                    unit_arrived(pe, UNITS2[u])
                    w = unit(UNITS2[u])
                    if n >= 2:
                        pe.wait_ge(s2_pev, n - 1)
                    if u == 3:
                        for t in range(KC):
                            ins = nt.matmul(ps[:, 6 + n % 2, :], hT[:, t, h * 128:h * 128 + 128], w[:, t, :], start=t == 0, stop=t == KC - 1)
                    else:
                        for cb in range(2):
                            c = (2 * h + cb) * 128
                            for t in range(KC):
                                ins = nt.matmul(ps[:, 6 + n % 2, cb * 256:cb * 256 + 256], w[:, t, c:c + 128], hT[:, t, :],
                                                start=t == 0, stop=t == KC - 1)
                    ins.then_inc(s2_proj, 1)
                    if h:
                        pe.wait_ge(s2_proj, n + 1)
                        pe.sem_inc(units_used, 2 if u == 0 else 1)

                def I(q):
                    pe.wait_ge(s2_pev, 2)
                    if q == 3:
                        pe.wait_ge(d_mx, 1)
                    for jj in (0, 2, 1, 3):
                        if jj == 1:
                            ins.then_inc(e_h, 1)
                            pe.wait_ge(e_h, q + 1)
                        for k in range(2):
                            r = 32 * jj
                            ins = nt.matmul(ps[:, 2 * k + jj // 2, (jj % 2) * 256:(jj % 2) * 256 + 256], BT[r:r + 32, k, q, :], uT[r:r + 32, q, :],
                                            start=True, stop=True, tile_position=(r, 0))
                    ins.then_inc(e_bu, 1)

                def C(q):
                    pe.wait_ge(e_pr, q + 1)
                    pe.wait_ge(e_pi, q + 1)
                    if q:
                        pe.wait_ge(e_y1, q)
                    for n, (k, x) in enumerate(((0, Y[0]), (1, U[0]), (0, Y[1]), (1, U[1]))):
                        for jj in range(4):
                            ins = nt.matmul(ps[32 * jj:32 * jj + 32, 4, 0:256], CT[:, k, q, 32 * jj:32 * jj + 32],
                                            x[:, jj * 256:jj * 256 + 256], start=n == 0, stop=n == 3, tile_position=(0, 32 * jj),
                                            skip_group_check=True)
                    ins.then_inc(e_y, 1)

                def Sc(i):
                    pe.wait_ge(s2_pev, 6)
                    pe.wait_ge(e_u, 6)
                    if i:
                        pe.wait_ge(d_tk, 1)
                    for h in range(4):
                        for m_ in range(2):
                            r = 64 * m_
                            for kb in range(i + 1):
                                c = (h % 2) * 256 + kb * 128
                                ins = nt.matmul(ps[:, 2 * m_ + h // 2, c:c + 128], q2T[r:r + 64, h, i * 128:i * 128 + 128],
                                                k2T[r:r + 64, h, kb * 128:kb * 128 + 128], start=True, stop=True)
                    ins.then_inc(d_s, 1)

                def Tr(i):
                    pe.wait_ge(d_p, i + 1)
                    pe.wait_ge(e_u, 8)
                    for kb in range(i + 1):
                        for h in range(4):
                            ins = nt.transpose(ps[:, kb, h * 128:h * 128 + 128], P2[:, h, kb * 128:kb * 128 + 128], ident)
                    ins.then_inc(d_t, 1)

                def O(i):
                    pe.wait_ge(s2_pev, 8)
                    pe.wait_ge(d_tk, [1, 3][i])
                    for h in range(4):
                        for kb in range(i + 1):
                            ins = nt.matmul(ps[:, 6 + i, h * 128:h * 128 + 128], PT2[:, kb, h, :], v2[:, kb, h * 128:h * 128 + 128],
                                            start=kb == 0, stop=kb == i)
                    ins.then_inc(d_o, 1)

                def Glu():
                    pe.wait_ge(e_z, 4)
                    unit_arrived(pe, K_GLU)
                    w = unit(K_GLU)
                    for b in range(2):
                        for cb in range(2):
                            for c in range(4):
                                col_ = (2 * b + cb) * 128
                                ins = nt.matmul(ps[:, 2 + b, cb * 256:cb * 256 + 256], w[:, c, col_:col_ + 128], zT[:, c, :],
                                                start=c == 0, stop=c == 3)
                        ins.then_inc(g_p, 1)
                    pe.wait_ge(g_p, 2)
                    pe.sem_inc(units_used, 1)
                    pe.wait_ge(d_n, 2)
                    for i in range(NT):
                        for h in range(4):
                            ins = nt.transpose(ps[:, h // 2, (h % 2) * 256 + i * 128:(h % 2) * 256 + i * 128 + 128],
                                               osq2[:, i, h * 128:h * 128 + 128], ident)
                    ins.then_inc(d_nt, 1)

                def Out():
                    pe.wait_ge(d_ntk, 2)
                    pe.wait_ge(e_y1, 4)
                    pe.wait_ge(g_s, 4)
                    spread_mod_pe(pe, 1, 0, k_sp)
                    for k, src in enumerate((aT, ssT)):
                        unit_arrived(pe, K_OUT2 + 2 * k)
                        if k:
                            pe.wait_ge(k_ad, 4)
                            spread_mod_pe(pe, 1, 1, k_sp)
                            pe.wait_ge(g_m, 1)
                        for i in range(NT):
                            for h in range(2):
                                for c in range(4):
                                    ins = nt.matmul(ps[:, 4 + 2 * i + h, :], src[:, c, i * 128:i * 128 + 128],
                                                    unit(K_OUT2 + 2 * k)[:, c, h * 512:h * 512 + 512], start=k == 0 and c == 0, stop=k == 1 and c == 3)
                            if k:
                                ins.then_inc(g_o, 1)
                    pe.wait_ge(g_o, 2)
                    pe.sem_inc(units_used, 3)

                follow(dict(P=P, I=I, C=C, S=Sc, T=Tr, O=O, Glu=Glu, Out=Out), ORDER2)

            @block.scalar
            def _(a):
                na = nc.scalar
                nA.act(a)
                a.wait_ge(s2_l, 1)
                na.activation(lam[:, 2:4], lam[:, 0:2], ACT.Exp).then_inc(s2_lk, 1)

                def P(n):
                    u, h = divmod(n, 2)
                    a.wait_ge(s2_proj, n + 1)
                    src = ps[:, 6 + n % 2, :]
                    if u == 3:
                        ins = na.activation(v2[:, h, :], src, ACT.Copy)
                    else:
                        dst = (uT, q2T, k2T)[u]
                        ins = na.activation(dst[:, 2 * h:2 * h + 2, :].rearrange("p a b -> p (a b)"), src, ACT.Copy)
                    ins.then_inc(s2_pev, 1)

                def sigmoid(q):
                    a.wait_ge(e_y1, q + 1)
                    na.activation(w4(q, 1), w4(q, 1), ACT.Sigmoid, scale=1.5957691216057308).then_inc(e_sg, 1)

                def I(q):
                    a.wait_ge(e_bu, q + 1)
                    if q:
                        a.wait_ge(e_y, q)
                    for k in range(2):
                        na.activation(U[k], ps[:, 2 * k:2 * k + 2, :].rearrange("p b c -> p (b c)"), ACT.Copy).then_inc(e_u, 1)
                    if q:
                        sigmoid(q - 1)

                def E(i):
                    nk = 128 * (i + 1)
                    a.wait_ge(d_mx, i + 1)
                    for h in range(8):
                        ins = na.activation(P2[:, h, 0:nk], P2[:, h, 0:nk], ACT.Exp, bias=w2s[:, 8 + h:9 + h], scale=0.125,
                                            accum_out=w2s[:, 16 + h:17 + h])
                    ins.then_inc(d_exp, 1)

                def Tr(i):
                    a.wait_ge(d_t, i + 1)
                    if i:
                        a.wait_ge(d_o, i)
                    for kb in range(i + 1):
                        na.activation(PT2[:, kb], ps[:, kb, :].rearrange("p (c q) -> p c q", c=4), ACT.Copy).then_inc(d_tk, 1)

                def H(q):
                    sigmoid(q)

                def N():
                    for i in range(NT):
                        a.wait_ge(d_o, i + 1)
                        na.activation(osq2[:, i], ps[:, 6 + i, :], ACT.Square).then_inc(d_sq, 1)
                    a.wait_ge(d_v, 1)
                    na.activation(w2s[:, 32:40], w2s[:, 32:40], ACT.Sqrt).then_inc(d_r, 1)

                def Glu():
                    for c in range(4):
                        a.wait_ge(g_p, c // 2 + 1)
                        na.activation(ssT[:, c, :], ps[:, 2 + c // 2, (c % 2) * 256:(c % 2) * 256 + 256], ACT.Sigmoid,
                                      bias=VT[:, 52 + c:53 + c]).then_inc(g_s, 1)
                    a.wait_ge(d_nt, 1)
                    for b in range(2):
                        na.activation(aT[:, 2 * b:2 * b + 2], ps[:, b, :].rearrange("p (a q) -> p a q", a=2), ACT.Copy,
                                      scale=lam[:, 5:6]).then_inc(d_ntk, 1)
                    a.wait_ge(e_pi, 4)
                    a.wait_ge(e_pr, 4)
                    a.dma_start(mod2, A["b_ada_2"][:, 3 * D:].to_broadcast([128, 3 * D])).then_inc(k_in, 16)
                    a.dma_start(grow[:], A["norm2_g_2"].to_broadcast([128, D])).then_inc(s_grow, 16)

                follow(dict(P=P, I=I, E=E, T=Tr, H=H, N=N, Glu=Glu), ORDER2)

            @block.gpsimd
            def _(g):
                clear(g, first_mixture)
                link = chain(g, "eg_chain")
                ng = nc.gpsimd

                def R(q):
                    W_r, W_i = table(q, 0), table(q, 1)
                    g.wait_ge(e_u, 2 * q + 2)
                    if q:
                        g.wait_ge(e_y, q)
                    ng.tensor_tensor(Y[1], U[1], W_r, ALU.mult)
                    link(ng.tensor_tensor(Z[1], U[0], W_i, ALU.mult))
                    ng.tensor_tensor(Y[1], Y[1], Z[1], ALU.subtract).then_inc(e_ri, 1)
                    g.wait_ge(e_zi, q + 1)
                    ng.tensor_tensor(U[1], Z[1], W_r, ALU.mult)
                    link(ng.tensor_scalar(Y[1], Z[1], -1.0, None, ALU.mult))
                    ng.tensor_tensor(Y[1], Y[1], W_i, ALU.mult).then_inc(e_pi, 1)
                follow(dict(R=R), ORDER2)

            @block.vector
            def _(v):
                link = chain(v, "v_chain")
                nv = nc.vector
                nA.dve(v, link)
                v.wait_ge(f_lq, 64)
                prod = junk[:, 0:128]
                for i in range(2):
                    ins = nv.tensor_tensor_reduce(out=prod[:, 64 * i:64 * i + 64], in0=lqk[:, 2 * i, :], in1=lqk[:, 2 * i + 1, :],
                                                  scale=1.0, scalar=0.0, op0=ALU.mult, op1=ALU.add, accum_out=lam[:, i:i + 1])
                ins.then_inc(s2_l, 1)
                v.wait_ge(s2_lk, 1)
                link(nv.tensor_tensor(lam[:, 4:5], lam[:, 3:4], lam[:, 2:3], ALU.subtract))
                link(nv.tensor_scalar(lam[:, 4:5], lam[:, 4:5], -0.2, None, ALU.add))
                link(nv.tensor_scalar(lam[:, 5:6], VT[:, 56:57], 0.8, None, ALU.mult))

                def G(q):
                    v.wait_ge(e_y, q + 1)
                    yq, wq = w4(q, 0), w4(q, 1)
                    link(nv.scalar_tensor_tensor(out=yq, in0=uT[:, q, :], scalar=VT[:, 48 + q:49 + q], in1=ps[:, 4, 0:256],
                                                 op0=ALU.mult, op1=ALU.add))
                    link(nv.tensor_tensor(wq, yq, yq, ALU.mult))
                    link(nv.tensor_scalar(wq, wq, 0.044715, 1.0, ALU.mult, ALU.add))
                    nv.tensor_tensor(wq, wq, yq, ALU.mult).then_inc(e_y1, 1)

                def H(q):
                    v.wait_ge(e_sg, q + 1)
                    nv.tensor_tensor(zT[:, q, :], w4(q, 0), w4(q, 1), ALU.mult).then_inc(e_z, 1)

                def R(q):
                    W_r, W_i = table(q, 0), table(q, 1)
                    if q:
                        G(q - 1)
                    v.wait_ge(e_u, 2 * q + 2)
                    nv.tensor_tensor(Y[0], U[0], W_r, ALU.mult)
                    link(nv.tensor_tensor(Z[0], U[1], W_i, ALU.mult))
                    link(nv.tensor_tensor(Y[0], Y[0], Z[0], ALU.add))
                    for part in range(2):
                        if part:
                            v.wait_ge(e_ri, q + 1)
                        for jj in range(4):
                            c = slice(256 * jj, 256 * jj + 256)
                            ins = nv.tensor_tensor_scan(Z[part][:, c], bc(dec[:, 4 * q + jj:4 * q + jj + 1], [128, T]), Y[part][:, c], 0.0,
                                                        ALU.mult, ALU.add)
                        if part == 0:
                            link(ins)
                        else:
                            ins.then_inc(e_zi, 1)
                    nv.tensor_tensor(Y[0], Z[0], W_r, ALU.mult)
                    nv.tensor_tensor(U[0], Z[0], W_i, ALU.mult).then_inc(e_pr, 1)
                    if q:
                        H(q - 1)

                def Sc(i):
                    nk = 128 * (i + 1)
                    P8 = P2[:, :, 0:nk]
                    v.wait_ge(d_s, i + 1)
                    if i:
                        v.wait_ge(d_t, i)
                    src = ps[:, 0:4, :].rearrange("p b (a k) -> p (b a) k", a=2)
                    ca = K("causal").rearrange("p (a k) -> p a k", a=1)
                    link(nv.tensor_tensor(P8[:, :, nk - 128:nk], src[:, :, nk - 128:nk], bc(ca, [128, 8, 128]), ALU.add))
                    if i:
                        link(nv.tensor_copy(P8[:, :, 0:128], src[:, :, 0:128]))
                    link(nv.tensor_reduce(w2s[:, 0:8], P8, AX.X, ALU.max))
                    nv.tensor_scalar(w2s[:, 8:16], w2s[:, 0:8], -0.125, None, ALU.mult).then_inc(d_mx, 1)

                def E(i):
                    nk = 128 * (i + 1)
                    P8 = P2[:, :, 0:nk]
                    v.wait_ge(d_exp, i + 1)
                    w8 = w2s[:, 16:24]
                    link(nv.reciprocal(w8, w8))
                    link(nv.tensor_scalar(w2s[:, 20:24], w2s[:, 20:24], lam[:, 4:5], None, ALU.mult))
                    link(nv.tensor_tensor(P8, P8, bc(w8.rearrange("p (h n) -> p h n", n=1), [128, 8, nk]), ALU.mult))
                    nv.tensor_tensor(P2[:, 0:4, 0:nk], P2[:, 0:4, 0:nk], P2[:, 4:8, 0:nk], ALU.add).then_inc(d_p, 1)

                def N():
                    v.wait_ge(d_sq, 2)
                    link(nv.tensor_reduce(w2s[:, 24:32], osq2.rearrange("p i (h c) -> p (i h) c", h=4), AX.X, ALU.add))
                    nv.tensor_scalar(w2s[:, 32:40], w2s[:, 24:32], 1.0 / 128, EPS, ALU.mult, ALU.add).then_inc(d_v, 1)
                    v.wait_ge(d_r, 1)
                    link(nv.reciprocal(w2s[:, 40:48], w2s[:, 32:40]))
                    for i in range(NT):
                        r = bc(w2s[:, 40 + 4 * i:44 + 4 * i].rearrange("p (h n) -> p h n", n=1), [128, 4, 128])
                        nv.tensor_tensor(osq2[:, i].rearrange("p (h c) -> p h c", h=4), ps[:, 6 + i, :].rearrange("p (h c) -> p h c", h=4),
                                         r, ALU.mult).then_inc(d_n, 1)

                def Out():
                    v.wait_ge(g_s, 4)
                    nv.tensor_tensor(ssT, ssT, zT[:], ALU.mult).then_inc(g_m, 1)
                    spread_mod(v, mod2, k_in, k_sp, k_ad)
                    v.wait_ge(s_grow, 80)
                    nv.scalar_tensor_tensor(out=grow[:], in0=mod2[:, D:2 * D], scalar=1.0, in1=grow[:], op0=ALU.add,
                                            op1=ALU.mult).then_inc(k_g, 1)
                    for i in range(NT):
                        v.wait_ge(g_o, i + 1)
                        link(nv.tensor_tensor(junk[:], ps[:, 4 + 2 * i:6 + 2 * i, :].rearrange("p b c -> p (b c)"), mod[:, 2 * D:3 * D], ALU.mult))
                        link(nv.tensor_tensor(X[:, i, :], X[:, i, :], junk[:], ALU.add))

                follow(dict(G=G, H=H, R=R, S=Sc, E=E, N=N, Out=Out), ORDER2)
        p2b.close()
        p2.close()
        retire(first_mixture)
        n3 = Norm("n3", shift=mod2[:, 0:D])
        n3.gains = 5
        m, acc = mixture("m2_", K_MOE2, 12, moe2_src, "w_router_2", "b_router_2", 4, False, n3, lambda sp: None, False)
        nz = Norm("nz")
        z_x, z_o = S("normed_out"), S("out_done")
        with nc.Block() as block:
            @block.scalar
            def _(a):
                a.dma_start(grow[:], A["final_g_2"].rearrange("(a d) -> a d", a=1).to_broadcast([128, D])).then_inc(s_grow, 16)
                nz.act_root(a)

            @block.vector
            def _(v):
                link = chain(v, "v_chain")
                nv = nc.vector
                for i in range(NT):
                    link(nv.tensor_tensor(acc[:, i, :], acc[:, i, :], mod2[:, 2 * D:3 * D], ALU.mult))
                    link(nv.tensor_tensor(X[:, i, :], X[:, i, :], acc[:, i, :], ALU.add))
                nz.dve_stats(v, link)
                v.wait_ge(s_grow, 96)
                for i in range(NT):
                    nv.scalar_tensor_tensor(out=X[:, i, :], in0=X[:, i, :], scalar=st[:, 4 + i:5 + i], in1=grow[:],
                                            op0=ALU.mult, op1=ALU.mult).then_inc(z_x, 1)

            @block.sync
            def _(sp):
                for i in range(NT):
                    sp.wait_ge(z_x, i + 1)
                    sp.dma_start(out[0, i * 128:i * 128 + 128, :], X[:, i, :]).then_inc(z_o, 16)
                sp.wait_ge(z_o, 32)
        m.close()
        s5.close()


def kernel(**inputs):
    import numpy as _np
    import concourse.bacc as _bacc
    from concourse import mybir as _mybir
    from concourse.bass_utils import run_bass_kernel_spmd as _run

    nc = _bacc.Bacc("TRN2", target_bir_lowering=False, num_devices=1)
    arrays, args = {}, {}
    for name, a in list(inputs.items()) + [("cst", constants())]:
        a = _np.ascontiguousarray(a)
        arrays[f"in_{name}_dram"] = a
        args[name] = nc.dram_tensor(f"in_{name}_dram", a.shape, _mybir.dt.from_np(a.dtype), kind="ExternalInput").ap()
    out = nc.dram_tensor("out_0_dram", (1, T, D), _mybir.dt.float32, kind="ExternalOutput").ap()
    bass_block_pair(nc, args, out)
    r = _run(nc, [arrays], core_ids=[0])
    return r.results[0]["out_0_dram"]
```
